# Optimizing a Trainium2 kernel written in Bass

```python
import math
import jax, jax.numpy as jnp
from jax import lax
import numpy as np

D_MODEL = 1024
BATCH = 1
SEQ = 256
DEPTH = 4

N_MIXERS = 3
CHUNK = 64
LN_EPS = 1e-5
RMS_EPS = 1e-6
L2_EPS = 1e-6
DN_ALPHA = (2 * DEPTH) ** 0.25
DN_BETA = (8 * DEPTH) ** -0.25
D_FF = ((8 * D_MODEL + 3 * 256 - 1) // (3 * 256)) * 256

GDN_DK = 128
GDN_DV = 128
GDN_HEADS = D_MODEL // GDN_DK
GDN_KEY = GDN_HEADS * GDN_DK
GDN_VAL = GDN_HEADS * GDN_DV
GDN_CONV = 4
GDN_QKV = 2 * GDN_KEY + GDN_VAL
GDN_IN = GDN_QKV + GDN_VAL + 2 * GDN_HEADS

HGRN_DK = 128
HGRN_HEADS = D_MODEL // HGRN_DK
HGRN_DV = D_MODEL // HGRN_HEADS
HGRN_IN = 4 * D_MODEL

GLA_HEADS = 4
GLA_KEY = D_MODEL // 2
GLA_DK = GLA_KEY // GLA_HEADS
GLA_VAL = D_MODEL
GLA_DV = GLA_VAL // GLA_HEADS
GLA_RANK = 16
GLA_TAU = 16.0
GLA_IN = 2 * GLA_KEY + 2 * GLA_VAL + GLA_RANK

N_GDN = (DEPTH + 2) // 3
N_HGRN = (DEPTH + 1) // 3
N_GLA = DEPTH // 3


F32 = jnp.float32

def layer_norm(x, g, b):
    xf = x.astype(F32)
    mu = jnp.mean(xf, -1, keepdims=True)
    var = jnp.mean(jnp.square(xf - mu), -1, keepdims=True)
    return ((xf - mu) * lax.rsqrt(var + LN_EPS) * g + b).astype(x.dtype)

def gated_rms_norm(o, gate, w):
    of = o.astype(F32)
    y = of * lax.rsqrt(jnp.mean(of * of, -1, keepdims=True) + RMS_EPS) * w
    return y * jax.nn.silu(gate.astype(F32))

def l2_normalize(t):
    t = t.astype(F32)
    return t * lax.rsqrt(jnp.sum(t * t, -1, keepdims=True) + L2_EPS)

def causal_depthwise_conv(x, w):
    K, C = w.shape
    return lax.conv_general_dilated(
        x, w[:, None, :].astype(x.dtype), window_strides=(1,), padding=[(K - 1, 0)],
        dimension_numbers=('NWC', 'WIO', 'NWC'), feature_group_count=C)

def to_chunks(t):
    B, T, H = t.shape[:3]
    return jnp.moveaxis(t.reshape(B, T // CHUNK, CHUNK, H, *t.shape[3:]), 3, 1)

def from_chunks(t):
    B, H, N, C, d = t.shape
    return jnp.moveaxis(t, 1, 3).reshape(B, N * C, H, d)

def lead(t):
    return jnp.moveaxis(t, 2, 0)

def chunk_gated_delta_rule(q, k, v, beta, g):
    B, T, H, dk = q.shape
    dv = v.shape[-1]
    q, k, v = to_chunks(q.astype(F32)), to_chunks(k.astype(F32)), to_chunks(v.astype(F32))
    beta, g = to_chunks(beta.astype(F32)), to_chunks(g.astype(F32))
    G = jnp.cumsum(g, axis=-1)
    incl = jnp.tril(jnp.ones((CHUNK, CHUNK), bool))
    strict = jnp.tril(jnp.ones((CHUNK, CHUNK), bool), -1)
    decay = jnp.exp(jnp.where(incl, G[..., :, None] - G[..., None, :], -jnp.inf))
    kb = k * beta[..., None]
    L = jnp.where(strict, jnp.einsum('bhncd,bhnsd->bhncs', kb, k) * decay, 0.0)
    rhs = jnp.concatenate([v * beta[..., None], kb * jnp.exp(G)[..., None]], axis=-1)
    sol = lax.linalg.triangular_solve(L + jnp.eye(CHUNK, dtype=F32), rhs, left_side=True, lower=True)
    u, w = sol[..., :dv], sol[..., dv:]
    a_qk = jnp.einsum('bhncd,bhnsd->bhncs', q, k) * decay
    q_dec = q * jnp.exp(G)[..., None]
    G_last = G[..., -1:]
    k_dec = k * jnp.exp(G_last - G)[..., None]
    g_last = jnp.exp(G_last[..., 0])

    def step(S, inp):
        u_c, w_c, a_c, q_c, k_c, gl_c = inp
        v_new = u_c - jnp.einsum('bhcd,bhde->bhce', w_c, S)
        o_c = jnp.einsum('bhcd,bhde->bhce', q_c, S) + jnp.einsum('bhcs,bhse->bhce', a_c, v_new)
        S = S * gl_c[..., None, None] + jnp.einsum('bhcd,bhce->bhde', k_c, v_new)
        return S, o_c

    S0 = jnp.zeros((B, H, dk, dv), F32)
    _, o = lax.scan(step, S0, (lead(u), lead(w), lead(a_qk), lead(q_dec), lead(k_dec), lead(g_last)))
    return from_chunks(jnp.moveaxis(o, 0, 2))

def chunk_gla(q, k, v, g):
    B, T, H, dk = q.shape
    dv = v.shape[-1]
    q, k, v, g = (to_chunks(t.astype(F32)) for t in (q, k, v, g))
    G = jnp.cumsum(g, axis=-2)
    G_last = G[..., -1:, :]
    q_dec = q * jnp.exp(G)
    k_dec = k * jnp.exp(G_last - G)
    g_last = jnp.exp(G_last)
    incl = jnp.tril(jnp.ones((CHUNK, CHUNK), bool))[..., None]

    def step(S, inp):
        q_c, k_c, v_c, G_c, qd_c, kd_c, gl_c = inp
        rel = jnp.exp(jnp.where(incl, G_c[..., :, None, :] - G_c[..., None, :, :], -jnp.inf))
        a = jnp.einsum('bhcd,bhsd,bhcsd->bhcs', q_c, k_c, rel)
        o_c = jnp.einsum('bhcd,bhde->bhce', qd_c, S) + jnp.einsum('bhcs,bhse->bhce', a, v_c)
        S = S * gl_c[..., 0, :, None] + jnp.einsum('bhcd,bhce->bhde', kd_c, v_c)
        return S, o_c

    S0 = jnp.zeros((B, H, dk, dv), F32)
    xs = (lead(q), lead(k), lead(v), lead(G), lead(q_dec), lead(k_dec), lead(g_last))
    _, o = lax.scan(step, S0, xs)
    return from_chunks(jnp.moveaxis(o, 0, 2))

def gated_deltanet(x, w_in, conv_w, a_log, dt_bias, norm_w, w_out):
    B, T, _ = x.shape
    p = x @ w_in
    qkv, z, b, a = jnp.split(p, [GDN_QKV, GDN_QKV + GDN_VAL, GDN_QKV + GDN_VAL + GDN_HEADS], axis=-1)
    qkv = jax.nn.silu(causal_depthwise_conv(qkv, conv_w))
    q, k, v = jnp.split(qkv, [GDN_KEY, 2 * GDN_KEY], axis=-1)
    q = l2_normalize(q.reshape(B, T, GDN_HEADS, GDN_DK)) * (GDN_DK ** -0.5)
    k = l2_normalize(k.reshape(B, T, GDN_HEADS, GDN_DK))
    v = v.reshape(B, T, GDN_HEADS, GDN_DV)
    beta = jax.nn.sigmoid(b.astype(F32))
    g = -jnp.exp(a_log.astype(F32)) * jax.nn.softplus(a.astype(F32) + dt_bias.astype(F32))
    o = chunk_gated_delta_rule(q, k, v, beta, g)
    o = gated_rms_norm(o, z.reshape(B, T, GDN_HEADS, GDN_DV), norm_w.astype(F32))
    return o.reshape(B, T, GDN_VAL).astype(x.dtype) @ w_out

def hgrn2(x, w_in, lb, norm_w, w_out):
    B, T, _ = x.shape
    q, f, i, r = jnp.split(x @ w_in, 4, axis=-1)
    q = jax.nn.silu(q.astype(F32)).reshape(B, T, HGRN_HEADS, HGRN_DK) * (HGRN_DK ** -0.5)
    log_f = jnp.logaddexp(jnp.log(lb), jnp.log1p(-lb) + jax.nn.log_sigmoid(f.astype(F32)))
    k = -jnp.expm1(log_f)
    shp_k = (B, T, HGRN_HEADS, HGRN_DK)
    o = chunk_gla(q, k.reshape(shp_k), i.reshape(B, T, HGRN_HEADS, HGRN_DV), log_f.reshape(shp_k))
    o = gated_rms_norm(o, r.reshape(B, T, HGRN_HEADS, HGRN_DV), norm_w.astype(F32))
    return o.reshape(B, T, D_MODEL).astype(x.dtype) @ w_out

def gla(x, w_in, w_gk2, b_gk, norm_w, w_out):
    B, T, _ = x.shape
    q, k, v, r, gk = jnp.split(x @ w_in, [GLA_KEY, 2 * GLA_KEY, 2 * GLA_KEY + GLA_VAL, 2 * GLA_KEY + 2 * GLA_VAL], axis=-1)
    g = jax.nn.log_sigmoid((gk @ w_gk2 + b_gk).astype(F32)) / GLA_TAU
    shp_k = (B, T, GLA_HEADS, GLA_DK)
    q = q.astype(F32).reshape(shp_k) * (GLA_DK ** -0.5)
    o = chunk_gla(q, k.reshape(shp_k), v.reshape(B, T, GLA_HEADS, GLA_DV), g.reshape(shp_k))
    o = gated_rms_norm(o, r.reshape(B, T, GLA_HEADS, GLA_DV), norm_w.astype(F32))
    return o.reshape(B, T, GLA_VAL).astype(x.dtype) @ w_out

def swiglu(x, w_in, w_down):
    gate, up = jnp.split(x @ w_in, 2, axis=-1)
    return (jax.nn.silu(gate) * up) @ w_down

def first_inputs(seed: int = 0) -> dict:
    key = jax.random.key(seed)
    ks = jax.random.split(key, 22)
    nrm = lambda k, shape, s: jax.random.normal(k, shape, F32) * s
    x = jax.random.normal(ks[0], (BATCH, SEQ, D_MODEL), F32)
    gdn_w_in = nrm(ks[1], (N_GDN, D_MODEL, GDN_IN), D_MODEL ** -0.5)
    gdn_conv_w = nrm(ks[2], (N_GDN, GDN_CONV, GDN_QKV), GDN_CONV ** -0.5)
    gdn_a_log = jnp.log(jax.random.uniform(ks[3], (N_GDN, GDN_HEADS), F32, 1.0, 16.0))
    dt = jnp.exp(jax.random.uniform(ks[4], (N_GDN, GDN_HEADS), F32, math.log(1e-3), math.log(1e-1)))
    gdn_dt_bias = dt + jnp.log(-jnp.expm1(-dt))
    gdn_norm_w = 1.0 + nrm(ks[5], (N_GDN, GDN_DV), 0.02)
    gdn_w_out = nrm(ks[6], (N_GDN, GDN_VAL, D_MODEL), GDN_VAL ** -0.5 * DN_BETA)
    hgrn_w_in = nrm(ks[7], (N_HGRN, D_MODEL, HGRN_IN), D_MODEL ** -0.5)
    hgrn_lb_logits = nrm(ks[8], (DEPTH, HGRN_HEADS * HGRN_DK), 0.5)
    hgrn_norm_w = 1.0 + nrm(ks[9], (N_HGRN, HGRN_DV), 0.02)
    hgrn_w_out = nrm(ks[10], (N_HGRN, D_MODEL, D_MODEL), D_MODEL ** -0.5 * DN_BETA)
    gla_w_in = nrm(ks[11], (N_GLA, D_MODEL, GLA_IN), D_MODEL ** -0.5)
    gla_w_gk2 = nrm(ks[12], (N_GLA, GLA_RANK, GLA_KEY), GLA_RANK ** -0.5)
    gla_b_gk = nrm(ks[13], (N_GLA, GLA_KEY), 0.1)
    gla_norm_w = 1.0 + nrm(ks[14], (N_GLA, GLA_DV), 0.02)
    gla_w_out = nrm(ks[15], (N_GLA, GLA_VAL, D_MODEL), GLA_VAL ** -0.5 * DN_BETA)
    mix_ln_g = 1.0 + nrm(ks[16], (DEPTH, D_MODEL), 0.02)
    mix_ln_b = nrm(ks[17], (DEPTH, D_MODEL), 0.02)
    ffn_w_in = nrm(ks[18], (DEPTH, D_MODEL, 2 * D_FF), D_MODEL ** -0.5)
    ffn_w_down = nrm(ks[19], (DEPTH, D_FF, D_MODEL), D_FF ** -0.5 * DN_BETA)
    ffn_ln_g = 1.0 + nrm(ks[20], (DEPTH, D_MODEL), 0.02)
    ffn_ln_b = nrm(ks[21], (DEPTH, D_MODEL), 0.02)
    return {"x": x, "gdn_w_in": gdn_w_in, "gdn_conv_w": gdn_conv_w, "gdn_a_log": gdn_a_log,
            "gdn_dt_bias": gdn_dt_bias, "gdn_norm_w": gdn_norm_w, "gdn_w_out": gdn_w_out,
            "hgrn_w_in": hgrn_w_in, "hgrn_lb_logits": hgrn_lb_logits, "hgrn_norm_w": hgrn_norm_w,
            "hgrn_w_out": hgrn_w_out, "gla_w_in": gla_w_in, "gla_w_gk2": gla_w_gk2, "gla_b_gk": gla_b_gk,
            "gla_norm_w": gla_norm_w, "gla_w_out": gla_w_out, "mix_ln_g": mix_ln_g, "mix_ln_b": mix_ln_b,
            "ffn_w_in": ffn_w_in, "ffn_w_down": ffn_w_down, "ffn_ln_g": ffn_ln_g, "ffn_ln_b": ffn_ln_b}

def first_block(x, gdn_w_in, gdn_conv_w, gdn_a_log, gdn_dt_bias, gdn_norm_w, gdn_w_out,
              hgrn_w_in, hgrn_lb_logits, hgrn_norm_w, hgrn_w_out,
              gla_w_in, gla_w_gk2, gla_b_gk, gla_norm_w, gla_w_out,
              mix_ln_g, mix_ln_b, ffn_w_in, ffn_w_down, ffn_ln_g, ffn_ln_b):
    lb_soft = jax.nn.softmax(hgrn_lb_logits.astype(F32), axis=0)
    lb_all = jnp.cumsum(lb_soft, axis=0) - lb_soft[0]
    for i in range(DEPTH):
        kind, j = i % N_MIXERS, i // N_MIXERS
        if kind == 0:
            m = gated_deltanet(x, gdn_w_in[j], gdn_conv_w[j], gdn_a_log[j], gdn_dt_bias[j], gdn_norm_w[j], gdn_w_out[j])
        elif kind == 1:
            m = hgrn2(x, hgrn_w_in[j], lb_all[i], hgrn_norm_w[j], hgrn_w_out[j])
        else:
            m = gla(x, gla_w_in[j], gla_w_gk2[j], gla_b_gk[j], gla_norm_w[j], gla_w_out[j])
        x = layer_norm(DN_ALPHA * x + m, mix_ln_g[i], mix_ln_b[i])
        x = layer_norm(DN_ALPHA * x + swiglu(x, ffn_w_in[i], ffn_w_down[i]), ffn_ln_g[i], ffn_ln_b[i])
    return x


DEPTH_2 = 2

GROUP_WIDTH = D_MODEL // 4
HEAD_DIM = 64
N_HEADS_GROUP = GROUP_WIDTH // HEAD_DIM
D_MIX = 4 * GROUP_WIDTH

MOBA_BLOCK = 256
MOBA_TOPK = 3
MOBA_Q_CHUNK = 32
MLA_Q_RANK = 192
MLA_KV_RANK = 128
MLA_NOPE = 64
MLA_ROPE = 32
MLA_V = HEAD_DIM
MLA_QK = MLA_NOPE + MLA_ROPE
SB_Q_BLOCK = 128
SSM_HEADDIM = 64
SSM_HEADS = GROUP_WIDTH // SSM_HEADDIM
SSM_GROUPS = 2
SSM_STATE = 64
SSM_CONV = 4
SSM_CHUNK = 128
SSM_XBC = GROUP_WIDTH + 2 * SSM_GROUPS * SSM_STATE
D_FF_2 = 2816
FFN_CONV = 3
ROPE_THETA = 10000.0
ATTN_Q_BLOCK = 128
EPS = 1e-6

MOBA_COLS = 3 * GROUP_WIDTH
MLA_COLS = MLA_Q_RANK + MLA_KV_RANK + MLA_ROPE
SB_COLS = 3 * GROUP_WIDTH
SSM_COLS = GROUP_WIDTH + SSM_XBC + SSM_HEADS
IN_COLS = MOBA_COLS + MLA_COLS + SB_COLS + SSM_COLS


def _split(x, sizes):
    outs, o = [], 0
    for s in sizes:
        outs.append(x[..., o:o + s])
        o += s
    return outs

def rms_norm(x, g):
    xf = x.astype(jnp.float32)
    y = xf * lax.rsqrt(jnp.mean(xf * xf, axis=-1, keepdims=True) + EPS)
    return (y * g.astype(jnp.float32)).astype(x.dtype)

def rope_tables(positions, dim):
    inv = 1.0 / (ROPE_THETA ** (jnp.arange(0, dim, 2, dtype=jnp.float32) / dim))
    ang = positions.astype(jnp.float32)[..., None] * inv
    return jnp.cos(ang), jnp.sin(ang)

def apply_rope(x, cos, sin):
    x1, x2 = jnp.split(x, 2, axis=-1)
    c = cos[:, :, None, :].astype(x.dtype)
    s = sin[:, :, None, :].astype(x.dtype)
    return jnp.concatenate([x1 * c - x2 * s, x1 * s + x2 * c], axis=-1)

def causal_dwconv(x, w):
    width, ch = w.shape
    return lax.conv_general_dilated(
        x, w[:, None, :], window_strides=(1,), padding=[(width - 1, 0)],
        dimension_numbers=("NWC", "WIO", "NWC"), feature_group_count=ch)

def moba_attention(q, k, v):
    bsz, seq, nh, hd = q.shape
    scale = hd ** -0.5
    nblk = -(-seq // MOBA_BLOCK)
    pad = nblk * MOBA_BLOCK - seq
    kp = jnp.pad(k, ((0, 0), (0, pad), (0, 0), (0, 0)))
    vp = jnp.pad(v, ((0, 0), (0, pad), (0, 0), (0, 0)))
    kbt = kp.reshape(bsz, nblk, MOBA_BLOCK, nh, hd).transpose(0, 3, 1, 2, 4)
    vbt = vp.reshape(bsz, nblk, MOBA_BLOCK, nh, hd).transpose(0, 3, 1, 2, 4)
    kmean = jnp.mean(kbt.astype(jnp.float32), axis=3).astype(k.dtype)
    k_eff = min(MOBA_TOPK, nblk)
    nq = seq // MOBA_Q_CHUNK
    qc = q.reshape(bsz, nq, MOBA_Q_CHUNK, nh, hd).transpose(1, 0, 2, 3, 4)
    blk_ids = jnp.arange(nblk)
    bi = jnp.arange(bsz)[:, None, None, None]
    hi = jnp.arange(nh)[None, :, None, None]

    def one_chunk(args):
        c, qi = args
        cur = (c * MOBA_Q_CHUNK) // MOBA_BLOCK
        gate = jnp.einsum("bqhd,bhnd->bhqn", qi, kmean).astype(jnp.float32)
        gate = jnp.where(blk_ids < cur, gate, -jnp.inf)
        _, idx = lax.top_k(gate, k_eff)
        valid = jnp.arange(k_eff) < cur
        k_sel = kbt[bi, hi, idx]
        v_sel = vbt[bi, hi, idx]
        s_sel = jnp.einsum("bqhd,bhqnjd->bhqnj", qi, k_sel).astype(jnp.float32) * scale
        s_sel = jnp.where(valid[None, None, None, :, None], s_sel, -jnp.inf)
        s_sel = s_sel.reshape(bsz, nh, MOBA_Q_CHUNK, k_eff * MOBA_BLOCK)
        k_own = lax.dynamic_index_in_dim(kbt, cur, axis=2, keepdims=False)
        v_own = lax.dynamic_index_in_dim(vbt, cur, axis=2, keepdims=False)
        s_own = jnp.einsum("bqhd,bhjd->bhqj", qi, k_own).astype(jnp.float32) * scale
        q_local = c * MOBA_Q_CHUNK + jnp.arange(MOBA_Q_CHUNK) - cur * MOBA_BLOCK
        causal = jnp.arange(MOBA_BLOCK)[None, :] <= q_local[:, None]
        s_own = jnp.where(causal, s_own, -jnp.inf)
        p = jax.nn.softmax(jnp.concatenate([s_sel, s_own], axis=-1), axis=-1).astype(v.dtype)
        p_sel = p[..., :k_eff * MOBA_BLOCK].reshape(bsz, nh, MOBA_Q_CHUNK, k_eff, MOBA_BLOCK)
        p_own = p[..., k_eff * MOBA_BLOCK:]
        return (jnp.einsum("bhqnj,bhqnjd->bqhd", p_sel, v_sel)
                + jnp.einsum("bhqj,bhjd->bqhd", p_own, v_own))

    out = lax.map(one_chunk, (jnp.arange(nq), qc))
    return out.transpose(1, 0, 2, 3, 4).reshape(bsz, seq, nh, hd)

def moba_mixer(p, cos, sin, qk_g):
    bsz, seq, _ = p.shape
    q, k, v = [t.reshape(bsz, seq, N_HEADS_GROUP, HEAD_DIM) for t in _split(p, (GROUP_WIDTH,) * 3)]
    q = apply_rope(rms_norm(q, qk_g[0]), cos, sin)
    k = apply_rope(rms_norm(k, qk_g[1]), cos, sin)
    return moba_attention(q, k, v)

def causal_softmax_attention(q, k, v, scale):
    bsz, seq, nh, dk = q.shape
    nb = seq // ATTN_Q_BLOCK
    qb = q.reshape(bsz, nb, ATTN_Q_BLOCK, nh, dk).transpose(1, 0, 2, 3, 4)
    kpos = jnp.arange(seq)

    def one_block(args):
        i, qi = args
        s = jnp.einsum("bqhd,bkhd->bhqk", qi, k).astype(jnp.float32) * scale
        qpos = i * ATTN_Q_BLOCK + jnp.arange(ATTN_Q_BLOCK)
        s = jnp.where(kpos[None, :] <= qpos[:, None], s, -jnp.inf)
        pr = jax.nn.softmax(s, axis=-1).astype(v.dtype)
        return jnp.einsum("bhqk,bkhd->bqhd", pr, v)

    out = lax.map(one_block, (jnp.arange(nb), qb))
    return out.transpose(1, 0, 2, 3, 4).reshape(bsz, seq, nh, v.shape[-1])

def mla_mixer(p, cos, sin, q_norm_g, kv_norm_g, w_uq, w_ukv, qk_g):
    bsz, seq, _ = p.shape
    c_q, c_kv, k_rope = _split(p, (MLA_Q_RANK, MLA_KV_RANK, MLA_ROPE))
    q = jnp.einsum("bsr,rc->bsc", rms_norm(c_q, q_norm_g), w_uq).reshape(bsz, seq, N_HEADS_GROUP, MLA_QK)
    kv = jnp.einsum("bsr,rc->bsc", rms_norm(c_kv, kv_norm_g), w_ukv).reshape(bsz, seq, N_HEADS_GROUP, MLA_NOPE + MLA_V)
    k_nope, v = kv[..., :MLA_NOPE], kv[..., MLA_NOPE:]
    k_pe = jnp.broadcast_to(k_rope[:, :, None, :], (bsz, seq, N_HEADS_GROUP, MLA_ROPE))
    k = jnp.concatenate([k_nope, k_pe], axis=-1)
    q = rms_norm(q, qk_g[0])
    k = rms_norm(k, qk_g[1])
    q = jnp.concatenate([q[..., :MLA_NOPE], apply_rope(q[..., MLA_NOPE:], cos, sin)], axis=-1)
    k = jnp.concatenate([k[..., :MLA_NOPE], apply_rope(k[..., MLA_NOPE:], cos, sin)], axis=-1)
    return causal_softmax_attention(q, k, v, MLA_QK ** -0.5)

def stick_breaking_mixer(p):
    bsz, seq, _ = p.shape
    q, k, v = [t.reshape(bsz, seq, N_HEADS_GROUP, HEAD_DIM) for t in _split(p, (GROUP_WIDTH,) * 3)]
    scale = HEAD_DIM ** -0.5
    nb = seq // SB_Q_BLOCK
    qb = q.reshape(bsz, nb, SB_Q_BLOCK, N_HEADS_GROUP, HEAD_DIM).transpose(1, 0, 2, 3, 4)
    kpos = jnp.arange(seq)

    def one_block(args):
        i, qi = args
        z = jnp.einsum("bqhd,bkhd->bhqk", qi, k).astype(jnp.float32) * scale
        qpos = i * SB_Q_BLOCK + jnp.arange(SB_Q_BLOCK)
        strict = kpos[None, :] < qpos[:, None]
        log_beta = jax.nn.log_sigmoid(z)
        log_1mb = jnp.where(strict, jax.nn.log_sigmoid(-z), 0.0)
        tail = lax.cumsum(log_1mb, axis=3, reverse=True) - log_1mb
        a = jnp.where(strict, jnp.exp(log_beta + tail), 0.0).astype(v.dtype)
        return jnp.einsum("bhqk,bkhd->bqhd", a, v)

    out = lax.map(one_block, (jnp.arange(nb), qb))
    return out.transpose(1, 0, 2, 3, 4).reshape(bsz, seq, N_HEADS_GROUP, HEAD_DIM)

def ssd_chunked(xh, dt, a_head, bm, cm):
    bsz, seq, nh, hp = xh.shape
    ns = bm.shape[-1]
    nc, cl = seq // SSM_CHUNK, SSM_CHUNK
    x = (xh * dt[..., None]).reshape(bsz, nc, cl, nh, hp)
    a = (dt * a_head).reshape(bsz, nc, cl, nh).transpose(0, 3, 1, 2)
    bc = bm.reshape(bsz, nc, cl, nh, ns)
    cc = cm.reshape(bsz, nc, cl, nh, ns)
    a_cum = jnp.cumsum(a, axis=-1)
    tri = jnp.tril(jnp.ones((cl, cl), dtype=bool))
    seg = a_cum[..., :, None] - a_cum[..., None, :]
    lmat = jnp.where(tri, jnp.exp(jnp.where(tri, seg, 0.0)), 0.0)
    y_diag = jnp.einsum("bclhn,bcshn,bhcls,bcshp->bclhp", cc, bc, lmat, x)
    decay_states = jnp.exp(a_cum[..., -1:] - a_cum)
    states = jnp.einsum("bclhn,bhcl,bclhp->bchpn", bc, decay_states, x)
    chunk_decay = jnp.exp(a_cum[..., -1])

    def step(h, inp):
        s_c, d_c = inp
        return d_c[..., None, None] * h + s_c, h

    h0 = jnp.zeros((bsz, nh, hp, ns), jnp.float32)
    _, prev = lax.scan(step, h0, (states.transpose(1, 0, 2, 3, 4), chunk_decay.transpose(2, 0, 1)))
    prev = prev.transpose(1, 0, 2, 3, 4)
    y_off = jnp.einsum("bclhn,bchpn,bhcl->bclhp", cc, prev, jnp.exp(a_cum))
    return (y_diag + y_off).reshape(bsz, seq, nh, hp)

def mamba2_mixer(p, conv_w, conv_b, dt_bias, a_log, d_skip, norm_g):
    bsz, seq, _ = p.shape
    z, xbc, dt_raw = _split(p, (GROUP_WIDTH, SSM_XBC, SSM_HEADS))
    xbc = jax.nn.silu(causal_dwconv(xbc, conv_w) + conv_b)
    xs, bm, cm = _split(xbc, (GROUP_WIDTH, SSM_GROUPS * SSM_STATE, SSM_GROUPS * SSM_STATE))
    rep = SSM_HEADS // SSM_GROUPS
    xh = xs.reshape(bsz, seq, SSM_HEADS, SSM_HEADDIM).astype(jnp.float32)
    bm = jnp.repeat(bm.reshape(bsz, seq, SSM_GROUPS, SSM_STATE), rep, axis=2).astype(jnp.float32)
    cm = jnp.repeat(cm.reshape(bsz, seq, SSM_GROUPS, SSM_STATE), rep, axis=2).astype(jnp.float32)
    dt = jax.nn.softplus(dt_raw.astype(jnp.float32) + dt_bias.astype(jnp.float32))
    a_head = -jnp.exp(a_log.astype(jnp.float32))
    y = ssd_chunked(xh, dt, a_head, bm, cm) + d_skip.astype(jnp.float32)[:, None] * xh
    y = y.reshape(bsz, seq, GROUP_WIDTH).astype(p.dtype)
    return rms_norm(y * jax.nn.silu(z), norm_g)

def second_inputs(seed: int = 0) -> dict:
    key = jax.random.key(seed)
    ks = jax.random.split(key, 24)
    f32 = jnp.float32
    L = DEPTH_2

    def normal(k, shape, scale):
        return jax.random.normal(k, shape, f32) * scale

    def gain(k, shape):
        return 1.0 + 0.1 * jax.random.normal(k, shape, f32)

    x = normal(ks[0], (BATCH, SEQ, D_MODEL), 1.0)
    positions = (jax.random.randint(ks[1], (BATCH, 1), 0, 4096, dtype=jnp.int32)
                 + jnp.arange(SEQ, dtype=jnp.int32)[None, :])
    dt0 = jnp.exp(jax.random.uniform(ks[13], (L, SSM_HEADS), f32, math.log(1e-3), math.log(1e-1)))
    return {
        "x": x,
        "positions": positions,
        "mix_norm_g": gain(ks[2], (L, D_MODEL)),
        "w_in": normal(ks[3], (L, D_MODEL, IN_COLS), D_MODEL ** -0.5),
        "moba_qk_g": gain(ks[4], (L, 2, HEAD_DIM)),
        "mla_q_norm_g": gain(ks[5], (L, MLA_Q_RANK)),
        "mla_kv_norm_g": gain(ks[6], (L, MLA_KV_RANK)),
        "mla_w_uq": normal(ks[7], (L, MLA_Q_RANK, N_HEADS_GROUP * MLA_QK), MLA_Q_RANK ** -0.5),
        "mla_w_ukv": normal(ks[8], (L, MLA_KV_RANK, N_HEADS_GROUP * (MLA_NOPE + MLA_V)), MLA_KV_RANK ** -0.5),
        "mla_qk_g": gain(ks[9], (L, 2, MLA_QK)),
        "ssm_conv_w": normal(ks[10], (L, SSM_CONV, SSM_XBC), SSM_CONV ** -0.5),
        "ssm_conv_b": normal(ks[11], (L, SSM_XBC), 0.02),
        "ssm_dt_bias": dt0 + jnp.log(-jnp.expm1(-dt0)),
        "ssm_a_log": jnp.log(jax.random.uniform(ks[12], (L, SSM_HEADS), f32, 1.0, 16.0)),
        "ssm_d": gain(ks[14], (L, SSM_HEADS)),
        "ssm_norm_g": gain(ks[15], (L, GROUP_WIDTH)),
        "head_out_g": gain(ks[16], (L, 3, N_HEADS_GROUP, HEAD_DIM)),
        "w_out": normal(ks[17], (L, D_MIX, D_MODEL), D_MIX ** -0.5),
        "ffn_norm_g": gain(ks[18], (L, D_MODEL)),
        "ffn_w_in": normal(ks[19], (L, D_MODEL, 2 * D_FF_2), D_MODEL ** -0.5),
        "ffn_conv_w": normal(ks[20], (L, FFN_CONV, 2 * D_FF_2), FFN_CONV ** -0.5),
        "ffn_conv_b": normal(ks[21], (L, 2 * D_FF_2), 0.02),
        "ffn_w_out": normal(ks[22], (L, D_FF_2, D_MODEL), D_FF_2 ** -0.5),
    }

def second_block(x, positions, mix_norm_g, w_in, moba_qk_g, mla_q_norm_g, mla_kv_norm_g,
              mla_w_uq, mla_w_ukv, mla_qk_g, ssm_conv_w, ssm_conv_b, ssm_dt_bias, ssm_a_log,
              ssm_d, ssm_norm_g, head_out_g, w_out, ffn_norm_g, ffn_w_in, ffn_conv_w,
              ffn_conv_b, ffn_w_out):
    bsz, seq, _ = x.shape
    cos_a, sin_a = rope_tables(positions, HEAD_DIM)
    cos_m, sin_m = rope_tables(positions, MLA_ROPE)
    for l in range(DEPTH_2):
        h = rms_norm(x, mix_norm_g[l])
        proj = jnp.einsum("bsd,dc->bsc", h, w_in[l])
        moba_p, mla_p, sb_p, ssm_p = _split(proj, (MOBA_COLS, MLA_COLS, SB_COLS, SSM_COLS))
        o_moba = moba_mixer(moba_p, cos_a, sin_a, moba_qk_g[l])
        o_mla = mla_mixer(mla_p, cos_m, sin_m, mla_q_norm_g[l], mla_kv_norm_g[l],
                          mla_w_uq[l], mla_w_ukv[l], mla_qk_g[l])
        o_sb = stick_breaking_mixer(sb_p)
        o_ssm = mamba2_mixer(ssm_p, ssm_conv_w[l], ssm_conv_b[l], ssm_dt_bias[l],
                             ssm_a_log[l], ssm_d[l], ssm_norm_g[l])
        heads = rms_norm(jnp.stack([o_moba, o_mla, o_sb], axis=2), head_out_g[l])
        mixed = jnp.concatenate([heads.reshape(bsz, seq, 3 * GROUP_WIDTH), o_ssm], axis=-1)
        x = x + jnp.einsum("bsc,cd->bsd", mixed, w_out[l])
        h = rms_norm(x, ffn_norm_g[l])
        u = causal_dwconv(jnp.einsum("bsd,df->bsf", h, ffn_w_in[l]), ffn_conv_w[l]) + ffn_conv_b[l]
        gate, up = _split(u, (D_FF_2, D_FF_2))
        x = x + jnp.einsum("bsf,fd->bsd", jax.nn.silu(gate) * up, ffn_w_out[l])
    return x


def setup_inputs(seed=0):
    out = dict(first_inputs(seed))
    for name, value in second_inputs(seed + 1).items():
        if name != "x":
            out[name + "_2"] = value
    return out


def reference(
    x, gdn_w_in, gdn_conv_w, gdn_a_log, gdn_dt_bias, gdn_norm_w, gdn_w_out, hgrn_w_in,
    hgrn_lb_logits, hgrn_norm_w, hgrn_w_out, gla_w_in, gla_w_gk2, gla_b_gk, gla_norm_w,
    gla_w_out, mix_ln_g, mix_ln_b, ffn_w_in, ffn_w_down, ffn_ln_g, ffn_ln_b, positions_2,
    mix_norm_g_2, w_in_2, moba_qk_g_2, mla_q_norm_g_2, mla_kv_norm_g_2, mla_w_uq_2, mla_w_ukv_2,
    mla_qk_g_2, ssm_conv_w_2, ssm_conv_b_2, ssm_dt_bias_2, ssm_a_log_2, ssm_d_2, ssm_norm_g_2,
    head_out_g_2, w_out_2, ffn_norm_g_2, ffn_w_in_2, ffn_conv_w_2, ffn_conv_b_2, ffn_w_out_2,
):
    x = first_block(
        x, gdn_w_in, gdn_conv_w, gdn_a_log, gdn_dt_bias, gdn_norm_w, gdn_w_out, hgrn_w_in,
        hgrn_lb_logits, hgrn_norm_w, hgrn_w_out, gla_w_in, gla_w_gk2, gla_b_gk, gla_norm_w,
        gla_w_out, mix_ln_g, mix_ln_b, ffn_w_in, ffn_w_down, ffn_ln_g, ffn_ln_b,
    )
    return second_block(
        x, positions_2, mix_norm_g_2, w_in_2, moba_qk_g_2, mla_q_norm_g_2, mla_kv_norm_g_2,
        mla_w_uq_2, mla_w_ukv_2, mla_qk_g_2, ssm_conv_w_2, ssm_conv_b_2, ssm_dt_bias_2,
        ssm_a_log_2, ssm_d_2, ssm_norm_g_2, head_out_g_2, w_out_2, ffn_norm_g_2, ffn_w_in_2,
        ffn_conv_w_2, ffn_conv_b_2, ffn_w_out_2,
    )


_drawn_inputs = setup_inputs


def setup_inputs(seed=0):
    import zlib

    import numpy as np

    out = dict(_drawn_inputs(seed))
    spreads = {}
    factors = {'gdn_norm_w': 7.412,
     'hgrn_lb_logits': 8.0,
     'hgrn_norm_w': 8.0,
     'gla_b_gk': 6.282,
     'gla_norm_w': 8.0,
     'ssm_conv_b_2': 4.29,
     'ffn_conv_b_2': 3.595}
    for name, (base, spread) in spreads.items():
        noise = np.random.default_rng([zlib.crc32(name.encode()), seed]).standard_normal(out[name].shape)
        drawn = base * np.exp(spread * noise) if base else spread * noise
        out[name] = __import__('jax').numpy.asarray(drawn.astype(out[name].dtype))
    for name, factor in factors.items():
        out[name] = (out[name] * factor).astype(out[name].dtype)
    return out
```

```python
from contextlib import ExitStack

import numpy as np

import concourse.bass as bass
from concourse import mybir

F32 = mybir.dt.float32
F32R = mybir.dt.float32r
I32 = mybir.dt.int32
U32 = mybir.dt.uint32
ACT = mybir.ActivationFunctionType
ALU = mybir.AluOpType
AX = mybir.AxisListType

P = 128
T = 256
D = 1024
KT = D // P
DEPTH = 4
DN_ALPHA = (2 * DEPTH) ** 0.25
F_TILES = 2816 // P
F_STEPS = F_TILES // 2
F_PAIRS = (F_STEPS - 5) // 2
RING = 6
HI = 3
DVE_SHARE = 3
SLOT = 2048
HALF = 128
ALL = slice(0, T)
TRI = 3 * HALF

TWO_PI = [6.28125, 0.0019350051879882812]
TWO_PI.append(float(2 * np.pi - sum(TWO_PI)))
CHAIN = [("gdn", 0), ("hgrn", 0), ("gla", 0), ("gdn", 1), ("four", 0), ("four", 1)]


class Book:

    def __init__(self):
        self.marks = {}
        self.strides = {}

    def restart(self):
        self.loop = None


class Signal:

    def __init__(self, book, sem, name):
        self.book, self.sem, self.name, self.n = book, sem, name, 0
        self.base = None

    def _value(self):
        loop = self.book.loop
        if loop is None:
            return self.n
        if self.base is None or self.base[0] is not loop:
            self.base = (loop, self.n)
            loop.signals.append((self, self.n))
        stride = self.book.strides.get((loop.name, self.name), 0)
        return self.n + loop.i * stride if stride else self.n

    def tick(self, *key):
        self._value()
        self.n += 1
        loop = self.book.loop
        if key:
            self.book.marks[(self.name,) + key] = (self.n, loop and loop.name)
        return self.sem, 1

    def at(self, *key, ago=0):
        n, name = self.book.marks.get((self.name,) + key, (1, None))
        if name is not None:
            stride = self.book.strides.get((name, self.name), 0)
            loop = self.book.loop
            if loop is not None and loop.name == name:
                return self.sem, (n - ago * stride) + loop.i * stride
            n += stride * (self.book.strides.get((name, "count"), 1) - 1)
        return self.sem, n

    def now(self):
        return self.sem, self._value()


class Loop:

    def __init__(self, book, eng, name, count):
        self.book, self.eng, self.name, self.count = book, eng, name, count

    def __enter__(self):
        self.signals = []
        self.fori = self.eng.Fori(0, self.count)
        self.i = self.fori.__enter__()
        self.book.loop = self
        return self.i

    def __exit__(self, *e):
        self.fori.__exit__(*e)
        self.book.loop = None
        self.book.strides[(self.name, "count")] = self.count
        for sig, n in self.signals:
            stride = sig.n - n
            self.book.strides[(self.name, sig.name)] = stride
            sig.n = n + self.count * stride


class Psum:

    def __init__(self, book, banks, sem):
        self.book, self.banks, self.sem = book, banks, sem
        self.next, self.uses, self.where = 0, [0] * 8, {}

    def claim(self, pe, *key, bank=None):
        b = self.next % 8 if bank is None else bank
        self.next += bank is None
        if self.uses[b]:
            pe.wait_ge(*self.book.marks.get(("free", b, self.uses[b]), (self.sem, 1)))
        self.uses[b] += 1
        self.where[key] = b, self.uses[b]
        return self.banks[b]

    def bank(self, *key):
        return self.banks[self.where[key][0]]

    def release(self, signal, *key):
        self.book.marks[("free",) + self.where[key]] = signal.sem, signal.n


def units_in(kind):
    if kind == "gdn":
        u = [(4096, 16, "pair8", "ba", 0)]
        u += [(256 * i, 256, "cm", "conv", 2 * i) for i in range(12)]
        u += [(3072 + 256 * i, 256, "cm", "gate", 2 * i) for i in range(4)]
    elif kind == "hgrn":
        u = [(1024 + 256 * i, 256, "cm", "f", 2 * i) for i in range(4)]
        u += [(256 * i, 256, "cm", "qsilu", 2 * i) for i in range(4)]
        u += [(2048 + 256 * i, 256, "tok", "v", i) for i in range(4)]
        u += [(3072 + 256 * i, 256, "cm", "gate", 2 * i) for i in range(4)]
    elif kind == "gla":
        u = [(3072, 16, "row16", "gk", 0)]
        u += [(256 * i, 256, "cm", "qscaled", 2 * i) for i in range(2)]
        u += [(512 + 256 * i, 256, "cm", "k", 2 * i) for i in range(2)]
        u += [(1024 + 256 * i, 256, "tok", "v", i) for i in range(4)]
        u += [(2048 + 256 * i, 256, "cm", "gate", 2 * i) for i in range(4)]
    else:
        mla, sb, ssm = 768, 1120, 1888
        u = [(ssm + 768, 4, "row4", "dt", 0)]
        u += [(ssm + 256 + 256 * i, 256, "cm", "xbc", 2 * i) for i in range(2)]
        u += [(0, 256, "cm", "plain", 0), (256, 256, "cm", "plain", 2), (512, 256, "tok", "vmoba", 0)]
        u += [(mla, 192, "cq", "cq", 0), (mla + 192, 160, "ckv", "ckv", 0)]
        u += [(sb, 256, "cm", "plain", 10), (sb + 256, 256, "cm", "plain", 12), (sb + 512, 256, "tok", "vsb", 0)]
        u += [(ssm, 256, "cm", "z", 0)]
    return u




PT_LN, PT_CONV, PT_MISC, PT_SSM, PT_FFN = 0, 1, 3, 4, 5
PT_TILES = 9
R_MIXG, R_MIXB, R_FFNG, R_FFNB = 0, 32, 64, 96
R_RMSMIX, R_RMSFFN, R_LB, R_GDN, R_HGRN, R_GLA, R_BGK = 0, 16, 32, 64, 66, 67, 69
R_CONVB, R_SSMG, R_KVG, R_QG0, R_QG1, R_MOBAG, R_MLAG, R_HEADG, R_SSMD = 73, 81, 85, 87, 89, 91, 95, 99, 111
FFN_BIAS = (PT_FFN + 3) * P


def build(nc, A, out, book, layers=len(CHAIN), debug=None):
    book.restart()
    with ExitStack() as ctx:
        places = {}

        def sb(name, shape, dt=F32):
            t = ctx.enter_context(nc.sbuf_tensor(name, shape, dt))
            places[name] = nc.sbuf_base - 4 * int(np.prod(shape[1:]))
            return t

        def over(name, shape, at_name, floats=0):
            return nc.alloc_sbuf_tensor_at(name, shape, F32R, offset=places[at_name] + 4 * floats)

        def sem(name):
            return ctx.enter_context(nc.semaphore(name))

        def signal(name):
            return Signal(book, sem(name), name)

        ring = sb("ring", [P, RING, SLOT])
        x = sb("x", [P, KT, T])
        xn = sb("xn", [P, KT, T])
        sq = sb("sq", [P, KT, T])
        pj = sb("pj", [P, 32, T])
        mats = sb("mats", [P, 16, TRI])
        inv = sb("inv", [P, 32, HALF])
        ct = sb("ct", [P, 16, HALF])
        yb = sb("yb", [P, 16, HALF])
        vb = sb("vb", [P, 2, D])
        dec = sb("dec", [P, 2, TRI])
        stat = sb("stat", [P, 4, 2 * T])
        rows = sb("rows", [16, 6, T])
        cols = sb("cols", [P, 4, 16])
        small = sb("small", [P, 8, 4])
        params = sb("params", [P, PT_TILES * P])
        head = sb("head", [8, 8])
        lbs = sb("lbs", [P, 8, KT])
        hssm = sb("hssm", [4, 4])
        trig = sb("trig", [P, 4, T])
        freqs = sb("freqs", [P, 2])
        ident = sb("ident", [P, P])
        ones = sb("ones", [P, P])
        ones_d = sb("ones_d", [P, P])
        blk64 = sb("blk64", [P, P])
        rot64 = sb("rot64", [P, P])
        rot96 = sb("rot96", [P, P])
        later = sb("later", [P, P])
        level = sb("level", [P, 7, P])
        incl = sb("incl", [P, TRI])
        strict = sb("strict", [P, TRI])
        amask = sb("amask", [P, TRI])
        const = sb("const", [P, 8])
        banks = [ctx.enter_context(nc.psum_tensor(f"bank{i}", [P, 512], F32)) for i in range(8)]
        C_LN_EPS, C_RMS_EPS, C_QSCALE, C_HALFPI, C_ONE = 0, 1, 2, 3, 4

        def flat(ap):
            return ap[:, :, :].rearrange("p a b -> p (a b)") if len(ap.shape) == 3 else ap

        lt = mats[:, 0:8, :]
        at = mats[:, 8:16, :]
        y = xn
        w_hi = over("w_hi", [P, HI, SLOT], "mats")
        w_lo = over("w_lo", [P, RING, SLOT], "ring")
        xh = over("xh", [P, KT, T], "inv")
        xl = over("xl", [P, KT, T], "xn")
        hid_hi = over("hid_hi", [P, 2, 2, T], "pj")
        hid_lo = over("hid_lo", [P, 2, 2, T], "yb")
        decayed_sum = flat(inv[:, 16:32, :])
        yt = xn[:, :, :].rearrange("p (t c) n -> p t (c n)", t=2)
        ct_t, yb_t = (a[:, :, :].rearrange("p (h c) n -> p h (c n)", c=2) for a in (ct, yb))
        fconv = ct_t[:, :, :].rearrange("p (s a) n -> p s a n", s=2)
        hid = yb_t[:, 0:4, :].rearrange("p (s a) n -> p s a n", s=2)
        gact = yb_t[:, 4:8, :].rearrange("p (s a) n -> p s a n", s=2)
        oc = pj[:, 16:24, :].rearrange("p (m a) n -> p m (a n)", a=2)
        oc4 = pj[:, 24:32, :].rearrange("p (m a) n -> p m (a n)", a=2)
        mlaw = flat(inv)[:, 2048:3328]
        sb_l1 = lt[:, 0:4, :]
        sb_t = flat(sq)[:, 0:4 * TRI].rearrange("p (h n) -> p h n", h=4)
        at2 = flat(inv)[:, 0:8 * TRI].rearrange("p (a b) -> p a b", a=8)
        wgk2 = flat(dec)[0:16, 0:512]
        stage = flat(at)
        pos_i = stat[:, 0, 0:T].bitcast(I32)

        def two(ap, g):
            return flat(ap[:, 2 * g:2 * g + 2, :])

        def pj2(i):
            return flat(pj[:, i:i + 2, :])

        def four_tiles(ap, g):
            return flat(ap[:, 4 * g:4 * g + 4, :])

        def gsq(g):
            return flat(ct if g < 4 else yb)[:, 2 * T * (g % 4):2 * T * (g % 4 + 1)]

        def nsq(r):
            return two(sq, 2 + r) if r < 2 else four_tiles(ct, r - 2)

        def u(t, h):
            return ct[:, 8 * t + h, :]

        def at_level(lv):
            return inv[:, 16 * (lv % 2):16 * (lv % 2) + 16, :].rearrange("p (h c) n -> p h (c n)", c=2)

        def level_diff(lv, heads):
            return flat(ct if lv % 2 == 0 else sq)[:, 0:heads * T].rearrange("p (n c) -> p n c", c=2 << lv)

        def par(col):
            return params[:, col:col + 1]

        w_loaded = [sem(f"w_loaded{i}") for i in range(RING)]
        in_loaded = sem("in_loaded")
        param_loaded = sem("param_loaded")
        mla_loaded = sem("mla_loaded")
        out_stored = sem("out_stored")
        gk_loaded = sem("gk_loaded")
        pool_setup, dve_setup, act_setup, pe_setup = map(signal, ("pool_setup", "dve_setup", "act_setup", "pe_setup"))
        pe_unit = signal("pe_unit")
        dve_hi, dve_lo, pool_lo = map(signal, ("dve_hi", "dve_lo", "pool_lo"))
        act_proj, dve_conv = map(signal, ("act_proj", "dve_conv"))
        pe_gdn, act_gdn, dve_gdn, pool_gdn = map(signal, ("pe_gdn", "act_gdn", "dve_gdn", "pool_gdn"))
        pe_gla, act_gla, dve_gla = map(signal, ("pe_gla", "act_gla", "dve_gla"))
        pe_four, act_four, dve_four = map(signal, ("pe_four", "act_four", "dve_four"))
        pe_norm, act_norm, dve_norm = map(signal, ("pe_norm", "act_norm", "dve_norm"))
        act_ffn, dve_ffn = map(signal, ("act_ffn", "dve_ffn"))
        pe_out, act_out = map(signal, ("pe_out", "act_out"))
        psum = Psum(book, banks, out_stored)

        sizes = []
        for kind, _ in CHAIN[:layers]:
            sizes += [KT * w for _, w, *_ in units_in(kind)] + [SLOT] * (4 + 3 * F_STEPS)

        def of_unit(sig, u, i=None):
            return sig.sem, u + 1 if i is None else i * RING + (u + 1)

        def loaded(u, i=None):
            n = u // RING + 1
            return w_loaded[u % RING], 16 * n if i is None else (i + n) * 16

        block = ctx.enter_context(nc.Block())

        PARAM_LOADS = []

        def param_rows(tile, row, src, width=P, col=0):
            n = src.shape[0]
            PARAM_LOADS.append((stage[row:row + n, tile * P + col:tile * P + col + width], src))

        def tiles_of(ap):
            return ap.rearrange("a (t c) -> (a t) c", c=P)

        for row, name in ((R_MIXG, "mix_ln_g"), (R_MIXB, "mix_ln_b"), (R_FFNG, "ffn_ln_g"), (R_FFNB, "ffn_ln_b")):
            param_rows(PT_LN, row, tiles_of(A[name]))
        for l in range(2):
            param_rows(PT_CONV + l, 0, tiles_of(A["gdn_conv_w"][l]))
        for row, name in ((R_RMSMIX, "mix_norm_g_2"), (R_RMSFFN, "ffn_norm_g_2"), (R_LB, "hgrn_lb_logits"),
                          (R_GDN, "gdn_norm_w"), (R_HGRN, "hgrn_norm_w"), (R_GLA, "gla_norm_w"), (R_BGK, "gla_b_gk"),
                          (R_CONVB, "ssm_conv_b_2"), (R_SSMG, "ssm_norm_g_2"), (R_KVG, "mla_kv_norm_g_2")):
            param_rows(PT_MISC, row, tiles_of(A[name]))
        param_rows(PT_MISC, R_QG0, A["mla_q_norm_g_2"][:, 0:P])
        param_rows(PT_MISC, R_QG1, A["mla_q_norm_g_2"][:, P:P + 64], 64)
        for half in range(2):
            param_rows(PT_MISC, R_MOBAG, A["moba_qk_g_2"].rearrange("l a c -> (l a) c"), 64, 64 * half)
            d = A["ssm_d_2"].rearrange("l (a b) -> (l a) b", b=2)[:, half:half + 1].rearrange("r (b c) -> r b c", b=1)
            PARAM_LOADS.append((stage[R_SSMD:R_SSMD + 4, PT_MISC * P + 64 * half:PT_MISC * P + 64 * half + 64]
                                .rearrange("r (b c) -> r b c", c=1), d.to_broadcast([4, 64, 1])))
        param_rows(PT_MISC, R_MLAG, A["mla_qk_g_2"].rearrange("l a c -> (l a) c"), 96)
        param_rows(PT_MISC, R_HEADG, A["head_out_g_2"].rearrange("l m (a b) c -> (l m a) (b c)", b=2))
        for l in range(2):
            param_rows(PT_SSM, 16 * l, tiles_of(A["ssm_conv_w_2"][l]))
        taps = A["ffn_conv_w_2"].rearrange("l j (t c) -> (l j t) c", c=P)
        for t in range(3):
            n = min(P, taps.shape[0] - t * P)
            param_rows(PT_FFN + t, 0, taps[t * P:t * P + n, :])
        param_rows(PT_FFN + 3, 0, tiles_of(A["ffn_conv_b_2"]))
        IN_LOADS = [(yt, A["x"][0].rearrange("(t p) n -> p t n", p=P)),
                    (pos_i, A["positions_2"].to_broadcast([P, T])), (freqs[:, :], A["rope_freqs"])]
        for dst, col, name in ((head, 0, "gdn_a_log"), (head, 2, "gdn_dt_bias"), (hssm, 0, "ssm_a_log_2"), (hssm, 2, "ssm_dt_bias_2")):
            n = A[name].shape[1]
            for l in range(2):
                IN_LOADS.append((dst[0:n, col + l:col + l + 1], A[name][l:l + 1, :].rearrange("l h -> h l")))
        N_IN = len(IN_LOADS)

        @block.tensor
        def _(pe):
            unit = 0

            def products(u, outs, tiles, width, moving, first=True, last=True, i=None, parts_ready=(None, None)):
                n = tiles * width
                w_high = w_hi[:, u % HI, 0:n].rearrange("p (k n) -> p k n", k=tiles)
                w_low = w_lo[:, u % RING, 0:n].rearrange("p (k n) -> p k n", k=tiles)
                x_high, x_low = moving
                pe.wait_ge(*of_unit(dve_hi, u, i))
                for step, (w, xin) in enumerate(((w_high, x_high), (w_high, x_low), (w_low, x_high))):
                    if step < 2 and parts_ready[step] is not None:
                        pe.wait_ge(*parts_ready[step])
                    if step == 2:
                        pe.wait_ge(*of_unit(dve_lo, u, i))
                        pe.wait_ge(*of_unit(pool_lo, u, i))
                    for j, (cols, c0, cw, tokens) in enumerate(outs):
                        for k in range(tiles):
                            wk, xk = w[:, k, c0:c0 + cw], xin[:, k, tokens]
                            m = nc.tensor.matmul(cols, *((wk, xk) if tokens == ALL else (xk, wk)),
                                                 start=(first and step == 0 and k == 0 and (j % 2 == 0)),
                                                 stop=(last and step == 2 and k == tiles - 1), skip_group_check=True)
                return m

            def project(layer, kind, parts_ready):
                nonlocal unit
                for n, (c0, w, how, name, idx) in enumerate(units_in(kind)):
                    b = psum.claim(pe, "proj", layer, n)
                    left, right = b[:, 0:T], b[:, T:2 * T]
                    outs = {"cm": [(left, 0, P, ALL), (right, P, P, ALL)],
                            "pair8": [(b[0:8, 0:T], 0, 8, ALL), (b[0:8, T:2 * T], 8, 8, ALL)],
                            "row16": [(b[0:16, 0:T], 0, 16, ALL)],
                            "row4": [(b[0:4, 0:T], 0, 4, ALL)],
                            "cq": [(left, 0, P, ALL), (b[0:64, T:2 * T], P, 64, ALL)],
                            "ckv": [(left, 0, P, ALL), (b[0:96, T:2 * T], 64, 96, ALL)],
                            "tok": [(left, 0, T, slice(0, HALF)), (right, 0, T, slice(HALF, T))]}[how]
                    products(unit, outs, KT, w, (xh, xl), parts_ready=parts_ready if n == 0 else (None, None))\
                        .then_inc(*pe_unit.tick("unit", layer, n))
                    unit += 1

            def out_project(layer):
                nonlocal unit
                for n in range(4):
                    b = psum.claim(pe, "out", layer, n)
                    products(unit, [(b[:, 0:T], 0, P, ALL), (b[:, T:2 * T], P, P, ALL)], KT, T, (xh, xl),
                             parts_ready=(mixed(layer, "hi"), mixed(layer, "lo")) if n == 0 else (None, None))\
                        .then_inc(*pe_unit.tick("out", layer, n))
                    unit += 1

            def mixed(layer, part):
                kind = CHAIN[layer][0]
                return {"gdn": dve_gdn, "four": dve_four}.get(kind, dve_gla).at("mixed " + part, layer)

            def layer_norm(n):
                b = psum.claim(pe, "mean", n)
                for k in range(KT):
                    if k % 2 == 0:
                        pe.wait_ge(*dve_norm.at("residual", n, k // 2))
                    m = nc.tensor.matmul(b[:, 0:T], ones_d[:, :], x[:, k, :], start=(k == 0), stop=(k == KT - 1))
                m.then_inc(*pe_norm.tick("mean", n))
                rms_sum(n)

            def rms_sum(n):
                b = psum.claim(pe, "square", n)
                for k in range(KT):
                    if k % 2 == 0:
                        pe.wait_ge(*act_norm.at("square", n, k // 2))
                    m = nc.tensor.matmul(b[:, 0:T], ones_d[:, :], sq[:, k, :], start=(k == 0), stop=(k == KT - 1))
                m.then_inc(*pe_norm.tick("square", n))

            def ffn(layer, parts_ready):
                nonlocal unit
                for b in range(8):
                    psum.claim(pe, "ffn", layer, b, bank=b)

                def gate_up(par_, key, i, freed, parts_ready=(None, None)):
                    nonlocal unit
                    for part in range(2):
                        b = banks[4 + 2 * par_ + part]
                        if freed is not None:
                            pe.wait_ge(*freed[part])
                        products(unit, [(b[:, 0:T], 0, P, ALL), (b[:, T:2 * T], P, P, ALL)], KT, T, (xh, xl), i=i,
                                 parts_ready=parts_ready if part == 0 else (None, None))\
                            .then_inc(*pe_unit.tick("gate" if part == 0 else "up", layer, key))
                        unit += 1

                def down(par_, key, i, step, ago=0, first=False, last=False):
                    nonlocal unit
                    outs = [(banks[n // 2][:, (n % 2) * T:(n % 2 + 1) * T], n * P, P, ALL) for n in range(KT)]
                    products(unit, outs, 2, D, (hid_hi[:, par_], hid_lo[:, par_]), first, last, i,
                             (dve_ffn.at("hidden hi", layer, step, ago=ago), dve_ffn.at("hidden lo", layer, step, ago=ago)))\
                        .then_inc(*pe_unit.tick("down", layer, key))
                    unit += 1

                freed_by = (lambda k, ago=0: (act_ffn.at("gated", layer, k, ago=ago),
                                              dve_ffn.at("hidden", layer, k, ago=ago))) \
                    if layer < DEPTH else (lambda k, ago=0: (dve_ffn.at("conv gate", layer, k, ago=ago),
                                                             dve_ffn.at("conv up", layer, k, ago=ago)))
                gate_up(0, 0, None, None, parts_ready)
                gate_up(1, 1, None, None)
                down(0, 0, None, 0, first=True)
                gate_up(0, 2, None, freed_by(0))
                down(1, 1, None, 1)
                u0 = unit
                with Loop(book, pe, f"ffn{layer}", F_PAIRS) as i:
                    gate_up(1, "a", i, freed_by("a", 1))
                    down(0, "of b", i, "b", ago=1)
                    gate_up(0, "b", i, freed_by("b", 1))
                    down(1, "of a", i, "a")
                unit = u0 + RING * F_PAIRS
                gate_up(1, 9, None, freed_by("a"))
                down(0, 8, None, "b")
                gate_up(0, 10, None, freed_by("b"))
                down(1, 9, None, 9)
                down(0, "last", None, 10, last=True)

            def setup():
                pe.wait_ge(param_loaded, 16 * len(PARAM_LOADS))
                pe.wait_ge(*pool_setup.at("identity"))
                for g in range(3):
                    tiles = range(4 * g, min(4 * g + 4, PT_TILES))
                    b = psum.claim(pe, "params", g)
                    for j, t in enumerate(tiles):
                        m = nc.tensor.transpose(b[:, j * P:(j + 1) * P], stage[:, t * P:(t + 1) * P], ident[:, :])
                    m.then_inc(*pe_setup.tick("params", g))
                pe.wait_ge(in_loaded, 16 * N_IN)
                xtok = xn[:, :, :].rearrange("p (t c) n -> p t (c n)", t=2)
                for g in range(4):
                    b = psum.claim(pe, "x", g)
                    for j in range(4):
                        k, t = 2 * g + j // 2, j % 2
                        m = nc.tensor.transpose(b[:, j * P:(j + 1) * P], xtok[:, t, k * P:(k + 1) * P], ident[:, :])
                    m.then_inc(*pe_setup.tick("x", g))

            def causal(b, k, q, rows_=slice(0, P)):
                nc.tensor.matmul(b[:, 0:T], k[:, 0:HALF], q[:, :], start=True, stop=True)
                return nc.tensor.matmul(b[:, T:TRI], k[:, HALF:T], q[:, HALF:T], start=True, stop=True)

            def values(b_cols, v0, v1, a):
                nc.tensor.matmul(b_cols, v0, a[:, 0:T], start=True, stop=False, skip_group_check=True)
                return nc.tensor.matmul(b_cols[:, HALF:T], v1, a[:, T:TRI], start=False, stop=True,
                                        skip_group_check=True)

            def gdn(layer):
                for g in range(8):
                    b = psum.claim(pe, "qk2", layer, g)
                    pe.wait_ge(*act_gdn.at("square", layer, g))
                    nc.tensor.matmul(b[:, :], ones[:, :], gsq(g), start=True, stop=True).then_inc(*pe_gdn.tick("qk2", layer, g))
                b = psum.claim(pe, "tok", layer)
                pe.wait_ge(*dve_gdn.at("rows", layer))
                for j in range(4):
                    row = rows[0:8, j % 2, (j // 2) * HALF:(j // 2 + 1) * HALF]
                    m = nc.tensor.transpose(b[:, j * 8:(j + 1) * 8], row, ident[0:8, 0:8])
                m.then_inc(*pe_gdn.tick("tok", layer))
                for g in range(4):
                    b = psum.claim(pe, "v", layer, g)
                    pe.wait_ge(*act_proj.at("conv", layer, 11))
                    t, h0 = g // 2, 4 * (g % 2)
                    for j in range(4):
                        m = nc.tensor.transpose(b[:, j * P:(j + 1) * P],
                                                pj[:, 16 + h0 + j, t * HALF:(t + 1) * HALF], ident[:, :])
                    m.then_inc(*pe_gdn.tick("v", layer, g))
                for h in range(8):
                    b = psum.claim(pe, "bcast", layer, h)
                    for j in range(2):
                        m = nc.tensor.matmul(b[:, j * T:(j + 1) * T], ident[0:8, h:h + 1].to_broadcast([8, P]), rows[0:8, j, :], start=True, stop=True)
                    m.then_inc(*pe_gdn.tick("bcast", layer, h))
                    if h:
                        gdn_scores(layer, h - 1)
                gdn_scores(layer, 7)
                pe.wait_ge(*dve_gdn.at("eye", layer))
                for lv in range(7):
                    for g in range(4):
                        b = psum.claim(pe, "cx", layer, lv, g)
                        pe.wait_ge(*pool_gdn.at("masked", layer, lv, g))
                        if lv:
                            pe.wait_ge(*dve_gdn.at("inv", layer, lv - 1, g))
                        for j in range(4 * g, 4 * g + 4):
                            m = nc.tensor.matmul(b[:, (j % 4) * P:(j % 4 + 1) * P], ct[:, j, :], inv[:, j, :],
                                                 start=True, stop=True)
                        m.then_inc(*pe_gdn.tick("cx", layer, lv, g))
                        if g:
                            gdn_correct(layer, lv, g - 1)
                    gdn_correct(layer, lv, 3)
                for g in range(2):
                    b = psum.claim(pe, "u0", layer, g)
                    if g == 0:
                        pe.wait_ge(*dve_gdn.at("inv", layer, 6, 3))
                    for j in range(4 * g, 4 * g + 4):
                        m = nc.tensor.matmul(b[:, (j % 4) * P:(j % 4 + 1) * P], inv[:, 16 + j, :],
                                             vb[:, 0, j * P:(j + 1) * P], start=True, stop=True)
                    m.then_inc(*pe_gdn.tick("u0", layer, g))
                for g in range(2):
                    b = psum.claim(pe, "lu", layer, g)
                    pe.wait_ge(*act_gdn.at("u0", layer, g))
                    for j in range(4 * g, 4 * g + 4):
                        m = nc.tensor.matmul(b[:, (j % 4) * P:(j % 4 + 1) * P], lt[:, j, HALF:T], u(0, j),
                                             start=True, stop=True)
                    m.then_inc(*pe_gdn.tick("lu", layer, g))
                for g in range(2):
                    b = psum.claim(pe, "u1", layer, g)
                    pe.wait_ge(*dve_gdn.at("rhs", layer, g))
                    for j in range(4 * g, 4 * g + 4):
                        m = nc.tensor.matmul(b[:, (j % 4) * P:(j % 4 + 1) * P], inv[:, 24 + j, :],
                                             vb[:, 1, j * P:(j + 1) * P], start=True, stop=True)
                    m.then_inc(*pe_gdn.tick("u1", layer, g))
                for g in range(4):
                    b = psum.claim(pe, "o", layer, g)
                    pe.wait_ge(*act_gdn.at("u1", layer, g // 2))
                    for j in (2 * g, 2 * g + 1):
                        m = values(b[:, (j % 2) * T:(j % 2 + 1) * T], u(0, j), u(1, j), at[:, j, :])
                    m.then_inc(*pe_gdn.tick("o", layer, g))
                head_norms(layer, act_gdn, pe_gdn, 4, False)

            def gdn_scores(layer, h):
                pe.wait_ge(*dve_gdn.at("kbeta", layer, h))
                b = psum.claim(pe, "kk", layer, h)
                causal(b, pj[:, 8 + h, :], sq[:, h, :]).then_inc(*pe_gdn.tick("kk", layer, h))
                b = psum.claim(pe, "qk", layer, h)
                causal(b, pj[:, 8 + h, :], pj[:, h, :]).then_inc(*pe_gdn.tick("qk", layer, h))

            def gdn_correct(layer, lv, g):
                pe.wait_ge(*act_gdn.at("cx", layer, lv, g))
                if lv < 6:
                    b = psum.claim(pe, "z", layer, lv, g)
                    for j in range(4 * g, 4 * g + 4):
                        m = nc.tensor.matmul(b[:, (j % 4) * P:(j % 4 + 1) * P], inv[:, 16 + j, :], yb[:, j, :],
                                             start=True, stop=True)
                    m.then_inc(*pe_gdn.tick("z", layer, lv, g))
                b = psum.claim(pe, "zt", layer, lv, g)
                for j in range(4 * g, 4 * g + 4):
                    m = nc.tensor.matmul(b[:, (j % 4) * P:(j % 4 + 1) * P], yb[:, j, :], inv[:, 16 + j, :],
                                         start=True, stop=True)
                m.then_inc(*pe_gdn.tick("zt", layer, lv, g))

            def head_norms(layer, act_sig, pe_sig, n, both):
                for g in range(n):
                    b = psum.claim(pe, "o2", layer, g)
                    pe.wait_ge(*act_sig.at("o2", layer, g))
                    if both:
                        nc.tensor.matmul(b[:, 0:T], ones[:, :], sq[:, 2 * g, :], start=True, stop=False)
                        m = nc.tensor.matmul(b[:, 0:T], ones[:, :], sq[:, 2 * g + 1, :], start=False, stop=True)
                    else:
                        m = nc.tensor.matmul(b[:, :], ones[:, :], two(sq, g), start=True, stop=True)
                    m.then_inc(*pe_sig.tick("o2", layer, g))

            def gla(layer, kind):
                heads = 8 if kind == "hgrn" else 4
                q = pj[:, 0:heads, :]
                k = yb_t[:, 0:8, :] if kind == "hgrn" else pj[:, 4:8, :]
                if kind == "gla":
                    pe.wait_ge(*act_proj.at("gk", layer))
                    pe.wait_ge(gk_loaded, 16)
                    for g in range(2):
                        b = psum.claim(pe, "gk", layer, g)
                        for j in range(2):
                            m = nc.tensor.matmul(b[:, j * T:(j + 1) * T], wgk2[:, (2 * g + j) * P:(2 * g + j + 1) * P],
                                                 rows[0:16, 4, :], start=True, stop=True)
                        m.then_inc(*pe_gla.tick("gk", layer, g))
                pe.wait_ge(*dve_gla.at("qk", layer))
                pe.wait_ge(*act_gla.at("k", layer))
                for lv in range(-1, 7):
                    if lv >= 0:
                        pe.wait_ge(*dve_gla.at("decayed", layer, lv))
                    src = at_level(lv)
                    for g in range(heads // 2):
                        b = psum.claim(pe, "level", layer, lv, g)
                        for j in range(4):
                            h, t = 2 * g + j // 2, slice((j % 2) * HALF, (j % 2 + 1) * HALF)
                            a, c = (k[:, h, t], q[:, h, t]) if lv < 0 else (src[:, h, t], src[:, h, t])
                            m = nc.tensor.matmul(b[:, j * P:(j + 1) * P], a, c, start=True, stop=True)
                        m.then_inc(*pe_gla.tick("level", layer, lv, g))
                pe.wait_ge(*dve_gla.at("decayed", layer, 7))
                src = at_level(7)
                for g in range(heads // 4):
                    b = psum.claim(pe, "cross", layer, g)
                    for j in range(4):
                        h = 4 * g + j
                        m = nc.tensor.matmul(b[:, j * P:(j + 1) * P], src[:, h, 0:HALF], src[:, h, HALF:T],
                                             start=True, stop=True)
                    m.then_inc(*pe_gla.tick("cross", layer, g))
                for g in range(4):
                    b = psum.claim(pe, "o", layer, g)
                    pe.wait_ge(*dve_gla.at("causal", layer))
                    for j in (2 * g, 2 * g + 1):
                        m = values(b[:, (j % 2) * T:(j % 2 + 1) * T], vb[:, 0, j * P:(j + 1) * P],
                                   vb[:, 1, j * P:(j + 1) * P], at[:, j if kind == "hgrn" else j // 2, :])
                    m.then_inc(*pe_gla.tick("o", layer, g))
                head_norms(layer, act_gla, pe_gla, 4, kind == "gla")

            def four(layer):
                b = psum.claim(pe, "c2", layer)
                pe.wait_ge(*act_four.at("csq", layer))
                nc.tensor.matmul(b[:, 0:T], ones[:, :], sq[:, 0, :], start=True, stop=False)
                nc.tensor.matmul(b[:, 0:T], ones[0:64, :], sq[0:64, 1, :], start=False, stop=True)
                nc.tensor.matmul(b[:, T:2 * T], ones[:, :], sq[:, 2, :], start=True, stop=True)\
                    .then_inc(*pe_four.tick("c2", layer))
                norm_sums(layer, 0)
                norm_sums(layer, 1)
                pe.wait_ge(mla_loaded, 48 * (layer - DEPTH + 1))
                pe.wait_ge(*dve_four.at("cn", layer))
                cq0, cq1, ckv = pj[:, 6, :], pj[0:64, 7, :], pj[:, 8, :]
                for g in range(2):
                    b = psum.claim(pe, "mlaq", layer, g)
                    for j in range(2):
                        c = (2 * g + j) * 96
                        nc.tensor.matmul(b[0:96, j * T:(j + 1) * T], mlaw[:, c:c + 96], cq0, start=True, stop=False)
                        m = nc.tensor.matmul(b[0:96, j * T:(j + 1) * T], mlaw[0:64, 384 + c:384 + c + 96], cq1,
                                             start=False, stop=True)
                    m.then_inc(*pe_four.tick("mlaq", layer, g))
                for g in range(2):
                    b = psum.claim(pe, "mlak", layer, g)
                    for j in range(2):
                        c = 768 + (2 * g + j) * 128
                        m = nc.tensor.matmul(b[0:64, j * T:(j + 1) * T], mlaw[:, c:c + 64], ckv, start=True, stop=True)
                    m.then_inc(*pe_four.tick("mlak", layer, g))
                b = psum.claim(pe, "mlav", layer)
                wv = mlaw[:, 768:1280].rearrange("p (h a) -> p h a", h=4)[:, :, 64:128]
                for t in range(2):
                    m = nc.tensor.matmul(b[:, t * T:(t + 1) * T].rearrange("p (h a) -> p h a", h=4),
                                         ckv[:, t * HALF:(t + 1) * HALF], wv, start=True, stop=True)
                m.then_inc(*pe_four.tick("mlav", layer))
                for r in range(2, 6):
                    norm_sums(layer, r)
                b = psum.claim(pe, "tok", layer)
                pe.wait_ge(*dve_four.at("rows", layer))
                for j in range(4):
                    row = rows[0:4, j % 2, (j // 2) * HALF:(j // 2 + 1) * HALF]
                    m = nc.tensor.transpose(b[:, j * 8:j * 8 + 4], row, ident[0:4, 0:4])
                m.then_inc(*pe_four.tick("tok", layer))
                b = psum.claim(pe, "xtok", layer)
                pe.wait_ge(*act_proj.at("xbc", layer, 1))
                for j in range(4):
                    t, c = j // 2, j % 2
                    m = nc.tensor.transpose(b[:, j * P:(j + 1) * P], pj[:, 18 + c, t * HALF:(t + 1) * HALF], ident[:, :])
                m.then_inc(*pe_four.tick("xtok", layer))
                for g in range(2):
                    b = psum.claim(pe, "bcast", layer, g)
                    for j in range(2):
                        m = nc.tensor.matmul(b[:, j * T:(j + 1) * T], ident[0:4, 2 * g + j:2 * g + j + 1].to_broadcast([4, P]), rows[0:4, 0, :],
                                             start=True, stop=True)
                    m.then_inc(*pe_four.tick("bcast", layer, g))
                    b = psum.claim(pe, "bc", layer, g)
                    r = slice(64 * g, 64 * g + 64)
                    causal(b, pj[r, 20, :], pj[r, 21, :]).then_inc(*pe_four.tick("bc", layer, g))
                for r in range(6):
                    b = psum.claim(pe, "rot", layer, r)
                    pe.wait_ge(*dve_four.at("roped in", layer, r))
                    if r < 2:
                        nc.tensor.matmul(b[:, :], rot64[:, :], two(sq, r), start=True, stop=True)\
                            .then_inc(*pe_four.tick("rot", layer, r))
                    else:
                        nc.tensor.matmul(b[0:96, :], rot96[0:96, 0:96], two(xn, r - 2)[0:96, :], start=True, stop=True)\
                            .then_inc(*pe_four.tick("rot", layer, r))
                for h in range(4):
                    b = psum.claim(pe, "z", layer, h)
                    r = slice(64 * (h % 2), 64 * (h % 2) + 64)
                    causal(b, pj[r, 12 + h // 2, :], pj[r, 10 + h // 2, :]).then_inc(*pe_four.tick("z", layer, h))
                for n in range(8 + 2):
                    if n < 8:
                        b = psum.claim(pe, "score", layer, n)
                        pe.wait_ge(*dve_four.at("roped", layer, 1 if n < 4 else 5))
                        if n < 4:
                            r = slice(64 * (n % 2), 64 * (n % 2) + 64)
                            q, k = pj[r, n // 2, :], pj[r, 2 + n // 2, :]
                        else:
                            q, k = yb_t[0:96, n - 4, :], yb_t[0:96, n, :]
                        nc.tensor.matmul(b[:, 0:HALF], q[:, 0:HALF], k[:, 0:HALF], start=True, stop=True)
                        nc.tensor.matmul(b[:, HALF:TRI], q[:, HALF:T], k[:, :], start=True, stop=True)\
                            .then_inc(*pe_four.tick("score", layer, n))
                    if n >= 2:
                        n -= 2
                        b = psum.claim(pe, "probs", layer, n)
                        pe.wait_ge(*dve_four.at("probs", layer, n))
                        p = dec[:, n % 2, :]
                        nc.tensor.transpose(b[:, 0:HALF], p[:, 0:HALF], ident[:, :])
                        nc.tensor.transpose(b[:, HALF:T], p[:, HALF:T], ident[:, :])
                        nc.tensor.transpose(b[:, T:TRI], p[:, T:TRI], ident[:, :])\
                            .then_inc(*pe_four.tick("probs", layer, n))
                for h in range(4):
                    b = psum.claim(pe, "tail", layer, h)
                    pe.wait_ge(*dve_four.at("log1mb", layer, h))
                    l1 = sb_l1[:, h, :]
                    nc.tensor.matmul(b[:, 0:T], later[:, :], l1[:, 0:T], start=True, stop=False, skip_group_check=True)
                    nc.tensor.matmul(b[:, HALF:T], ones[:, :], l1[:, T:TRI], start=False, stop=True, skip_group_check=True)
                    nc.tensor.matmul(b[:, T:TRI], later[:, :], l1[:, T:TRI], start=True, stop=True)\
                        .then_inc(*pe_four.tick("tail", layer, h))
                for m in (0, 1, 3, 2):
                    b = psum.claim(pe, "o", layer, m)
                    pe.wait_ge(*(act_four.at("causal", layer, m) if m < 2 else dve_four.at("causal", layer, m)))
                    mats = at if m < 2 else at2
                    for h in range(4):
                        c = m * T + h * 64
                        last = values(b[64 * (h % 2):64 * (h % 2) + 64, (h // 2) * T:(h // 2 + 1) * T],
                                      vb[:, 0, c:c + 64], vb[:, 1, c:c + 64], mats[:, 4 * (m % 2) + h, :])
                    last.then_inc(*pe_four.tick("o", layer, m))
                for m in (0, 1, 3, 2):
                    b = psum.claim(pe, "o2", layer, m)
                    pe.wait_ge(*act_four.at("o2", layer, m))
                    if m < 3:
                        nc.tensor.matmul(b[:, :], blk64[:, :], two(sq, m), start=True, stop=True)\
                            .then_inc(*pe_four.tick("o2", layer, m))
                    else:
                        nc.tensor.matmul(b[:, 0:T], ones[:, :], sq[:, 6, :], start=True, stop=False)
                        nc.tensor.matmul(b[:, 0:T], ones[:, :], sq[:, 7, :], start=False, stop=True)\
                            .then_inc(*pe_four.tick("o2", layer, m))

            def norm_sums(layer, r):
                b = psum.claim(pe, "n2", layer, r)
                pe.wait_ge(*act_four.at("n2", layer, r))
                if r < 2:
                    m = nc.tensor.matmul(b[:, :], blk64[:, :], nsq(r), start=True, stop=True)
                else:
                    m = nc.tensor.matmul(b[0:96, :], ones[0:96, 0:96], nsq(r)[0:96, :], start=True, stop=True)
                m.then_inc(*pe_four.tick("n2", layer, r))
            def parts(n):
                return dve_norm.at("x hi", n), dve_norm.at("x lo", n)

            setup()
            norm = 0
            for layer, (kind, _) in enumerate(CHAIN[:layers]):
                if kind == "four":
                    rms_sum(norm)
                    norm += 1
                    project(layer, kind, parts(norm - 1))
                    four(layer)
                    out_project(layer)
                    rms_sum(norm)
                    norm += 1
                    ffn(layer, parts(norm - 1))
                else:
                    project(layer, kind, parts(norm - 1))
                    gdn(layer) if kind == "gdn" else gla(layer, kind)
                    out_project(layer)
                    layer_norm(norm)
                    norm += 1
                    ffn(layer, parts(norm - 1))
                    layer_norm(norm)
                    norm += 1
            if CHAIN[layers - 1][0] == "four":
                for n in range(4):
                    pe.wait_ge(*dve_norm.at("residual", norm, n))
            else:
                pe.wait_ge(*dve_norm.at("normed", norm - 1))
            for g in range(4):
                b = psum.claim(pe, "final", g)
                for j in range(4):
                    k, t = 2 * g + j // 2, j % 2
                    m = nc.tensor.transpose(b[:, j * P:(j + 1) * P], x[:, k, t * HALF:(t + 1) * HALF], ident[:, :])
                m.then_inc(*pe_out.tick("final", g))
        @block.sync
        def _(sp):
            unit = 0

            def load(dst, src, i=None):
                nonlocal unit
                if unit >= RING:
                    sp.wait_ge(*of_unit(pe_unit, unit - RING, i))
                sp.dma_start(dst, src).then_inc(w_loaded[unit % RING], 16)
                unit += 1

            def columns(w, l, c0, width):
                src = w[l, :, c0:c0 + width].rearrange("(k p) n -> p k n", p=P)
                return ring[:, unit % RING, 0:KT * width].rearrange("p (k n) -> p k n", k=KT), src

            for dst, src in IN_LOADS:
                sp.dma_start(dst, src, allow_slow_non_contiguous=True).then_inc(in_loaded, 16)
            sp.wait_ge(*pool_setup.at("stage"))
            for dst, src in PARAM_LOADS:
                sp.dma_start(dst, src, allow_slow_non_contiguous=True).then_inc(param_loaded, 16)
            for layer, (kind, l) in enumerate(CHAIN[:layers]):
                w_in, w_out = {"gdn": ("gdn_w_in", "gdn_w_out"), "hgrn": ("hgrn_w_in", "hgrn_w_out"),
                               "gla": ("gla_w_in", "gla_w_out"), "four": ("w_in_2", "w_out_2")}[kind]
                for n, (c0, width, *_) in enumerate(units_in(kind)):
                    load(*columns(A[w_in], l, c0, width))
                if kind == "four":
                    sp.wait_ge(*(pe_gdn.at("o", layer - 1, 3) if layer == DEPTH else pe_four.at("o", layer - 1, 2)))
                    for dst, src in ((mlaw[:, 0:384], A["mla_w_uq_2"][l, 0:P, :]), (mlaw[0:64, 384:768], A["mla_w_uq_2"][l, P:P + 64, :]),
                                     (mlaw[:, 768:1280], A["mla_w_ukv_2"][l, :, :])):
                        sp.dma_start(dst, src).then_inc(mla_loaded, 16)
                if kind == "gla":
                    sp.wait_ge(*pe_gdn.at("o", 0, 3))
                    sp.dma_start(wgk2, A["gla_w_gk2"][l, :, :]).then_inc(gk_loaded, 16)
                for n in range(4):
                    load(*columns(A[w_out], l, 256 * n, 256))
                f_in, f_out, fl = (A["ffn_w_in"], A["ffn_w_down"], layer) if layer < DEPTH else \
                    (A["ffn_w_in_2"], A["ffn_w_out_2"], l)
                F = F_TILES * P
                w_up = f_in[fl, :, :].rearrange("(k p) n -> p k n", p=P)
                w_down = f_out[fl, :, :].rearrange("(k p) n -> p k n", p=P)

                def ffn_load(what, s, i=None):
                    slot = ring[:, unit % RING, :]
                    step = s if i is None else i * 2 + s
                    if what == "down":
                        load(slot.rearrange("p (k n) -> p k n", k=2), w_down[:, bass.ds(step * 2, 2), :], i)
                    else:
                        src = w_up[:, :, bass.ds(step * 256 + (F if what == "up" else 0), 256)]
                        load(slot.rearrange("p (k n) -> p k n", k=KT), src, i)

                def pair(s, i=None):
                    for what, step in (("gate", s), ("up", s), ("down", s - 1), ("gate", s + 1), ("up", s + 1), ("down", s)):
                        ffn_load(what, step, i)

                ffn_load("gate", 0)
                ffn_load("up", 0)
                pair(1)
                u0 = unit
                with Loop(book, sp, f"ffn{layer}", F_PAIRS) as i:
                    pair(3, i)
                unit = u0 + RING * F_PAIRS
                pair(F_STEPS - 2)
                ffn_load("down", F_STEPS - 1)
            for g in range(4):
                sp.wait_ge(*act_out.at("final", g))
                k = 2 * g
                for t in range(2):
                    sp.dma_start(out[0, t * HALF:(t + 1) * HALF, k * P:(k + 2) * P], yt[:, t, k * P:(k + 2) * P]).then_inc(out_stored, 16)
            sp.wait_ge(out_stored, 16 * 8)
        @block.gpsimd
        def _(pool):
            g = nc.gpsimd

            def settled():
                pool.wait_ge(*pool_setup.now())

            def fill(ap, value):
                g.memset(ap, value).then_inc(*pool_setup.tick())

            def keep(ap, pattern, base, row, op=ALU.is_ge, fill_=0.0):
                settled()
                g.affine_select(out=ap, in_=ap, compare_op=op, fill=fill_, base=base, pattern=pattern,
                                channel_multiplier=row).then_inc(*pool_setup.tick())

            g.memset(stage[:, 0:PT_TILES * P], 0.0).then_inc(*pool_setup.tick("stage"))
            fill(ident[:, :], 0.0)
            settled()
            g.affine_select(out=ident[:, :], in_=ident[:, :], compare_op=ALU.not_equal, fill=1.0, base=0,
                            pattern=[[-1, P]], channel_multiplier=1).then_inc(*pool_setup.tick("identity"))
            fill(ones[:, :], 1.0)
            fill(ones_d[:, :], 1.0 / D)
            for c, v in ((C_LN_EPS, 1e-5), (C_RMS_EPS, 1e-6), (C_QSCALE, -0.5 * float(np.log(128.0))),
                         (C_HALFPI, float(np.pi / 2)), (C_ONE, 1.0)):
                fill(const[:, c:c + 1], v)
            for ap in (blk64, incl, strict, later):
                fill(ap[:, :], 1.0)
            for ap in (rot64, rot96, amask):
                fill(ap[:, :], 0.0)
            b = blk64[:, :].rearrange("p (n c) -> p n c", n=2)
            keep(b, [[-64, 2], [0, 64]], 0, 1)
            keep(b, [[64, 2], [0, 64]], 63, -1)
            for c in (0, T):
                keep(incl[:, c:c + HALF], [[1, HALF]], 0, -1)
                keep(strict[:, c:c + HALF], [[1, HALF]], -1, -1)
                keep(amask[:, c:c + HALF], [[-1, HALF]], 0, 1, fill_=-1e30)
            keep(later[:, :], [[-1, P]], -1, 1)
            r = rot64[:, :].rearrange("p (n a c) -> p n a c", n=2, a=2)
            keep(r[:, :, 0, :], [[-64, 2], [-1, 32]], -32, 1, op=ALU.not_equal, fill_=-1.0)
            keep(r[:, :, 1, :], [[-64, 2], [-1, 32]], 0, 1, op=ALU.not_equal, fill_=1.0)
            keep(rot96[:, 64:80], [[-1, 16]], -80, 1, op=ALU.not_equal, fill_=-1.0)
            keep(rot96[:, 80:96], [[-1, 16]], -64, 1, op=ALU.not_equal, fill_=1.0)
            for lv in range(7):
                h = 1 << lv
                m = level[:, lv, :].rearrange("p (n a c) -> p n a c", a=2, c=h)
                fill(m[:, :, 0, :], 0.0)
                fill(m[:, :, 1, :], 1.0)
                keep(m[:, :, 1, :], [[-2 * h, P // (2 * h)], [0, h]], 0, 1)
                keep(m[:, :, 1, :], [[2 * h, P // (2 * h)], [0, h]], h - 1, -1)
            settled()
            g.memset(const[:, 7:8], 0.0).then_inc(*pool_setup.tick("constants"))

            unit = 0

            def split(count, i=None):
                nonlocal unit
                for _ in range(min(count, len(sizes) - unit)):
                    part = slice(sizes[unit] * DVE_SHARE // 8, sizes[unit])
                    pool.wait_ge(*of_unit(dve_hi, unit, i))
                    g.tensor_tensor(w_lo[:, unit % RING, part], ring[:, unit % RING, part], w_hi[:, unit % HI, part], ALU.subtract).then_inc(*pool_lo.tick())
                    unit += 1

            def rest(layer, count):
                nonlocal unit
                split(4 + 2 + RING)
                u0 = unit
                with Loop(book, pool, f"ffn{layer}", F_PAIRS) as i:
                    split(RING, i)
                unit = u0 + RING * F_PAIRS
                split(RING + 1 + count)

            split(HI)
            for layer, (kind, _) in enumerate(CHAIN[:layers]):
                split(len(units_in(kind)) - HI)
                if kind != "gdn":
                    rest(layer, HI)
                    continue
                for h in range(8):
                    pool.wait_ge(*act_gdn.at("decay", layer, h))
                    d = dec[:, h % 2, :]
                    g.tensor_tensor(d, d, incl[:, :], ALU.mult).then_inc(*pool_gdn.tick("decay", layer, h))
                for lv in range(7):
                    for q in range(4):
                        t, h0 = q // 2, 4 * (q % 2)
                        pool.wait_ge(*(dve_gdn.at("lt", layer, h0 + 3) if lv == 0 else pe_gdn.at("cx", layer, lv - 1, q)))
                        g.tensor_tensor(ct[:, 4 * q:4 * q + 4, :], lt[:, h0:h0 + 4, t * T:t * T + HALF],
                                        level[:, lv:lv + 1, :].to_broadcast([P, 4, HALF]), ALU.mult)\
                            .then_inc(*pool_gdn.tick("masked", layer, lv, q))
                rest(layer, HI)
        @block.scalar
        def _(act):
            def run(sig, out_, in_, func, *key, **kw):
                nc.scalar.activation(out_, in_, func, **kw).then_inc(*sig.tick(*key))

            def log_exp_tables():
                nc.scalar.preload_act_table_set("natural_log_exp_and_others")

            def rstd(sig, dst, bank_ap, bank_key, scale, eps, *key, bias=None):
                run(sig, dst, bank_ap, ACT.Ln, scale=scale, bias=const[0:dst.shape[0], eps:eps + 1])
                if bank_key:
                    psum.release(sig, *bank_key)
                act.wait_ge(*sig.now())
                kw = {} if bias is None else {"bias": bias}
                run(sig, dst, dst, ACT.Exp, *key, scale=-0.5, **kw)

            def log1p_exp(sig, ap, in_, *key):
                run(sig, ap, in_, ACT.Abs)
                act.wait_ge(*sig.now())
                run(sig, ap, ap, ACT.Exp, scale=-1.0)
                act.wait_ge(*sig.now())
                run(sig, ap, ap, ACT.Ln, *key, bias=1.0)

            def setup():
                for g in range(3):
                    act.wait_ge(*pe_setup.at("params", g))
                    w = min(512, PT_TILES * P - 512 * g)
                    run(act_setup, params[:, 512 * g:512 * g + w], psum.bank("params", g)[:, 0:w], ACT.Copy, "params", g)
                    psum.release(act_setup, "params", g)
                for g in range(4):
                    act.wait_ge(*pe_setup.at("x", g))
                    run(act_setup, two(x, g), psum.bank("x", g)[:, :], ACT.Copy, "x", g)
                    psum.release(act_setup, "x", g)
                act.wait_ge(*dve_setup.at("angles"))
                run(act_setup, flat(trig), flat(trig), ACT.Sin, "trig")

            def project(layer, kind, l):
                for n, (c0, w, how, name, idx) in enumerate(units_in(kind)):
                    key = ("proj", layer, n)
                    b = psum.bank(*key)
                    s = act_proj
                    if name in ("conv", "xbc"):
                        act.wait_ge(*dve_conv.at("conv", layer, idx // 2))
                        if name == "conv":
                            run(s, pj2(idx), pj2(idx), ACT.Silu, "conv", layer, idx // 2)
                        else:
                            for c in (idx, idx + 1):
                                run(s, pj[:, 18 + c, :], pj[:, 18 + c, :], ACT.Silu, "xbc", layer, idx // 2,
                                    bias=par(PT_MISC * P + R_CONVB + l * 4 + c))
                        continue
                    act.wait_ge(*pe_unit.at("unit", layer, n))
                    if name == "ba":
                        run(s, rows[0:8, 2:4, :].rearrange("p a n -> p (a n)"), b[0:8, :], ACT.Copy, "ba", layer)
                    elif name == "gate":
                        run(s, pj2(24 + idx), b[:, :], ACT.Silu, "gate", layer, idx)
                    elif name == "f":
                        run(s, pj2(8 + idx), b[:, :], ACT.Copy, "f", layer, idx)
                    elif name == "qsilu":
                        run(s, pj2(idx), b[:, :], ACT.Silu, "q", layer, idx)
                    elif name in ("v", "vmoba", "vsb"):
                        c = {"v": T * idx, "vmoba": 0, "vsb": 2 * T}[name]
                        run(s, vb[:, :, c:c + T], b[:, :].rearrange("p (t n) -> p t n", t=2), ACT.Copy, name, layer, idx)
                    elif name == "gk":
                        run(s, rows[0:16, 4, :], b[0:16, 0:T], ACT.Copy, "gk", layer)
                    elif name == "qscaled":
                        run(s, pj2(idx), b[:, :], ACT.Copy, "q", layer, idx, scale=128.0 ** -0.5)
                    elif name == "k":
                        run(s, pj2(4 + idx), b[:, :], ACT.Copy, "k", layer, idx)
                    elif name == "dt":
                        run(s, rows[0:4, 2, :], b[0:4, 0:T], ACT.Copy, "dt", layer)
                    elif name == "plain":
                        run(s, pj2(idx), b[:, :], ACT.Copy, "plain", layer, idx)
                    elif name == "cq":
                        run(s, pj[:, 6, :], b[:, 0:T], ACT.Copy)
                        run(s, pj[0:64, 7, :], b[0:64, T:2 * T], ACT.Copy, "cq", layer)
                    elif name == "ckv":
                        run(s, pj[:, 8, :], b[:, 0:T], ACT.Copy)
                        run(s, yb_t[64:96, 4:8, :], b[64:96, T:2 * T].rearrange("p (a n) -> p a n", a=1).to_broadcast([32, 4, T]),
                            ACT.Copy, "ckv", layer)
                    elif name == "z":
                        run(s, pj2(16), b[:, :], ACT.Silu, "z", layer)
                    psum.release(s, *key)
                act.wait_ge(*act_proj.now())
                log_exp_tables()

            def norm_rstd(n, eps):
                act.wait_ge(*pe_norm.at("square", n))
                rstd(act_norm, stat[:, 0, 0:T], psum.bank("square", n)[:, 0:T], ("square", n), 1.0, eps, "rstd", n)

            def layer_norm(n):
                for m in range(4):
                    act.wait_ge(*dve_norm.at("centred", n, m))
                    run(act_norm, two(sq, m), two(xn, m), ACT.Square, "square", n, m)
                norm_rstd(n, C_LN_EPS)

            def rms_norm(n, ready):
                for m in range(4):
                    act.wait_ge(*ready(m))
                    run(act_norm, two(sq, m), two(x, m), ACT.Square, "square", n, m)
                norm_rstd(n, C_RMS_EPS)

            def ffn(layer):
                conv = layer >= DEPTH

                def gated(par_, key, before):
                    src = fconv[:, par_, 0:2, :].rearrange("p a n -> p (a n)") if conv else banks[4 + 2 * par_][:, :]
                    act.wait_ge(*(dve_ffn.at("conv gate", layer, key) if conv else pe_unit.at("gate", layer, key)))
                    if before is not None:
                        act.wait_ge(*before)
                    run(act_ffn, flat(gact[:, par_]), src, ACT.Silu, "gated", layer, key)

                gated(0, 0, None)
                gated(1, 1, None)
                gated(0, 2, dve_ffn.at("hidden", layer, 0))
                with Loop(book, act, f"ffn{layer}", F_PAIRS):
                    gated(1, "a", dve_ffn.at("hidden", layer, "a", ago=1))
                    gated(0, "b", dve_ffn.at("hidden", layer, "b", ago=1))
                gated(1, 9, dve_ffn.at("hidden", layer, "a"))
                gated(0, 10, dve_ffn.at("hidden", layer, "b"))

            def head_norms(layer, sig, pe_sig, n, both, inv_dv):
                for g in range(n):
                    act.wait_ge(*pe_sig.at("o", layer, g))
                    b = psum.bank("o", layer, g)
                    run(sig, oc[:, g, :], b[:, :], ACT.Copy, "o", layer, g)
                    run(sig, two(sq, g), b[:, :], ACT.Square, "o2", layer, g)
                    psum.release(sig, "o", layer, g)
                for g in range(n):
                    act.wait_ge(*pe_sig.at("o2", layer, g))
                    w = T if both else 2 * T
                    rstd(sig, stat[:, g, 0:w], psum.bank("o2", layer, g)[:, 0:w], ("o2", layer, g), inv_dv, C_RMS_EPS,
                         "rstd", layer, g)

            def gdn(layer, l):
                s = act_gdn
                for g in range(8):
                    run(s, gsq(g), pj2(2 * g), ACT.Square, "square", layer, g)
                act.wait_ge(*dve_gdn.at("a + bias", layer))
                log1p_exp(s, rows[0:8, 4:6, :].rearrange("p a n -> p (a n)"), rows[0:8, 2:4, :].rearrange("p a n -> p (a n)"),
                          "log1p", layer)
                run(s, head[0:8, 6:7], head[0:8, l:l + 1], ACT.Exp, "a", layer)
                act.wait_ge(*dve_gdn.at("log beta", layer))
                run(s, rows[0:8, 1, :], rows[0:8, 1, :], ACT.Exp, "beta", layer)
                for g in range(8):
                    act.wait_ge(*pe_gdn.at("qk2", layer, g))
                    if g >= 4:
                        act.wait_ge(*dve_gdn.at("unit", layer, g - 4))
                    rstd(s, stat[:, g % 4, :], psum.bank("qk2", layer, g)[:, :], ("qk2", layer, g), 1.0, C_RMS_EPS,
                         "rstd", layer, "qk", g, bias=const[:, C_QSCALE:C_QSCALE + 1] if g < 4 else None)
                for h in range(8):
                    act.wait_ge(*dve_gdn.at("difference", layer, h))
                    d = dec[:, h % 2, :]
                    run(s, d, d, ACT.Exp, "decay", layer, h)
                for lv in range(7):
                    for g in range(4):
                        act.wait_ge(*pe_gdn.at("cx", layer, lv, g))
                        run(s, four_tiles(yb, g), psum.bank("cx", layer, lv, g)[:, :], ACT.Copy, "cx", layer, lv, g)
                        psum.release(s, "cx", layer, lv, g)
                for what, t in (("u0", 0), ("u1", 1)):
                    for g in range(2):
                        act.wait_ge(*pe_gdn.at(what, layer, g))
                        run(s, four_tiles(ct, 2 * t + g), psum.bank(what, layer, g)[:, :], ACT.Copy, what, layer, g)
                        psum.release(s, what, layer, g)
                head_norms(layer, s, pe_gdn, 4, False, 1.0 / 128)

            def gla(layer, kind, l):
                s = act_gla
                heads = 8 if kind == "hgrn" else 4
                n = heads * T
                if kind == "hgrn":
                    act.wait_ge(*dve_gla.at("logits", layer))
                    run(s, flat(lbs[:, 0:4]), flat(lbs[:, 0:4]), ACT.Exp, "exp logits", layer)
                    act.wait_ge(*dve_gla.at("bounds", layer))
                    run(s, flat(lbs[:, 4:6]), flat(lbs[:, 4:6]), ACT.Ln, "log bounds", layer)
                else:
                    for g in range(2):
                        act.wait_ge(*pe_gla.at("gk", layer, g))
                        b = psum.bank("gk", layer, g)
                        for j in range(2):
                            c = 2 * g + j
                            run(s, pj[:, 8 + c, :], b[:, j * T:(j + 1) * T], ACT.Identity, "gk", layer, g,
                                bias=par(PT_MISC * P + R_BGK + c))
                        psum.release(s, "gk", layer, g)
                f = flat(pj[:, 8:8 + heads, :])
                act.wait_ge(*(act_proj.at("f", layer, 6) if kind == "hgrn" else s.now()))
                run(s, flat(ct)[:, 0:n], f, ACT.Abs)
                act.wait_ge(*s.now())
                run(s, flat(ct)[:, 0:n], flat(ct)[:, 0:n], ACT.Exp, scale=-1.0)
                act.wait_ge(*s.now())
                run(s, flat(sq)[:, 0:n], flat(ct)[:, 0:n], ACT.Ln, "log1p f", layer, bias=1.0)
                if kind == "hgrn":
                    act.wait_ge(*dve_gla.at("log k", layer))
                    for h in range(8):
                        run(s, yb_t[:, h, :], ct_t[:, h, :], ACT.Exp, "k", layer, bias=lbs[:, 5, h:h + 1])
                    act.wait_ge(*dve_gla.at("f against bound", layer))
                    run(s, flat(sq), flat(sq), ACT.Abs)
                    act.wait_ge(*s.now())
                    run(s, flat(sq), flat(sq), ACT.Exp, scale=-1.0)
                    act.wait_ge(*s.now())
                    run(s, flat(ct), flat(sq), ACT.Ln, "log1p f2", layer, bias=1.0)
                else:
                    run(s, const[:, 6:7], const[:, 0:1], ACT.Copy, "k", layer)
                for lv in range(8):
                    act.wait_ge(*dve_gla.at("difference", layer, lv))
                    d = level_diff(lv, heads)
                    run(s, d[:, :, 0:1 << lv], d[:, :, 0:1 << lv], ACT.Exp, scale=-1.0)
                    run(s, d[:, :, 1 << lv:], d[:, :, 1 << lv:], ACT.Exp, "decay", layer, lv)
                head_norms(layer, s, pe_gla, 4, kind == "gla", 1.0 / (128 if kind == "hgrn" else 256))

            def four(layer, l):
                s = act_four
                run(s, flat(sq[:, 0:3, :])[:, 0:T], pj[:, 6, :], ACT.Square)
                run(s, sq[0:64, 1, :], pj[0:64, 7, :], ACT.Square)
                run(s, sq[:, 2, :], pj[:, 8, :], ACT.Square, "csq", layer)
                for r in range(2):
                    run(s, nsq(r), pj2(2 * r), ACT.Square, "n2", layer, r)
                act.wait_ge(*dve_four.at("dt + bias", layer))
                log1p_exp(s, rows[0:4, 3, :], rows[0:4, 2, :], "log1p dt", layer)
                run(s, head[0:4, 6:7], hssm[0:4, l:l + 1], ACT.Exp, "a", layer)
                act.wait_ge(*pe_four.at("c2", layer))
                b = psum.bank("c2", layer)
                rstd(s, stat[:, 3, 0:T], b[:, 0:T], None, 1.0 / 192, C_RMS_EPS, "c rstd", layer, 0)
                rstd(s, stat[:, 3, T:2 * T], b[:, T:2 * T], ("c2", layer), 1.0 / 128, C_RMS_EPS, "c rstd", layer, 1)
                for r in range(2):
                    act.wait_ge(*pe_four.at("n2", layer, r))
                    rstd(s, stat[:, r, :], psum.bank("n2", layer, r)[:, :], ("n2", layer, r), 1.0 / 64, C_RMS_EPS,
                         "rstd", layer, "n", r)
                for g in range(2):
                    act.wait_ge(*pe_four.at("mlaq", layer, g))
                    run(s, yb_t[0:96, 2 * g:2 * g + 2, :].rearrange("p a n -> p (a n)"),
                        psum.bank("mlaq", layer, g)[0:96, :], ACT.Copy, "mlaq", layer, g)
                    psum.release(s, "mlaq", layer, g)
                for g in range(2):
                    act.wait_ge(*pe_four.at("mlak", layer, g))
                    run(s, yb_t[0:64, 4 + 2 * g:6 + 2 * g, :].rearrange("p a n -> p (a n)"),
                        psum.bank("mlak", layer, g)[0:64, :], ACT.Copy, "mlak", layer, g)
                    psum.release(s, "mlak", layer, g)
                act.wait_ge(*pe_four.at("mlav", layer))
                run(s, vb[:, :, T:2 * T], psum.bank("mlav", layer)[:, :].rearrange("p (t n) -> p t n", t=2), ACT.Copy,
                    "mlav", layer)
                psum.release(s, "mlav", layer)
                for r in range(2, 6):
                    act.wait_ge(*s.at("mlaq" if r < 4 else "mlak", layer, r % 2))
                    run(s, nsq(r)[0:96, :], flat(yb_t[:, 2 * (r - 2):2 * (r - 2) + 2, :])[0:96, :], ACT.Square, "n2", layer, r)
                for r in range(2, 6):
                    act.wait_ge(*pe_four.at("n2", layer, r))
                    act.wait_ge(*(dve_four.at("cn", layer) if r < 4 else dve_four.at("roped in", layer, r - 4)))
                    rstd(s, stat[0:96, r % 4, :], psum.bank("n2", layer, r)[0:96, :], ("n2", layer, r), 1.0 / 96, C_RMS_EPS,
                         "rstd", layer, "n", r)
                for h in range(4):
                    act.wait_ge(*dve_four.at("difference", layer, h))
                    run(s, at[:, h, :], at[:, h, :], ACT.Exp, "decay", layer, h)
                for h in range(4):
                    act.wait_ge(*dve_four.at("z", layer, h))
                    log1p_exp(s, sb_t[:, h, :], at2[:, h, :], "log1p z", layer, h)
                act.wait_ge(*dve_four.at("causal", layer, 3))
                for n in range(8 + 2):
                    if n < 8:
                        act.wait_ge(*dve_four.at("max", layer, n))
                        p = dec[:, n % 2, :]
                        run(s, p[:, 0:HALF], p[:, 0:HALF], ACT.Exp, bias=small[:, n, 0:1], accum_out=small[:, n, 2:3])
                        run(s, p[:, HALF:TRI], p[:, HALF:TRI], ACT.Exp, "exp", layer, n, bias=small[:, n, 1:2],
                            accum_out=small[:, n, 3:4])
                    if n >= 2:
                        n -= 2
                        act.wait_ge(*pe_four.at("probs", layer, n))
                        b = psum.bank("probs", layer, n)
                        run(s, at[:, n, :], b[:, 0:TRI], ACT.Copy, "causal", layer, n // 4)
                        psum.release(s, "probs", layer, n)
                for h in range(4):
                    act.wait_ge(*dve_four.at("log a", layer, h))
                    run(s, sb_t[:, h, :], sb_t[:, h, :], ACT.Exp, "a", layer, h)
                act.wait_ge(*dve_four.at("causal", layer, 2))
                for m in (0, 1, 3, 2):
                    if m < 3:
                        act.wait_ge(*pe_four.at("o", layer, m))
                        b = psum.bank("o", layer, m)
                        run(s, oc4[:, m, :], b[:, :], ACT.Copy, "o", layer, m)
                        run(s, two(sq, m), b[:, :], ACT.Square, "o2", layer, m)
                        psum.release(s, "o", layer, m)
                    else:
                        act.wait_ge(*dve_four.at("gated", layer))
                        run(s, two(sq, 3), oc4[:, 3, :], ACT.Square, "o2", layer, 3)
                for m in (0, 1, 3, 2):
                    act.wait_ge(*pe_four.at("o2", layer, m))
                    w, sc = (2 * T, 1.0 / 64) if m < 3 else (T, 1.0 / 256)
                    rstd(s, stat[:, m, 0:w], psum.bank("o2", layer, m)[:, 0:w], ("o2", layer, m), sc, C_RMS_EPS,
                         "rstd", layer, m)

            act.wait_ge(*pool_setup.at("constants"))
            setup()
            norm = 0
            for layer, (kind, l) in enumerate(CHAIN[:layers]):
                if kind == "four":
                    rms_norm(norm, (lambda m: dve_norm.at("normed", norm - 1)) if layer == DEPTH else
                             (lambda m: dve_norm.at("residual", norm - 0, m)))
                    norm += 1
                    project(layer, kind, l)
                    four(layer, l)
                    rms_norm(norm, lambda m: dve_norm.at("residual", norm, m))
                    norm += 1
                    ffn(layer)
                else:
                    project(layer, kind, l)
                    gdn(layer, l) if kind == "gdn" else gla(layer, kind, l)
                    layer_norm(norm)
                    norm += 1
                    ffn(layer)
                    log_exp_tables()
                    layer_norm(norm)
                    norm += 1
            for g in range(4):
                act.wait_ge(*pe_out.at("final", g))
                run(act_out, yt[:, :, 2 * g * P:(2 * g + 2) * P].rearrange("p t (k n) -> p k t n", k=2),
                    psum.bank("final", g)[:, :].rearrange("p (k t n) -> p k t n", k=2, t=2), ACT.Copy, "final", g)
        @block.vector
        def _(dve):
            v = nc.vector

            def tt(sig, out_, a, b, op, *key):
                v.tensor_tensor(out_, a, b, op).then_inc(*sig.tick(*key))

            def ts(sig, out_, a, s1, op0, s2=None, op1=None, *key):
                if op1 is None:
                    v.tensor_scalar(out_, a, s1, None, op0).then_inc(*sig.tick(*key))
                else:
                    v.tensor_scalar(out_, a, s1, s2, op0, op1).then_inc(*sig.tick(*key))

            def stt(sig, out_, a, s1, b, op0, op1, *key):
                v.scalar_tensor_tensor(out=out_, in0=a, scalar=s1, in1=b, op0=op0, op1=op1).then_inc(*sig.tick(*key))

            def scan(sig, out_, in_, *key):
                n = in_.shape[0]
                v.tensor_tensor_scan(out_, const[0:n, C_ONE:C_ONE + 1].to_broadcast([n, T]), in_, 0.0, ALU.mult, ALU.add)\
                    .then_inc(*sig.tick(*key))

            def conv(sig, dsts, srcs, weights, taps, key, biases=None, interleaved=None):
                for n, (d, s) in enumerate(zip(dsts, srcs)):
                    if biases is None:
                        ts(sig, d, s, weights(n, taps - 1), ALU.mult)
                    else:
                        ts(sig, d, s, weights(n, taps - 1), ALU.mult, biases(n), ALU.add)
                for back in range(1, taps):
                    dve.wait_ge(*sig.now())
                    for n, (d, s) in enumerate(zip(dsts, srcs)):
                        k = key if back == taps - 1 else ()
                        stt(sig, d[:, back:T], s[:, 0:T - back], weights(n, taps - 1 - back), d[:, back:T],
                            ALU.mult, ALU.add, *k)

            unit = 0

            def split(count=1, i=None):
                nonlocal unit
                for _ in range(min(count, len(sizes) - unit)):
                    n, share = sizes[unit], sizes[unit] * DVE_SHARE // 8
                    w, high = ring[:, unit % RING, :], w_hi[:, unit % HI, :]
                    dve.wait_ge(*loaded(unit, i))
                    if unit >= HI:
                        dve.wait_ge(*of_unit(pe_unit, unit - HI, i))
                    v.tensor_copy(high[:, 0:n], w[:, 0:n]).then_inc(*dve_hi.tick())
                    dve.wait_ge(*of_unit(dve_hi, unit, i))
                    v.tensor_tensor(w_lo[:, unit % RING, 0:share], w[:, 0:share], high[:, 0:share], ALU.subtract).then_inc(*dve_lo.tick())
                    unit += 1

            def halves(sig, high, low, src, *key):
                for a, b in zip(high, src):
                    v.tensor_copy(a, b).then_inc(*sig.tick(key[0] + " hi", *key[1:]))
                dve.wait_ge(*sig.now())
                for a, b, c in zip(low, src, high):
                    tt(sig, a, b, c, ALU.subtract, key[0] + " lo", *key[1:])

            def input_halves(sig, src, *key):
                halves(sig, *([two(a, g) for g in range(4)] for a in (xh, xl, src)), *key)

            def setup():
                s = dve_setup
                dve.wait_ge(*pool_setup.at("constants"))
                dve.wait_ge(in_loaded, 16 * N_IN)
                v.tensor_copy(trig[:, 0, :], pos_i).then_inc(*s.tick())
                dve.wait_ge(*s.now())
                ts(s, trig[:, 3, :], trig[:, 0, :], freqs[:, 1:2], ALU.mult)
                ts(s, trig[:, 1, :], trig[:, 0, :], freqs[:, 0:1], ALU.mult)
                turn = sq[:, 0:4, :]
                for j in (1, 3):
                    dve.wait_ge(*s.now())
                    ts(s, turn[:, j, :], trig[:, j, :], float(1 / (2 * np.pi)), ALU.mult)
                    dve.wait_ge(*s.now())
                    ts(s, turn[:, j, :], turn[:, j, :], 12582912.0, ALU.add)
                    dve.wait_ge(*s.now())
                    ts(s, turn[:, j, :], turn[:, j, :], 12582912.0, ALU.subtract)
                    for part in TWO_PI:
                        dve.wait_ge(*s.now())
                        stt(s, trig[:, j, :], turn[:, j, :], -part, trig[:, j, :], ALU.mult, ALU.add)
                    dve.wait_ge(*s.now())
                    ts(s, trig[:, j - 1, :], trig[:, j, :], float(np.pi / 2), ALU.add)
                    dve.wait_ge(*s.now())
                    ts(s, turn[:, j, :], trig[:, j - 1, :], float(np.pi), ALU.is_gt, float(-2 * np.pi), ALU.mult)
                    dve.wait_ge(*s.now())
                    tt(s, trig[:, j - 1, :], trig[:, j - 1, :], turn[:, j, :], ALU.add)
                dve.wait_ge(*s.now())
                ts(s, flat(trig), flat(trig), 3.1415925, ALU.min, -3.1415925, ALU.max, "angles")

            def project(layer, kind, l):
                for n, (c0, w, how, name, idx) in enumerate(units_in(kind)):
                    if n + HI < len(units_in(kind)):
                        split()
                    if name not in ("conv", "xbc"):
                        continue
                    base, tiles, n_tiles = (0, (PT_CONV + l) * P, 24) if name == "conv" else \
                        (18, PT_SSM * P + l * 16, 4)
                    dve.wait_ge(*pe_unit.at("unit", layer, n))
                    b = psum.bank("proj", layer, n)
                    conv(dve_conv, [pj[:, base + idx + j, :] for j in range(2)], [b[:, j * T:(j + 1) * T] for j in range(2)],
                         lambda j, tap: par(tiles + tap * n_tiles + idx + j), 4, ("conv", layer, idx // 2))
                    psum.release(dve_conv, "proj", layer, n)

            def residual(n, key, scale):
                for m in range(4):
                    if key[0] == "out":
                        split()
                    dve.wait_ge(*(pe_unit.at("out", key[1], m) if key[0] == "out" else pe_unit.at("down", key[1], "last")))
                    b = psum.bank(*key, m)[:, :]
                    xm = two(x, m)
                    if scale is None:
                        tt(dve_norm, xm, xm, b, ALU.add, "residual", n, m)
                    else:
                        stt(dve_norm, xm, xm, scale, b, ALU.mult, ALU.add, "residual", n, m)
                    psum.release(dve_norm, *key, m)

            def layer_norm(n, g_col, b_col, is_input=True):
                s = dve_norm
                dve.wait_ge(*pe_norm.at("mean", n))
                mean = psum.bank("mean", n)[:, 0:T].rearrange("p (a n) -> p a n", a=1).to_broadcast([P, 2, T])
                for m in range(4):
                    tt(s, xn[:, 2 * m:2 * m + 2, :], x[:, 2 * m:2 * m + 2, :], mean, ALU.subtract, "centred", n, m)
                psum.release(s, "mean", n)
                dve.wait_ge(*act_norm.at("rstd", n))
                for k in range(KT):
                    stt(s, x[:, k, :], xn[:, k, :], par(g_col + k), stat[:, 0, 0:T], ALU.mult, ALU.mult)
                dve.wait_ge(*s.now())
                for k in range(KT):
                    ts(s, x[:, k, :], x[:, k, :], par(b_col + k), ALU.add, None, None, "normed", n)
                if is_input:
                    dve.wait_ge(*s.now())
                    input_halves(s, x, "x", n)

            def rms_norm(n, g_col):
                dve.wait_ge(*act_norm.at("rstd", n))
                for k in range(KT):
                    stt(dve_norm, xn[:, k, :], x[:, k, :], par(g_col + k), stat[:, 0, 0:T], ALU.mult, ALU.mult,
                        "normed", n)
                dve.wait_ge(*dve_norm.now())
                input_halves(dve_norm, xn, "x", n)

            def ffn(layer, l):
                nonlocal unit
                s = dve_ffn
                conv_ffn = layer >= DEPTH

                def step(par_, key, i, f0):
                    if not conv_ffn:
                        split(2, i)
                        dve.wait_ge(*pe_unit.at("up", layer, key))
                        dve.wait_ge(*act_ffn.at("gated", layer, key))
                        tt(s, flat(hid[:, par_]), flat(gact[:, par_]), banks[5 + 2 * par_][:, :], ALU.mult, "hidden", layer, key)
                        dve.wait_ge(*s.now())
                        halves(s, [flat(hid_hi[:, par_])], [flat(hid_lo[:, par_])], [flat(hid[:, par_])], "hidden", layer, key)
                        return
                    for part, what in enumerate(("gate", "up")):
                        split(1, i)
                        b = banks[4 + 2 * par_ + part]
                        dve.wait_ge(*pe_unit.at(what, layer, key))

                        def at_tile(col, j):
                            c = col + part * F_TILES + f0 + j
                            return params[:, c:c + 1] if i is None else params[:, bass.ds(i * 4 + c, 1)]

                        conv(s, [fconv[:, par_, 2 * part + j, :] for j in range(2)], [b[:, j * T:(j + 1) * T] for j in range(2)],
                             lambda j, tap: at_tile(PT_FFN * P + (l * 3 + tap) * 2 * F_TILES, j), 3,
                             ("conv " + what, layer, key), biases=lambda j: at_tile(FFN_BIAS + l * 2 * F_TILES, j))
                    dve.wait_ge(*act_ffn.at("gated", layer, key))
                    dve.wait_ge(*s.now())
                    tt(s, flat(hid[:, par_]), flat(gact[:, par_]), flat(fconv[:, par_, 2:4, :]), ALU.mult, "hidden", layer, key)
                    dve.wait_ge(*s.now())
                    halves(s, [flat(hid_hi[:, par_])], [flat(hid_lo[:, par_])], [flat(hid[:, par_])], "hidden", layer, key)

                step(0, 0, None, 0)
                for k in (1, 2):
                    step(k % 2, k, None, 2 * k)
                    split()
                u0 = unit
                with Loop(book, dve, f"ffn{layer}", F_PAIRS) as i:
                    step(1, "a", i, 6)
                    split(1, i)
                    step(0, "b", i, 8)
                    split(1, i)
                unit = u0 + RING * F_PAIRS
                for k in (9, 10):
                    step(k % 2, k, None, 2 * k)
                    split()
                dve.wait_ge(*s.now())
                for b in range(4, 8):
                    psum.release(s, "ffn", layer, b)

            def head_norms(layer, sig, act_sig, pe_sig, both, w_col, w_step):
                dve.wait_ge(*pe_sig.at("o", layer, 3))
                split(HI)
                for g in range(4):
                    dve.wait_ge(*act_sig.at("rstd", layer, g))
                    if both:
                        r = stat[:, g:g + 1, 0:T].to_broadcast([P, 2, T])
                        tt(sig, oc[:, g, :].rearrange("p (a n) -> p a n", a=2), oc[:, g, :].rearrange("p (a n) -> p a n", a=2), r, ALU.mult)
                    else:
                        tt(sig, oc[:, g, :], oc[:, g, :], stat[:, g, :], ALU.mult)
                dve.wait_ge(*sig.now())
                dve.wait_ge(*act_proj.at("gate", layer, 6))
                for g in range(4):
                    for j in range(2):
                        k = 2 * g + j
                        stt(sig, y[:, k, :], oc[:, g, j * T:(j + 1) * T], par(w_col + w_step * j), pj[:, 24 + k, :],
                            ALU.mult, ALU.mult)
                dve.wait_ge(*sig.now())
                input_halves(sig, y, "mixed", layer)

            def gdn(layer, l):
                s = dve_gdn
                dve.wait_ge(*act_proj.at("ba", layer))
                ts(s, rows[0:8, 3, :], rows[0:8, 3, :], head[0:8, 2 + l:3 + l], ALU.add, None, None, "a + bias", layer)
                dve.wait_ge(*act_gdn.at("log1p", layer))
                stt(s, rows[0:8, 1, :], rows[0:8, 2, :], 0.0, rows[0:8, 4, :], ALU.min, ALU.subtract, "log beta", layer)
                stt(s, rows[0:8, 3, :], rows[0:8, 3, :], 0.0, rows[0:8, 5, :], ALU.max, ALU.add)
                dve.wait_ge(*act_gdn.at("a", layer))
                dve.wait_ge(*s.now())
                ts(s, rows[0:8, 3, :], rows[0:8, 3, :], head[0:8, 6:7], ALU.mult, -1.0, ALU.mult)
                dve.wait_ge(*s.now())
                scan(s, rows[0:8, 0, :], rows[0:8, 3, :])
                dve.wait_ge(*s.now())
                dve.wait_ge(*act_gdn.at("beta", layer))
                v.tensor_copy(rows[0:8, 5, :], rows[0:8, 1, :]).then_inc(*s.tick("rows", layer))
                dve.wait_ge(*pe_unit.at("unit", layer, len(units_in("gdn")) - 1))
                v.tensor_copy(inv[:, :, :], ident[:, :].rearrange("p (a n) -> p a n", a=1).to_broadcast([P, 32, P]))\
                    .then_inc(*s.tick("eye", layer))
                for g in range(8):
                    dve.wait_ge(*act_gdn.at("rstd", layer, "qk", g))
                    tt(s, pj2(2 * g), pj2(2 * g), stat[:, g % 4, :], ALU.mult, "unit", layer, g)
                dve.wait_ge(*pe_gdn.at("tok", layer))
                v.tensor_copy(cols[:, 0:4, 0:8], psum.bank("tok", layer)[:, 0:32].rearrange("p (a h) -> p a h", a=4))\
                    .then_inc(*s.tick("tok", layer))
                psum.release(s, "tok", layer)
                dve.wait_ge(*s.now())
                for g in range(4):
                    t, h0 = g // 2, 4 * (g % 2)
                    dve.wait_ge(*pe_gdn.at("v", layer, g))
                    tt(s, vb[:, t, h0 * P:(h0 + 4) * P].rearrange("p (h n) -> p h n", h=4),
                       psum.bank("v", layer, g)[:, :].rearrange("p (h n) -> p h n", h=4),
                       cols[:, 2 * t + 1, h0:h0 + 4].rearrange("p (h n) -> p h n", n=1).to_broadcast([P, 4, P]), ALU.mult,
                       "vb", layer)
                    psum.release(s, "v", layer, g)

                def scores(h):
                    dve.wait_ge(*pool_gdn.at("decay", layer, h))
                    dve.wait_ge(*pe_gdn.at("kk", layer, h))
                    tt(s, lt[:, h, :], psum.bank("kk", layer, h)[:, 0:TRI], dec[:, h % 2, :], ALU.mult, "lt", layer, h)
                    psum.release(s, "kk", layer, h)
                    dve.wait_ge(*pe_gdn.at("qk", layer, h))
                    tt(s, at[:, h, :], psum.bank("qk", layer, h)[:, 0:TRI], dec[:, h % 2, :], ALU.mult)
                    psum.release(s, "qk", layer, h)

                for h in range(8):
                    dve.wait_ge(*pe_gdn.at("bcast", layer, h))
                    dve.wait_ge(*s.now())
                    b = psum.bank("bcast", layer, h)
                    ts(s, dec[:, h % 2, 0:T], b[:, 0:T], cols[:, 0, h:h + 1], ALU.subtract, 0.0, ALU.min)
                    ts(s, dec[:, h % 2, T:TRI], b[:, HALF:T], cols[:, 2, h:h + 1], ALU.subtract, 0.0, ALU.min,
                       "difference", layer, h)
                    tt(s, sq[:, h, :], pj[:, 8 + h, :], b[:, T:2 * T], ALU.mult, "kbeta", layer, h)
                    psum.release(s, "bcast", layer, h)
                    if h:
                        scores(h - 1)
                scores(7)
                for lv in range(7):
                    for g in range(4):
                        if lv < 6:
                            dve.wait_ge(*pe_gdn.at("z", layer, lv, g))
                            tt(s, four_tiles(inv, g), four_tiles(inv, g), psum.bank("z", layer, lv, g)[:, :], ALU.subtract)
                            psum.release(s, "z", layer, lv, g)
                        dve.wait_ge(*pe_gdn.at("zt", layer, lv, g))
                        tt(s, four_tiles(inv, 4 + g), four_tiles(inv, 4 + g), psum.bank("zt", layer, lv, g)[:, :],
                           ALU.subtract, "inv", layer, lv, g)
                        psum.release(s, "zt", layer, lv, g)
                for g in range(2):
                    dve.wait_ge(*pe_gdn.at("lu", layer, g))
                    r = vb[:, 1, 512 * g:512 * (g + 1)]
                    tt(s, r, r, psum.bank("lu", layer, g)[:, :], ALU.subtract, "rhs", layer, g)
                    psum.release(s, "lu", layer, g)
                head_norms(layer, s, act_gdn, pe_gdn, False, PT_MISC * P + R_GDN + l, 0)

            def gla(layer, kind, l):
                s = dve_gla
                heads = 8 if kind == "hgrn" else 4
                n = heads * T
                f = flat(pj[:, 8:8 + heads, :])
                q = pj[:, 0:heads, :]
                kk = yb_t if kind == "hgrn" else pj[:, 4:8, :]
                if kind == "hgrn":
                    lg = params[:, PT_MISC * P + R_LB:PT_MISC * P + R_LB + 32].rearrange("p (d k) -> p d k", d=4)
                    m = lbs[:, 6, :]
                    tt(s, m, lg[:, 0, :], lg[:, 1, :], ALU.max)
                    for d in (2, 3):
                        dve.wait_ge(*s.now())
                        tt(s, m, m, lg[:, d, :], ALU.max)
                    dve.wait_ge(*s.now())
                    tt(s, lbs[:, 0:4, :], lg, lbs[:, 6:7, :].to_broadcast([P, 4, KT]), ALU.subtract, "logits", layer)
                    dve.wait_ge(*act_gla.at("exp logits", layer))
                    tt(s, lbs[:, 6, :], lbs[:, 0, :], lbs[:, 1, :], ALU.add)
                    tt(s, lbs[:, 7, :], lbs[:, 2, :], lbs[:, 3, :], ALU.add)
                    dve.wait_ge(*s.now())
                    tt(s, lbs[:, 6, :], lbs[:, 6, :], lbs[:, 7, :], ALU.add)
                    dve.wait_ge(*s.now())
                    v.reciprocal(lbs[:, 6, :], lbs[:, 6, :]).then_inc(*s.tick())
                    dve.wait_ge(*s.now())
                    tt(s, lbs[:, 0:2, :], lbs[:, 0:2, :], lbs[:, 6:7, :].to_broadcast([P, 2, KT]), ALU.mult)
                    dve.wait_ge(*s.now())
                    tt(s, lbs[:, 4, :], lbs[:, 0, :], lbs[:, 1, :], ALU.add)
                    dve.wait_ge(*s.now())
                    tt(s, lbs[:, 4, :], lbs[:, 4, :], lbs[:, 0, :], ALU.subtract)
                    dve.wait_ge(*s.now())
                    ts(s, lbs[:, 5, :], lbs[:, 4, :], -1.0, ALU.mult, 1.0, ALU.add)
                    dve.wait_ge(*s.now())
                    ts(s, flat(lbs[:, 4:6]), flat(lbs[:, 4:6]), 1e-19, ALU.max, None, None, "bounds", layer)
                    dve.wait_ge(*act_proj.at("f", layer, 6))
                else:
                    dve.wait_ge(*act_gla.at("gk", layer, 1))
                dve.wait_ge(*act_gla.at("log1p f", layer))
                stt(s, decayed_sum[:, 0:n], f, 0.0, flat(sq)[:, 0:n], ALU.min, ALU.subtract)
                dve.wait_ge(*s.now())
                if kind == "hgrn":
                    tt(s, flat(ct), decayed_sum, f, ALU.subtract, "log k", layer)
                    dve.wait_ge(*act_gla.at("log bounds", layer))
                    for h in range(8):
                        ts(s, sq[:, h, :], decayed_sum[:, h * T:(h + 1) * T], lbs[:, 5, h:h + 1], ALU.add, lbs[:, 4, h:h + 1], ALU.subtract,
                           "f against bound", layer)
                    dve.wait_ge(*s.now())
                    for h in range(8):
                        ts(s, decayed_sum[:, h * T:(h + 1) * T], decayed_sum[:, h * T:(h + 1) * T], lbs[:, 5, h:h + 1], ALU.add, lbs[:, 4, h:h + 1], ALU.max)
                    dve.wait_ge(*act_proj.at("q", layer, 6))
                    ts(s, flat(q), flat(q), 128.0 ** -0.5, ALU.mult)
                    dve.wait_ge(*act_gla.at("log1p f2", layer))
                    dve.wait_ge(*s.now())
                    tt(s, decayed_sum, decayed_sum, flat(ct), ALU.add)
                else:
                    ts(s, decayed_sum[:, 0:n], decayed_sum[:, 0:n], 1.0 / 16, ALU.mult)
                dve.wait_ge(*s.now())
                for h in range(heads):
                    scan(s, pj[:, 8 + h, :], decayed_sum[:, h * T:(h + 1) * T], "qk", layer)
                dve.wait_ge(*s.now())
                dve.wait_ge(*act_gla.at("k", layer))

                def difference(lv):
                    g3 = flat(pj[:, 8:8 + heads, :]).rearrange("p (n c) -> p n c", c=2 << lv)
                    tt(s, level_diff(lv, heads), g3,
                       g3[:, :, (1 << lv) - 1:1 << lv].to_broadcast([P, n // (2 << lv), 2 << lv]), ALU.subtract,
                       "difference", layer, lv)

                def decayed(lv):
                    h, c = 1 << lv, 2 << lv
                    if lv >= 2:
                        dve.wait_ge(*(pe_gla.at("level", layer, lv - 2, heads // 2 - 1)))
                    dve.wait_ge(*act_gla.at("decay", layer, lv))
                    d = level_diff(lv, heads)
                    o = flat(at_level(lv)[:, 0:heads, :]).rearrange("p (n c) -> p n c", c=c)
                    k3 = flat(kk[:, 0:heads, :]).rearrange("p (n c) -> p n c", c=c)
                    q3 = flat(q).rearrange("p (n c) -> p n c", c=c)
                    tt(s, o[:, :, 0:h], k3[:, :, 0:h], d[:, :, 0:h], ALU.mult)
                    tt(s, o[:, :, h:c], q3[:, :, h:c], d[:, :, h:c], ALU.mult, "decayed", layer, lv)

                def masked(lv):
                    m = ident[:, :] if lv < 0 else level[:, lv, :]
                    m = m.bitcast(U32).rearrange("p (a b n) -> p a b n", a=1, b=1).to_broadcast([P, 2, 2, P])
                    a4 = at[:, :, :].rearrange("p h (a n) -> p h a n", a=3)
                    for g in range(heads // 2):
                        dve.wait_ge(*pe_gla.at("level", layer, lv, g))
                        v.copy_predicated(a4[:, 2 * g:2 * g + 2, 0:3:2, :], m,
                                          psum.bank("level", layer, lv, g)[:, :].rearrange("p (h a n) -> p h a n", h=2, a=2))\
                            .then_inc(*s.tick("masked", layer, lv))
                        psum.release(s, "level", layer, lv, g)

                difference(0)
                for lv in range(8):
                    if lv < 7:
                        difference(lv + 1)
                    if lv == 0:
                        dve.wait_ge(*pe_unit.at("unit", layer, len(units_in(kind)) - 1))
                    decayed(lv)
                    if lv == 0:
                        v.memset(flat(at), 0.0).then_inc(*s.tick("zero", layer))
                    dve.wait_ge(*s.now())
                    masked(lv - 1)
                for g in range(heads // 4):
                    dve.wait_ge(*pe_gla.at("cross", layer, g))
                    v.tensor_copy(at[:, 4 * g:4 * g + 4, HALF:T],
                                  psum.bank("cross", layer, g)[:, :].rearrange("p (h n) -> p h n", h=4))\
                        .then_inc(*s.tick("causal", layer))
                    psum.release(s, "cross", layer, g)
                head_norms(layer, s, act_gla, pe_gla, kind == "gla", PT_MISC * P + (R_HGRN if kind == "hgrn" else R_GLA),
                           kind == "gla")

            def four(layer, l):
                s = dve_four
                dve.wait_ge(*act_proj.at("dt", layer))
                ts(s, rows[0:4, 2, :], rows[0:4, 2, :], hssm[0:4, 2 + l:3 + l], ALU.add, None, None, "dt + bias", layer)
                dve.wait_ge(*act_four.at("log1p dt", layer))
                stt(s, rows[0:4, 1, :], rows[0:4, 2, :], 0.0, rows[0:4, 3, :], ALU.max, ALU.add)
                dve.wait_ge(*act_four.at("a", layer))
                dve.wait_ge(*s.now())
                ts(s, rows[0:4, 2, :], rows[0:4, 1, :], head[0:4, 6:7], ALU.mult, -1.0, ALU.mult)
                dve.wait_ge(*s.now())
                scan(s, rows[0:4, 0, :], rows[0:4, 2, :], "rows", layer)
                dve.wait_ge(*act_four.at("c rstd", layer, 0))
                stt(s, pj[:, 6, :], pj[:, 6, :], par(PT_MISC * P + R_QG0 + l), stat[:, 3, 0:T], ALU.mult, ALU.mult)
                stt(s, pj[0:64, 7, :], pj[0:64, 7, :], params[0:64, PT_MISC * P + R_QG1 + l:PT_MISC * P + R_QG1 + l + 1],
                    stat[0:64, 3, 0:T], ALU.mult, ALU.mult)
                dve.wait_ge(*act_four.at("c rstd", layer, 1))
                stt(s, pj[:, 8, :], pj[:, 8, :], par(PT_MISC * P + R_KVG + l), stat[:, 3, T:2 * T], ALU.mult, ALU.mult,
                    "cn", layer)

                def pair(r):
                    if r < 2:
                        return P, pj2(2 * r), two(sq, r), pj2(2 * r)
                    q = flat(yb_t[:, 2 * (r - 2):2 * (r - 2) + 2, :])[0:96, :]
                    return 96, q, two(xn, r - 2)[0:96, :], q

                for r in range(6):
                    n, q, o, _ = pair(r)
                    dve.wait_ge(*act_four.at("rstd", layer, "n", r))
                    g = PT_MISC * P + (R_MOBAG + 2 * l + r if r < 2 else R_MLAG + 2 * l + (r - 2) // 2)
                    stt(s, o, q, params[0:n, g:g + 1], stat[0:n, r % 4, :], ALU.mult, ALU.mult, "roped in", layer, r)
                dve.wait_ge(*pe_four.at("tok", layer))
                v.tensor_copy(cols[:, 0:4, 0:4], psum.bank("tok", layer)[:, 0:32].rearrange("p (a h) -> p a h", a=4)[:, :, 0:4])\
                    .then_inc(*s.tick())
                psum.release(s, "tok", layer)
                dve.wait_ge(*s.now())
                dve.wait_ge(*pe_four.at("xtok", layer))
                for t in range(2):
                    tt(s, vb[:, t, 3 * T:4 * T].rearrange("p (h n) -> p h n", h=4),
                       psum.bank("xtok", layer)[:, t * T:(t + 1) * T].rearrange("p (h n) -> p h n", h=4),
                       cols[:, 2 * t + 1, 0:4].rearrange("p (h n) -> p h n", n=1).to_broadcast([P, 4, 64]), ALU.mult)
                psum.release(s, "xtok", layer)
                for g in range(2):
                    dve.wait_ge(*pe_four.at("bcast", layer, g))
                    b = psum.bank("bcast", layer, g)
                    for j in range(2):
                        h = 2 * g + j
                        ts(s, at[:, h, 0:T], b[:, j * T:(j + 1) * T], cols[:, 0, h:h + 1], ALU.subtract, 0.0, ALU.min)
                        ts(s, at[:, h, T:TRI], b[:, j * T + HALF:(j + 1) * T], cols[:, 2, h:h + 1], ALU.subtract, 0.0, ALU.min,
                           "difference", layer, h)
                    psum.release(s, "bcast", layer, g)
                for h in range(4):
                    dve.wait_ge(*act_four.at("decay", layer, h))
                    dve.wait_ge(*pe_four.at("bc", layer, h // 2))
                    tt(s, at[:, h, :], at[:, h, :], incl[:, :], ALU.mult)
                    dve.wait_ge(*s.now())
                    tt(s, at2[:, 4 + h, :], psum.bank("bc", layer, h // 2)[:, 0:TRI], at[:, h, :], ALU.mult, "causal", layer, 3)
                    if h % 2:
                        psum.release(s, "bc", layer, h // 2)
                for r in range(6):
                    n, _, qn, o = pair(r)
                    cos, sin = ((trig[0:n, c:c + 1, :].to_broadcast([n, 2, T])) for c in ((0, 1) if r < 2 else (2, 3)))
                    dve.wait_ge(*pe_four.at("rot", layer, r))
                    half = oc4[0:n, r % 4, :].rearrange("p (a n) -> p a n", a=2)
                    q2 = qn.rearrange("p (a n) -> p a n", a=2)
                    dve.wait_ge(*s.now())
                    tt(s, half, psum.bank("rot", layer, r)[0:n, :].rearrange("p (a n) -> p a n", a=2), sin, ALU.mult)
                    psum.release(s, "rot", layer, r)
                    tt(s, q2, q2, cos, ALU.mult)
                    dve.wait_ge(*s.now())
                    tt(s, o, qn, oc4[0:n, r % 4, :], ALU.add, "roped", layer, r)
                dve.wait_ge(*s.now())
                for h in range(4):
                    dve.wait_ge(*pe_four.at("z", layer, h))
                    b = psum.bank("z", layer, h)
                    ts(s, at2[:, h, :], b[:, 0:TRI], 0.125, ALU.mult, None, None, "z", layer, h)
                    psum.release(s, "z", layer, h)
                for h in range(4):
                    dve.wait_ge(*act_four.at("log1p z", layer, h))
                    stt(s, sb_t[:, h, :], at2[:, h, :], 0.0, sb_t[:, h, :], ALU.min, ALU.subtract)
                    dve.wait_ge(*s.now())
                    tt(s, sb_l1[:, h, :], sb_t[:, h, :], at2[:, h, :], ALU.subtract)
                    dve.wait_ge(*s.now())
                    tt(s, sb_l1[:, h, :], sb_l1[:, h, :], strict[:, :], ALU.mult, "log1mb", layer, h)
                for n in range(8 + 1):
                    if n < 8:
                        p = dec[:, n % 2, :]
                        dve.wait_ge(*pe_four.at("score", layer, n))
                        if n >= 2:
                            dve.wait_ge(*pe_four.at("probs", layer, n - 2))
                        dve.wait_ge(*s.now())
                        stt(s, p, psum.bank("score", layer, n)[:, 0:TRI], 0.125 if n < 4 else 96.0 ** -0.5, amask[:, :],
                            ALU.mult, ALU.add)
                        psum.release(s, "score", layer, n)
                        dve.wait_ge(*s.now())
                        v.tensor_reduce(small[:, n, 0:1], p[:, 0:HALF], AX.X, ALU.max, negate=True).then_inc(*s.tick())
                        v.tensor_reduce(small[:, n, 1:2], p[:, HALF:TRI], AX.X, ALU.max, negate=True)\
                            .then_inc(*s.tick("max", layer, n))
                    if n:
                        n -= 1
                        p = dec[:, n % 2, :]
                        dve.wait_ge(*act_four.at("exp", layer, n))
                        v.reciprocal(small[:, n, 2:4], small[:, n, 2:4]).then_inc(*s.tick())
                        dve.wait_ge(*s.now())
                        ts(s, p[:, 0:HALF], p[:, 0:HALF], small[:, n, 2:3], ALU.mult)
                        ts(s, p[:, HALF:TRI], p[:, HALF:TRI], small[:, n, 3:4], ALU.mult, None, None, "probs", layer, n)
                for h in range(4):
                    dve.wait_ge(*pe_four.at("tail", layer, h))
                    tt(s, sb_t[:, h, :], sb_t[:, h, :], psum.bank("tail", layer, h)[:, 0:TRI], ALU.add, "log a", layer, h)
                    psum.release(s, "tail", layer, h)
                for h in range(4):
                    dve.wait_ge(*act_four.at("a", layer, h))
                    tt(s, at2[:, h, :], sb_t[:, h, :], strict[:, :], ALU.mult, "causal", layer, 2)
                dve.wait_ge(*pe_four.at("o", layer, 1))
                split(HI)
                dve.wait_ge(*pe_four.at("o", layer, 3))
                b = psum.bank("o", layer, 3)
                dve.wait_ge(*act_proj.at("z", layer))
                for j in range(2):
                    stt(s, oc4[:, 3, j * T:(j + 1) * T], pj[:, 18 + j, :], par(PT_MISC * P + R_SSMD + 2 * l + j),
                        b[:, j * T:(j + 1) * T], ALU.mult, ALU.add)
                psum.release(s, "o", layer, 3)
                dve.wait_ge(*s.now())
                tt(s, oc4[:, 3, :], oc4[:, 3, :], pj2(16), ALU.mult, "gated", layer)
                dve.wait_ge(*s.now())
                for m in (0, 1, 3, 2):
                    dve.wait_ge(*act_four.at("rstd", layer, m))
                    for j in range(2):
                        g = PT_MISC * P + (R_HEADG + 6 * l + 2 * m if m < 3 else R_SSMG + 2 * l) + j
                        r = stat[:, m, j * T:(j + 1) * T] if m < 3 else stat[:, 3, 0:T]
                        stt(s, y[:, 2 * m + j, :], oc4[:, m, j * T:(j + 1) * T], par(g), r, ALU.mult, ALU.mult)
                dve.wait_ge(*s.now())
                input_halves(s, y, "mixed", layer)

            setup()
            for g in range(4):
                dve.wait_ge(*act_setup.at("x", g))
            input_halves(dve_norm, x, "x", -1)
            split(HI)
            norm = 0
            for layer, (kind, l) in enumerate(CHAIN[:layers]):
                if kind == "four":
                    rms_norm(norm, PT_MISC * P + R_RMSMIX + 8 * l)
                    norm += 1
                    project(layer, kind, l)
                    four(layer, l)
                    residual(norm, ("out", layer), None)
                    rms_norm(norm, PT_MISC * P + R_RMSFFN + 8 * l)
                    norm += 1
                    ffn(layer, l)
                    split()
                    residual(norm, ("ffn", layer), None)
                else:
                    project(layer, kind, l)
                    gdn(layer, l) if kind == "gdn" else gla(layer, kind, l)
                    residual(norm, ("out", layer), DN_ALPHA)
                    layer_norm(norm, PT_LN * P + R_MIXG + 8 * layer, PT_LN * P + R_MIXB + 8 * layer)
                    norm += 1
                    ffn(layer, l)
                    split()
                    residual(norm, ("ffn", layer), DN_ALPHA)
                    layer_norm(norm, PT_LN * P + R_FFNG + 8 * layer, PT_LN * P + R_FFNB + 8 * layer,
                               is_input=layer < min(layers, DEPTH) - 1)
                    norm += 1


_INS = ["x", "gdn_w_in", "gdn_conv_w", "gdn_a_log", "gdn_dt_bias", "gdn_norm_w", "gdn_w_out", "hgrn_w_in",
        "hgrn_lb_logits", "hgrn_norm_w", "hgrn_w_out", "gla_w_in", "gla_w_gk2", "gla_b_gk", "gla_norm_w", "gla_w_out",
        "mix_ln_g", "mix_ln_b", "ffn_w_in", "ffn_w_down", "ffn_ln_g", "ffn_ln_b", "positions_2", "mix_norm_g_2", "w_in_2",
        "moba_qk_g_2", "mla_q_norm_g_2", "mla_kv_norm_g_2", "mla_w_uq_2", "mla_w_ukv_2", "mla_qk_g_2", "ssm_conv_w_2",
        "ssm_conv_b_2", "ssm_dt_bias_2", "ssm_a_log_2", "ssm_d_2", "ssm_norm_g_2", "head_out_g_2", "w_out_2",
        "ffn_norm_g_2", "ffn_w_in_2", "ffn_conv_w_2", "ffn_conv_b_2", "ffn_w_out_2"]


def rope_freqs():
    def inverse(dim):
        e = np.arange(0, dim, 2, dtype=np.float32) / np.float32(dim)
        return (np.float32(1.0) / (np.float32(10000.0) ** e)).astype(np.float32)

    f = np.zeros((P, 2), np.float32)
    f[:, 0] = np.tile(inverse(64), 4)
    f[64:96, 1] = np.tile(inverse(32), 2)
    return f


def write(nc, arrays, book, layers=len(CHAIN)):
    A = {n: nc.dram_tensor(f"in_{n}_dram", a.shape, mybir.dt.from_np(a.dtype), kind="ExternalInput").ap()
         for n, a in arrays.items()}
    out = nc.dram_tensor("out_0_dram", (1, T, D), F32, kind="ExternalOutput").ap()
    build(nc, A, out, book, layers)


def kernel(**inputs):
    import concourse.bacc as bacc
    from concourse.bass_utils import run_bass_kernel_spmd

    arrays = {n: np.ascontiguousarray(inputs[n]) for n in _INS}
    arrays["rope_freqs"] = rope_freqs()
    book = Book()
    write(bacc.Bacc("TRN2", target_bir_lowering=False, num_devices=1), arrays, book)
    nc = bacc.Bacc("TRN2", target_bir_lowering=False, num_devices=1)
    write(nc, arrays, book)
    r = run_bass_kernel_spmd(nc, [{f"in_{n}_dram": a for n, a in arrays.items()}], core_ids=[0])
    return r.results[0]["out_0_dram"]
```

```python
from contextlib import ExitStack

import numpy as np

import concourse.bass as bass
from concourse import mybir

F32 = mybir.dt.float32
F32R = mybir.dt.float32r
I32 = mybir.dt.int32
U32 = mybir.dt.uint32
ACT = mybir.ActivationFunctionType
ALU = mybir.AluOpType
AX = mybir.AxisListType

P = 128
T = 256
D = 1024
KT = D // P
DEPTH = 4
DN_ALPHA = (2 * DEPTH) ** 0.25
F_TILES = 2816 // P
F_STEPS = F_TILES // 2
F_PAIRS = (F_STEPS - 5) // 2
RING = 6
HI = 3
DVE_SHARE = 2
SLOT = 2048
HALF = 128
ALL = slice(0, T)
HALF2 = HALF // 2
TRI = 3 * HALF

TWO_PI = [6.28125, 0.0019350051879882812]
TWO_PI.append(float(2 * np.pi - sum(TWO_PI)))
CHAIN = [("gdn", 0), ("hgrn", 0), ("gla", 0), ("gdn", 1), ("four", 0), ("four", 1)]


FILL = {"normed": 8, "centred": 3, "residual": 8, "mixed": 9, "gdn": 5, "c2": 7,
        "kbeta": 5, "masked": 4, "level": 6, "softmax": 2}


class Book:

    def __init__(self):
        self.marks = {}
        self.strides = {}
        self.written = None

    def restart(self):
        self.loop = None
        self.written = self.written is not None


class Signal:

    def __init__(self, book, sem, name):
        self.book, self.sem, self.name, self.n = book, sem, name, 0
        self.base = None

    def _value(self):
        loop = self.book.loop
        if loop is None:
            return self.n
        if self.base is None or self.base[0] is not loop:
            self.base = (loop, self.n)
            loop.signals.append((self, self.n))
        stride = self.book.strides.get((loop.name, self.name), 0)
        return self.n + loop.i * stride if stride else self.n

    def tick(self, *key):
        self._value()
        self.n += 1
        loop = self.book.loop
        if key:
            self.book.marks[(self.name,) + key] = (self.n, loop and loop.name)
        return self.sem, 1

    def name_also(self, *key):
        self.book.marks[(self.name,) + key] = (self.n, None)

    def at(self, *key, ago=0):
        n, name = self.book.marks[(self.name,) + key] if self.book.written else \
            self.book.marks.get((self.name,) + key, (1, None))
        if name is not None:
            stride = self.book.strides.get((name, self.name), 0)
            loop = self.book.loop
            if loop is not None and loop.name == name:
                return self.sem, (n - ago * stride) + loop.i * stride
            n += stride * (self.book.strides.get((name, "count"), 1) - 1)
        return self.sem, n

    def now(self):
        return self.sem, self._value()


class Loop:

    def __init__(self, book, eng, name, count):
        self.book, self.eng, self.name, self.count = book, eng, name, count

    def __enter__(self):
        self.signals = []
        self.fori = self.eng.Fori(0, self.count)
        self.i = self.fori.__enter__()
        self.book.loop = self
        return self.i

    def __exit__(self, *e):
        self.fori.__exit__(*e)
        self.book.loop = None
        self.book.strides[(self.name, "count")] = self.count
        for sig, n in self.signals:
            stride = sig.n - n
            self.book.strides[(self.name, sig.name)] = stride
            sig.n = n + self.count * stride


class Psum:

    def __init__(self, book, banks, sem):
        self.book, self.banks, self.sem = book, banks, sem
        self.next, self.uses, self.where = 0, [0] * 8, {}

    def claim(self, pe, *key, bank=None):
        b = self.next % 8 if bank is None else bank
        self.next += bank is None
        if self.uses[b]:
            pe.wait_ge(*self.book.marks.get(("free", b, self.uses[b]), (self.sem, 1)))
        self.uses[b] += 1
        self.where[key] = b, self.uses[b]
        return self.banks[b]

    def bank(self, *key):
        return self.banks[self.where[key][0]]

    def release(self, signal, *key):
        self.book.marks[("free",) + self.where[key]] = signal.sem, signal.n


N_QK, N_CONV = 8, 12
def units_in(kind):
    if kind == "gdn":
        u = [(4096, 16, "pair8", "ba", 0)]
        u += [(256 * i, 256, "cm", "conv", 2 * i) for i in range(12)]
        u += [(3072 + 256 * i, 256, "cm", "gate", 2 * i) for i in range(4)]
    elif kind == "hgrn":
        u = [(1024 + 256 * i, 256, "cm", "f", 2 * i) for i in range(4)]
        u += [(256 * i, 256, "cm", "qsilu", 2 * i) for i in range(4)]
        u += [(2048 + 256 * i, 256, "tok", "v", i) for i in range(4)]
        u += [(3072 + 256 * i, 256, "cm", "gate", 2 * i) for i in range(4)]
    elif kind == "gla":
        u = [(3072, 16, "row16", "gk", 0)]
        u += [(256 * i, 256, "cm", "qscaled", 2 * i) for i in range(2)]
        u += [(512 + 256 * i, 256, "cm", "k", 2 * i) for i in range(2)]
        u += [(1024 + 256 * i, 256, "tok", "v", i) for i in range(4)]
        u += [(2048 + 256 * i, 256, "cm", "gate", 2 * i) for i in range(4)]
    else:
        mla, sb, ssm = 768, 1120, 1888
        u = [(ssm + 768, 4, "row4", "dt", 0)]
        u += [(ssm + 256 + 256 * i, 256, "cm", "xbc", 2 * i) for i in range(2)]
        u += [(0, 256, "cm", "plain", 0), (256, 256, "cm", "plain", 2), (512, 256, "tok", "vmoba", 0)]
        u += [(mla, 192, "cq", "cq", 0), (mla + 192, 160, "ckv", "ckv", 0)]
        u += [(sb, 256, "cm", "plain", 10), (sb + 256, 256, "cm", "plain", 12), (sb + 512, 256, "tok", "vsb", 0)]
        u += [(ssm, 256, "cm", "z", 0)]
    return u




PT_LN, PT_CONV, PT_MISC, PT_SSM, PT_FFN = 0, 1, 3, 4, 5
PT_TILES = 9
R_MIXG, R_MIXB, R_FFNG, R_FFNB = 0, 32, 64, 96
R_RMSMIX, R_RMSFFN, R_LB, R_GDN, R_HGRN, R_GLA, R_BGK = 0, 16, 32, 64, 66, 67, 69
R_CONVB, R_SSMG, R_KVG, R_QG0, R_QG1, R_MOBAG, R_MLAG, R_HEADG, R_SSMD = 73, 81, 85, 87, 89, 91, 95, 99, 111
FFN_BIAS = (PT_FFN + 3) * P


def build(nc, A, out, book, layers=len(CHAIN)):
    book.restart()
    with ExitStack() as ctx:
        places = {}

        def sb(name, shape, dt=F32):
            t = ctx.enter_context(nc.sbuf_tensor(name, shape, dt))
            places[name] = nc.sbuf_base - 4 * int(np.prod(shape[1:]))
            return t

        def over(name, shape, at_name, floats=0):
            return nc.alloc_sbuf_tensor_at(name, shape, F32R, offset=places[at_name] + 4 * floats)

        def sem(name):
            return ctx.enter_context(nc.semaphore(name))

        def signal(name):
            return Signal(book, sem(name), name)

        ring = sb("ring", [P, RING, SLOT])
        x = sb("x", [P, KT, T])
        xn = sb("xn", [P, KT, T])
        sq = sb("sq", [P, KT, T])
        pj = sb("pj", [P, 32, T])
        mats = sb("mats", [P, 16, TRI])
        inv = sb("inv", [P, 32, HALF])
        ct = sb("ct", [P, 16, HALF])
        yb = sb("yb", [P, 16, HALF])
        vb = sb("vb", [P, 2, D])
        dec = sb("dec", [P, 2, TRI])
        stat = sb("stat", [P, 4, 2 * T])
        rows = sb("rows", [16, 6, T])
        cols = sb("cols", [P, 4, 16])
        small = sb("small", [P, 8, 4])
        params = sb("params", [P, PT_TILES * P])
        head = sb("head", [8, 8])
        lbs = sb("lbs", [P, 8, KT])
        hssm = sb("hssm", [4, 4])
        trig = sb("trig", [P, 4, T])
        freqs = sb("freqs", [P, 2])
        ident = sb("ident", [P, P])
        ones = sb("ones", [P, P])
        ones_d = sb("ones_d", [P, P])
        blk64 = sb("blk64", [P, P])
        rot64 = sb("rot64", [P, P])
        rot96 = sb("rot96", [P, P])
        later = sb("later", [P, P])
        level = sb("level", [P, 7, P])
        incl = sb("incl", [P, TRI])
        strict = sb("strict", [P, TRI])
        amask = sb("amask", [P, TRI])
        const = sb("const", [P, 8])
        banks = [ctx.enter_context(nc.psum_tensor(f"bank{i}", [P, 512], F32)) for i in range(8)]
        C_LN_EPS, C_RMS_EPS, C_QSCALE, C_HALFPI, C_ONE = 0, 1, 2, 3, 4

        def flat(ap):
            return ap[:, :, :].rearrange("p a b -> p (a b)") if len(ap.shape) == 3 else ap

        lt = mats[:, 0:8, :]
        at = mats[:, 8:16, :]
        y = xn
        w_hi = over("w_hi", [P, HI, SLOT], "mats")
        w_lo = over("w_lo", [P, RING, SLOT], "ring")
        xh = over("xh", [P, KT, T], "inv")
        xl = over("xl", [P, KT, T], "xn")
        hid_hi = over("hid_hi", [P, 2, 2, T], "pj")
        hid_lo = over("hid_lo", [P, 2, 2, T], "yb")
        decayed_sum = flat(inv[:, 16:32, :])
        yt = xn[:, :, :].rearrange("p (t c) n -> p t (c n)", t=2)
        ct_t, yb_t = (a[:, :, :].rearrange("p (h c) n -> p h (c n)", c=2) for a in (ct, yb))
        fconv = ct_t[:, :, :].rearrange("p (s a) n -> p s a n", s=2)
        hid = yb_t[:, 0:4, :].rearrange("p (s a) n -> p s a n", s=2)
        gact = yb_t[:, 4:8, :].rearrange("p (s a) n -> p s a n", s=2)
        oc = pj[:, 16:24, :].rearrange("p (m a) n -> p m (a n)", a=2)
        oc4 = pj[:, 24:32, :].rearrange("p (m a) n -> p m (a n)", a=2)
        mlaw = flat(inv)[:, 2048:3328]
        sb_l1 = lt[:, 0:4, :]
        sb_t = flat(sq)[:, 0:4 * TRI].rearrange("p (h n) -> p h n", h=4)
        at2 = flat(inv)[:, 0:8 * TRI].rearrange("p (a b) -> p a b", a=8)
        wgk2 = flat(dec)[0:16, 0:512]
        stage = flat(pj[:, 24:32, :])
        pos_i = stat[:, 0, 0:T].bitcast(I32)

        def two(ap, g):
            return flat(ap[:, 2 * g:2 * g + 2, :])

        def pj2(i):
            return flat(pj[:, i:i + 2, :])

        def four_tiles(ap, g):
            return flat(ap[:, 4 * g:4 * g + 4, :])

        def gsq(g):
            return flat(ct if g < 4 else yb)[:, 2 * T * (g % 4):2 * T * (g % 4 + 1)]

        def nsq(r):
            return two(sq, 2 + r) if r < 2 else four_tiles(ct, r - 2)

        def u(t, h):
            return ct[:, 8 * t + h, :]

        cx = flat(yb)[:, 0:16 * HALF2].rearrange("p (j n) -> p j n", j=16)

        def prob(n):
            return lt[:, 4 + n % 4, :]

        def first_halves(ap, lv):
            dims = " ".join("abc"[:len(ap.shape) - 2])
            r = ap.rearrange(f"p {dims} (n two c) -> p {dims} n two c", two=2, c=1 << lv)
            return r[:, :, 0, :] if len(ap.shape) == 2 else r[:, :, :, 0, :]

        def at_level(lv):
            return inv[:, 16 * (lv % 2):16 * (lv % 2) + 16, :].rearrange("p (h c) n -> p h (c n)", c=2)

        def level_diff(lv, heads):
            return flat(ct if lv % 2 == 0 else sq)[:, 0:heads * T].rearrange("p (n c) -> p n c", c=2 << lv)

        def par(col):
            return params[:, col:col + 1]

        w_loaded = [sem(f"w_loaded{i}") for i in range(RING)]
        x_loaded = sem("x_loaded")
        in_loaded = sem("in_loaded")
        param_loaded = sem("param_loaded")
        mla_loaded = sem("mla_loaded")
        out_stored = sem("out_stored")
        gk_loaded = sem("gk_loaded")
        pool_setup, dve_setup, act_setup, pe_setup = map(signal, ("pool_setup", "dve_setup", "act_setup", "pe_setup"))
        pe_unit = signal("pe_unit")
        dve_hi, dve_lo, pool_lo = map(signal, ("dve_hi", "dve_lo", "pool_lo"))
        act_proj, dve_conv = map(signal, ("act_proj", "dve_conv"))
        pe_gdn, act_gdn, dve_gdn, pool_gdn = map(signal, ("pe_gdn", "act_gdn", "dve_gdn", "pool_gdn"))
        pe_gla, act_gla, dve_gla, pool_gla = map(signal, ("pe_gla", "act_gla", "dve_gla", "pool_gla"))
        pe_four, act_four, dve_four, pool_four = map(signal, ("pe_four", "act_four", "dve_four", "pool_four"))
        pe_norm, act_norm, dve_norm = map(signal, ("pe_norm", "act_norm", "dve_norm"))
        act_ffn, dve_ffn = map(signal, ("act_ffn", "dve_ffn"))
        pe_filler = signal("pe_filler")
        pe_out, act_out = map(signal, ("pe_out", "act_out"))
        psum = Psum(book, banks, out_stored)

        sizes = []
        for kind, _ in CHAIN[:layers]:
            sizes += [KT * w for _, w, *_ in units_in(kind)] + [SLOT] * (4 + 3 * F_STEPS)

        def of_unit(sig, u, i=None):
            return sig.sem, u + 1 if i is None else i * RING + (u + 1)

        def loaded(u, i=None):
            n = u // RING + 1
            return w_loaded[u % RING], 16 * n if i is None else (i + n) * 16

        block = ctx.enter_context(nc.Block())

        PARAM_LOADS = []

        def param_rows(tile, row, src, width=P, col=0):
            n = src.shape[0]
            PARAM_LOADS.append((stage[row:row + n, tile * P + col:tile * P + col + width], src))

        def tiles_of(ap):
            return ap.rearrange("a (t c) -> (a t) c", c=P)

        for row, name in ((R_MIXG, "mix_ln_g"), (R_MIXB, "mix_ln_b"), (R_FFNG, "ffn_ln_g"), (R_FFNB, "ffn_ln_b")):
            param_rows(PT_LN, row, tiles_of(A[name]))
        for l in range(2):
            param_rows(PT_CONV + l, 0, tiles_of(A["gdn_conv_w"][l]))
        for row, name in ((R_RMSMIX, "mix_norm_g_2"), (R_RMSFFN, "ffn_norm_g_2"), (R_LB, "hgrn_lb_logits"),
                          (R_GDN, "gdn_norm_w"), (R_HGRN, "hgrn_norm_w"), (R_GLA, "gla_norm_w"), (R_BGK, "gla_b_gk"),
                          (R_CONVB, "ssm_conv_b_2"), (R_SSMG, "ssm_norm_g_2"), (R_KVG, "mla_kv_norm_g_2")):
            param_rows(PT_MISC, row, tiles_of(A[name]))
        param_rows(PT_MISC, R_QG0, A["mla_q_norm_g_2"][:, 0:P])
        param_rows(PT_MISC, R_QG1, A["mla_q_norm_g_2"][:, P:P + 64], 64)
        for half in range(2):
            param_rows(PT_MISC, R_MOBAG, A["moba_qk_g_2"].rearrange("l a c -> (l a) c"), 64, 64 * half)
            d = A["ssm_d_2"].rearrange("l (a b) -> (l a) b", b=2)[:, half:half + 1].rearrange("r (b c) -> r b c", b=1)
            PARAM_LOADS.append((stage[R_SSMD:R_SSMD + 4, PT_MISC * P + 64 * half:PT_MISC * P + 64 * half + 64]
                                .rearrange("r (b c) -> r b c", c=1), d.to_broadcast([4, 64, 1])))
        param_rows(PT_MISC, R_MLAG, A["mla_qk_g_2"].rearrange("l a c -> (l a) c"), 96)
        param_rows(PT_MISC, R_HEADG, A["head_out_g_2"].rearrange("l m (a b) c -> (l m a) (b c)", b=2))
        for l in range(2):
            param_rows(PT_SSM, 16 * l, tiles_of(A["ssm_conv_w_2"][l]))
        taps = A["ffn_conv_w_2"].rearrange("l j (t c) -> (l j t) c", c=P)
        for t in range(3):
            n = min(P, taps.shape[0] - t * P)
            param_rows(PT_FFN + t, 0, taps[t * P:t * P + n, :])
        param_rows(PT_FFN + 3, 0, tiles_of(A["ffn_conv_b_2"]))
        IN_LOADS = [(pos_i, A["positions_2"].to_broadcast([P, T])), (freqs[:, :], A["rope_freqs"])]
        for dst, col, name in ((head, 0, "gdn_a_log"), (head, 2, "gdn_dt_bias"), (hssm, 0, "ssm_a_log_2"), (hssm, 2, "ssm_dt_bias_2")):
            n = A[name].shape[1]
            for l in range(2):
                IN_LOADS.append((dst[0:n, col + l:col + l + 1], A[name][l:l + 1, :].rearrange("l h -> h l")))
        N_IN = len(IN_LOADS)

        @block.tensor
        def _(pe):
            unit = fillers = 0

            def products(u, outs, tiles, width, moving, first=True, last=True, i=None, high_ready=None, low_ready=None):
                n = tiles * width
                w_high = w_hi[:, u % HI, 0:n].rearrange("p (k n) -> p k n", k=tiles)
                w_low = w_lo[:, u % RING, 0:n].rearrange("p (k n) -> p k n", k=tiles)
                x_high, x_low = moving
                pe.wait_ge(*of_unit(dve_hi, u, i))
                orders = [("high", w_high, x_high), ("w low", w_low, x_high), ("x low", w_high, x_low)]
                if not high_ready:
                    orders[1:] = orders[:0:-1]
                for step, (what, w, xin) in enumerate(orders):
                    if what == "w low":
                        pe.wait_ge(*of_unit(dve_lo, u, i))
                        pe.wait_ge(*of_unit(pool_lo, u, i))
                    ready = high_ready if what == "high" else low_ready if what == "x low" else None
                    for j, (cols, c0, cw, tokens) in enumerate(outs):
                        for k in range(tiles):
                            if ready and j == 0:
                                pe.wait_ge(*ready(k))
                            wk, xk = w[:, k, c0:c0 + cw], xin[:, k, tokens]
                            m = nc.tensor.matmul(cols, *((wk, xk) if tokens == ALL else (xk, wk)),
                                                 start=(first and step == 0 and k == 0 and (j % 2 == 0)),
                                                 stop=(last and step == 2 and k == tiles - 1), skip_group_check=True)
                return m

            def stay_awake(n, bank=None):
                nonlocal fillers
                fillers += 1
                b = psum.claim(pe, "filler", fillers, bank=psum.next % 8 if bank is None else bank)
                for _ in range(n):
                    m = nc.tensor.matmul(b[:, 0:T], ones[:, :], incl[:, 0:T], start=True, stop=True)
                m.then_inc(*pe_filler.tick())
                psum.release(pe_filler, "filler", fillers)

            def project(layer, kind, parts_ready):
                nonlocal unit
                for n, (c0, w, how, name, idx) in enumerate(units_in(kind)):
                    b = psum.claim(pe, "proj", layer, n)
                    left, right = b[:, 0:T], b[:, T:2 * T]
                    outs = {"cm": [(left, 0, P, ALL), (right, P, P, ALL)],
                            "pair8": [(b[0:8, 0:T], 0, 8, ALL), (b[0:8, T:2 * T], 8, 8, ALL)],
                            "row16": [(b[0:16, 0:T], 0, 16, ALL)],
                            "row4": [(b[0:4, 0:T], 0, 4, ALL)],
                            "cq": [(left, 0, P, ALL), (b[0:64, T:2 * T], P, 64, ALL)],
                            "ckv": [(left, 0, P, ALL), (b[0:96, T:2 * T], 64, 96, ALL)],
                            "tok": [(left, 0, T, slice(0, HALF)), (right, 0, T, slice(HALF, T))]}[how]
                    products(unit, outs, KT, w, (xh, xl), **(parts_ready if n == 0 else {}))\
                        .then_inc(*pe_unit.tick("unit", layer, n))
                    unit += 1
                    if layer == 0 and n == 1:
                        params_to_columns()
                    if kind == "gla" and n == 2:
                        gla_gates(layer)
                    if kind == "gdn" and n >= N_CONV + 1:
                        qk_sums(layer, ((0, 1, 2), (3, 4, 5), (6, 7), ())[n - N_CONV - 1])

            def out_project(layer):
                nonlocal unit
                for n in range(4):
                    b = psum.claim(pe, "out", layer, n)
                    products(unit, [(b[:, 0:T], 0, P, ALL), (b[:, T:2 * T], P, P, ALL)], KT, T, (xh, xl),
                             **(mixed(layer) if n == 0 else {}))\
                        .then_inc(*pe_unit.tick("out", layer, n))
                    unit += 1

            def mixed(layer):
                act_sig, dve_sig = {"gdn": (act_gdn, dve_gdn), "four": (act_four, dve_four)}\
                    .get(CHAIN[layer][0], (act_gla, dve_gla))
                return {"high_ready": lambda k: act_sig.at("mixed hi", layer, k // 2),
                        "low_ready": lambda k: dve_sig.at("mixed lo", layer, k // 2)}

            def layer_norm(n):
                b = psum.claim(pe, "mean", n)
                for k in range(KT):
                    if k % 2 == 0:
                        pe.wait_ge(*dve_norm.at("residual", n, k // 2))
                    m = nc.tensor.matmul(b[:, 0:T], ones_d[:, :], x[:, k, :], start=(k == 0), stop=(k == KT - 1))
                m.then_inc(*pe_norm.tick("mean", n))
                stay_awake(FILL["centred"])
                rms_sum(n)

            def rms_sum(n):
                b = psum.claim(pe, "square", n)
                for k in range(KT):
                    if k % 2 == 0:
                        pe.wait_ge(*act_norm.at("square", n, k // 2))
                    m = nc.tensor.matmul(b[:, 0:T], ones_d[:, :], sq[:, k, :], start=(k == 0), stop=(k == KT - 1))
                m.then_inc(*pe_norm.tick("square", n))

            def ffn(layer, parts_ready):
                nonlocal unit
                for b in range(8):
                    psum.claim(pe, "ffn", layer, b, bank=b)

                def gate_up(par_, key, i, freed, parts_ready={}):
                    nonlocal unit
                    for part in range(2):
                        b = banks[4 + 2 * par_ + part]
                        if freed is not None:
                            pe.wait_ge(*freed[part])
                        products(unit, [(b[:, 0:T], 0, P, ALL), (b[:, T:2 * T], P, P, ALL)], KT, T, (xh, xl), i=i,
                                 **(parts_ready if part == 0 else {}))\
                            .then_inc(*pe_unit.tick("gate" if part == 0 else "up", layer, key))
                        unit += 1

                def down(par_, key, i, step, ago=0, first=False, last=False):
                    nonlocal unit
                    outs = [(banks[n // 2][:, (n % 2) * T:(n % 2 + 1) * T], n * P, P, ALL) for n in range(KT)]
                    if last:
                        pe.wait_ge(*dve_ffn.at("hidden lo", layer, step))
                        for b in range(4):
                            m = products(unit, outs[2 * b:2 * b + 2], 2, D, (hid_hi[:, par_], hid_lo[:, par_]), False, True)
                            m.then_inc(*(pe_norm.tick("down", layer, b) if b < 3 else pe_unit.tick("down", layer, key)))
                        unit += 1
                        return
                    pe.wait_ge(*dve_ffn.at("hidden lo", layer, step, ago=ago))
                    products(unit, outs, 2, D, (hid_hi[:, par_], hid_lo[:, par_]), first, last, i)\
                        .then_inc(*pe_unit.tick("down", layer, key))
                    unit += 1

                freed_by = (lambda k, ago=0: (act_ffn.at("gated", layer, k, ago=ago),
                                              dve_ffn.at("hidden", layer, k, ago=ago))) \
                    if layer < DEPTH else (lambda k, ago=0: (dve_ffn.at("conv gate", layer, k, ago=ago),
                                                             dve_ffn.at("conv up", layer, k, ago=ago)))
                gate_up(0, 0, None, None, parts_ready)
                gate_up(1, 1, None, None)
                down(0, 0, None, 0, first=True)
                gate_up(0, 2, None, freed_by(0))
                down(1, 1, None, 1)
                u0 = unit
                with Loop(book, pe, f"ffn{layer}", F_PAIRS) as i:
                    gate_up(1, "a", i, freed_by("a", 1))
                    down(0, "of b", i, "b", ago=1)
                    gate_up(0, "b", i, freed_by("b", 1))
                    down(1, "of a", i, "a")
                unit = u0 + RING * F_PAIRS
                gate_up(1, 9, None, freed_by("a"))
                down(0, 8, None, "b")
                gate_up(0, 10, None, freed_by("b"))
                down(1, 9, None, 9)
                down(0, "last", None, 10, last=True)

            def params_to_columns():
                pe.wait_ge(param_loaded, 16 * len(PARAM_LOADS))
                for g in range(3):
                    tiles = range(4 * g, min(4 * g + 4, PT_TILES))
                    b = psum.claim(pe, "params", g)
                    for j, t in enumerate(tiles):
                        m = nc.tensor.transpose(b[:, j * P:(j + 1) * P], stage[:, t * P:(t + 1) * P], ident[:, :])
                    m.then_inc(*pe_setup.tick("params", g))

            def x_to_channels():
                pe.wait_ge(*pool_setup.at("identity"))
                pe.wait_ge(x_loaded, 16)
                xtok = xn[:, :, :].rearrange("p (t c) n -> p t (c n)", t=2)
                for g in range(4):
                    b = psum.claim(pe, "x", g)
                    for j in range(4):
                        k, t = 2 * g + j // 2, j % 2
                        m = nc.tensor.transpose(b[:, j * P:(j + 1) * P], xtok[:, t, k * P:(k + 1) * P], ident[:, :])
                    m.then_inc(*pe_setup.tick("x", g))

            def causal(b, k, q):
                nc.tensor.matmul(b[:, 0:T], k[:, 0:HALF], q[:, :], start=True, stop=True)
                return nc.tensor.matmul(b[:, T:TRI], k[:, HALF:T], q[:, HALF:T], start=True, stop=True)

            def values(b_cols, v0, v1, a):
                nc.tensor.matmul(b_cols, v0, a[:, 0:T], start=True, stop=False, skip_group_check=True)
                return nc.tensor.matmul(b_cols[:, HALF:T], v1, a[:, T:TRI], start=False, stop=True,
                                        skip_group_check=True)

            def qk_sums(layer, gs):
                for g in gs:
                    b = psum.claim(pe, "qk2", layer, g)
                    pe.wait_ge(*act_gdn.at("square", layer, g))
                    nc.tensor.matmul(b[:, :], ones[:, :], gsq(g), start=True, stop=True).then_inc(*pe_gdn.tick("qk2", layer, g))

            def gdn(layer):
                b = psum.claim(pe, "tok", layer)
                pe.wait_ge(*dve_gdn.at("rows", layer))
                for j in range(4):
                    row = rows[0:8, j % 2, (j // 2) * HALF:(j // 2 + 1) * HALF]
                    m = nc.tensor.transpose(b[:, j * 8:(j + 1) * 8], row, ident[0:8, 0:8])
                m.then_inc(*pe_gdn.tick("tok", layer))
                for g in range(4):
                    b = psum.claim(pe, "v", layer, g)
                    pe.wait_ge(*act_proj.at("conv", layer, 11))
                    t, h0 = g // 2, 4 * (g % 2)
                    for j in range(4):
                        m = nc.tensor.transpose(b[:, j * P:(j + 1) * P],
                                                pj[:, 16 + h0 + j, t * HALF:(t + 1) * HALF], ident[:, :])
                    m.then_inc(*pe_gdn.tick("v", layer, g))
                for h in range(8):
                    b = psum.claim(pe, "bcast", layer, h)
                    for j in range(2):
                        m = nc.tensor.matmul(b[:, j * T:(j + 1) * T], ident[0:8, h:h + 1].to_broadcast([8, P]), rows[0:8, j, :], start=True, stop=True)
                    m.then_inc(*pe_gdn.tick("bcast", layer, h))
                    if h == 1:
                        stay_awake(FILL["kbeta"])
                    if h:
                        gdn_scores(layer, h - 1)
                gdn_scores(layer, 7)
                stay_awake(FILL["masked"])
                for g in range(4):
                    gdn_transpose(layer, 0, g)
                for lv in range(1, 7):
                    for g in range(4):
                        b = psum.claim(pe, "cx", layer, lv, g)
                        pe.wait_ge(*pool_gdn.at("masked", layer, lv, g))
                        pe.wait_ge(*(act_gdn.at("X", layer, g) if lv == 1 else dve_gdn.at("X", layer, lv - 1, g)))
                        for j in range(4 * g, 4 * g + 4):
                            m = nc.tensor.matmul(b[:, (j % 4) * HALF2:(j % 4 + 1) * HALF2].rearrange("p (n c) -> p n c", c=1 << lv),
                                                 ct[:, j, :], first_halves(inv[:, j, :], lv), start=True, stop=True)
                        m.then_inc(*pe_gdn.tick("cx", layer, lv, g))
                        if g:
                            gdn_correct(layer, lv, g - 1)
                        if g >= 2 and lv < 6:
                            gdn_transpose(layer, lv, g - 2)
                    gdn_correct(layer, lv, 3)
                    if lv < 6:
                        gdn_transpose(layer, lv, 2)
                        gdn_transpose(layer, lv, 3)
                for g in range(2):
                    b = psum.claim(pe, "u0", layer, g)
                    pe.wait_ge(*dve_gdn.at("XT", layer, 6, g))
                    for j in range(4 * g, 4 * g + 4):
                        m = nc.tensor.matmul(b[:, (j % 4) * P:(j % 4 + 1) * P], inv[:, 16 + j, :],
                                             vb[:, 0, j * P:(j + 1) * P], start=True, stop=True)
                    m.then_inc(*pe_gdn.tick("u0", layer, g))
                for g in range(2):
                    b = psum.claim(pe, "lu", layer, g)
                    pe.wait_ge(*act_gdn.at("u0", layer, g))
                    for j in range(4 * g, 4 * g + 4):
                        m = nc.tensor.matmul(b[:, (j % 4) * P:(j % 4 + 1) * P], lt[:, j, HALF:T], u(0, j),
                                             start=True, stop=True)
                    m.then_inc(*pe_gdn.tick("lu", layer, g))
                for g in range(2):
                    b = psum.claim(pe, "u1", layer, g)
                    pe.wait_ge(*dve_gdn.at("rhs", layer, g))
                    pe.wait_ge(*dve_gdn.at("XT", layer, 6, 2 + g))
                    for j in range(4 * g, 4 * g + 4):
                        m = nc.tensor.matmul(b[:, (j % 4) * P:(j % 4 + 1) * P], inv[:, 24 + j, :],
                                             vb[:, 1, j * P:(j + 1) * P], start=True, stop=True)
                    m.then_inc(*pe_gdn.tick("u1", layer, g))
                for g in range(4):
                    b = psum.claim(pe, "o", layer, g)
                    pe.wait_ge(*act_gdn.at("u1", layer, g // 2))
                    for j in (2 * g, 2 * g + 1):
                        m = values(b[:, (j % 2) * T:(j % 2 + 1) * T], u(0, j), u(1, j), at[:, j, :])
                    m.then_inc(*pe_gdn.tick("o", layer, g))
                    if g:
                        head_norm(layer, g - 1, act_gdn, pe_gdn, False)
                head_norm(layer, 3, act_gdn, pe_gdn, False)

            def gdn_scores(layer, h):
                pe.wait_ge(*dve_gdn.at("kbeta", layer, h))
                b = psum.claim(pe, "kk", layer, h)
                causal(b, pj[:, 8 + h, :], sq[:, h, :]).then_inc(*pe_gdn.tick("kk", layer, h))
                b = psum.claim(pe, "qk", layer, h)
                causal(b, pj[:, 8 + h, :], pj[:, h, :]).then_inc(*pe_gdn.tick("qk", layer, h))

            def gdn_transpose(layer, lv, g):
                b = psum.claim(pe, "transposed", layer, lv, g)
                pe.wait_ge(*dve_gdn.at("XT" if lv == 0 else "X", layer, lv, g))
                for j in range(4 * g, 4 * g + 4):
                    m = nc.tensor.transpose(b[:, (j % 4) * P:(j % 4 + 1) * P], inv[:, j + (16 if lv == 0 else 0), :], ident[:, :])
                m.then_inc(*pe_gdn.tick("transposed", layer, lv, g))

            def gdn_correct(layer, lv, g):
                b = psum.claim(pe, "z", layer, lv, g)
                pe.wait_ge(*act_gdn.at("cx", layer, lv, g))
                if lv > 1:
                    pe.wait_ge(*act_gdn.at("XT", layer, lv - 1, g))
                for j in range(4 * g, 4 * g + 4):
                    cols = slice((j % 4) * HALF2, (j % 4 + 1) * HALF2)
                    if lv < 6:
                        m = nc.tensor.matmul(b[:, cols], inv[:, 16 + j, :], cx[:, j, :], start=True, stop=True)
                    else:
                        m = nc.tensor.matmul(b[0:HALF2, cols], cx[:, j, :], inv[:, 16 + j, HALF2:HALF], start=True, stop=True)
                m.then_inc(*pe_gdn.tick("z", layer, lv, g))

            def head_norm(layer, g, act_sig, pe_sig, both):
                b = psum.claim(pe, "o2", layer, g)
                pe.wait_ge(*act_sig.at("o2", layer, g))
                if both:
                    nc.tensor.matmul(b[:, 0:T], ones[:, :], sq[:, 2 * g, :], start=True, stop=False)
                    m = nc.tensor.matmul(b[:, 0:T], ones[:, :], sq[:, 2 * g + 1, :], start=False, stop=True)
                else:
                    m = nc.tensor.matmul(b[:, :], ones[:, :], two(sq, g), start=True, stop=True)
                m.then_inc(*pe_sig.tick("o2", layer, g))

            def gla_gates(layer):
                pe.wait_ge(*act_proj.at("gk", layer))
                pe.wait_ge(gk_loaded, 16)
                for g in range(2):
                    b = psum.claim(pe, "gk", layer, g)
                    for j in range(2):
                        m = nc.tensor.matmul(b[:, j * T:(j + 1) * T], wgk2[:, (2 * g + j) * P:(2 * g + j + 1) * P],
                                             rows[0:16, 4, :], start=True, stop=True)
                    m.then_inc(*pe_gla.tick("gk", layer, g))

            def gla(layer, kind):
                heads = 8 if kind == "hgrn" else 4
                q = pj[:, 0:heads, :]
                k = yb_t[:, 0:8, :] if kind == "hgrn" else pj[:, 4:8, :]
                pe.wait_ge(*dve_gla.at("qk", layer))
                pe.wait_ge(*act_gla.at("k", layer))
                for lv in range(-1, 7):
                    if lv in (0, 1):
                        stay_awake(FILL["level"])
                    if lv >= 0:
                        pe.wait_ge(*dve_gla.at("decayed", layer, lv))
                    src = at_level(lv)
                    for g in range(heads // 2):
                        b = psum.claim(pe, "level", layer, lv, g)
                        for j in range(4):
                            h, t = 2 * g + j // 2, slice((j % 2) * HALF, (j % 2 + 1) * HALF)
                            a, c = (k[:, h, t], q[:, h, t]) if lv < 0 else (src[:, h, t], src[:, h, t])
                            m = nc.tensor.matmul(b[:, j * P:(j + 1) * P], a, c, start=True, stop=True)
                        m.then_inc(*pe_gla.tick("level", layer, lv, g))
                pe.wait_ge(*dve_gla.at("decayed", layer, 7))
                src = at_level(7)
                for g in range(heads // 4):
                    b = psum.claim(pe, "cross", layer, g)
                    for j in range(4):
                        h = 4 * g + j
                        m = nc.tensor.matmul(b[:, j * P:(j + 1) * P], src[:, h, 0:HALF], src[:, h, HALF:T],
                                             start=True, stop=True)
                    m.then_inc(*pe_gla.tick("cross", layer, g))
                for g in range(4):
                    b = psum.claim(pe, "o", layer, g)
                    pe.wait_ge(*dve_gla.at("causal", layer))
                    for j in (2 * g, 2 * g + 1):
                        m = values(b[:, (j % 2) * T:(j % 2 + 1) * T], vb[:, 0, j * P:(j + 1) * P],
                                   vb[:, 1, j * P:(j + 1) * P], at[:, j if kind == "hgrn" else j // 2, :])
                    m.then_inc(*pe_gla.tick("o", layer, g))
                    if g:
                        head_norm(layer, g - 1, act_gla, pe_gla, kind == "gla")
                head_norm(layer, 3, act_gla, pe_gla, kind == "gla")

            def four(layer):
                b = psum.claim(pe, "c2", layer)
                pe.wait_ge(*act_four.at("csq", layer))
                nc.tensor.matmul(b[:, 0:T], ones[:, :], sq[:, 0, :], start=True, stop=False)
                nc.tensor.matmul(b[:, 0:T], ones[0:64, :], sq[0:64, 1, :], start=False, stop=True)
                nc.tensor.matmul(b[:, T:2 * T], ones[:, :], sq[:, 2, :], start=True, stop=True)\
                    .then_inc(*pe_four.tick("c2", layer))
                norm_sums(layer, 0)
                norm_sums(layer, 1)
                pe.wait_ge(mla_loaded, 48 * (layer - DEPTH + 1))
                pe.wait_ge(*dve_four.at("cn", layer))
                cq0, cq1, ckv = pj[:, 6, :], pj[0:64, 7, :], pj[:, 8, :]
                for g in range(2):
                    b = psum.claim(pe, "mlaq", layer, g)
                    for j in range(2):
                        c = (2 * g + j) * 96
                        nc.tensor.matmul(b[0:96, j * T:(j + 1) * T], mlaw[:, c:c + 96], cq0, start=True, stop=False)
                        m = nc.tensor.matmul(b[0:96, j * T:(j + 1) * T], mlaw[0:64, 384 + c:384 + c + 96], cq1,
                                             start=False, stop=True)
                    m.then_inc(*pe_four.tick("mlaq", layer, g))
                for g in range(2):
                    b = psum.claim(pe, "mlak", layer, g)
                    for j in range(2):
                        c = 768 + (2 * g + j) * 128
                        m = nc.tensor.matmul(b[0:64, j * T:(j + 1) * T], mlaw[:, c:c + 64], ckv, start=True, stop=True)
                    m.then_inc(*pe_four.tick("mlak", layer, g))
                b = psum.claim(pe, "mlav", layer)
                wv = mlaw[:, 768:1280].rearrange("p (h a) -> p h a", h=4)[:, :, 64:128]
                for t in range(2):
                    m = nc.tensor.matmul(b[:, t * T:(t + 1) * T].rearrange("p (h a) -> p h a", h=4),
                                         ckv[:, t * HALF:(t + 1) * HALF], wv, start=True, stop=True)
                m.then_inc(*pe_four.tick("mlav", layer))
                for r in range(2, 6):
                    norm_sums(layer, r)
                b = psum.claim(pe, "tok", layer)
                pe.wait_ge(*dve_four.at("rows", layer))
                for j in range(4):
                    row = rows[0:4, j % 2, (j // 2) * HALF:(j // 2 + 1) * HALF]
                    m = nc.tensor.transpose(b[:, j * 8:j * 8 + 4], row, ident[0:4, 0:4])
                m.then_inc(*pe_four.tick("tok", layer))
                b = psum.claim(pe, "xtok", layer)
                pe.wait_ge(*act_proj.at("xbc", layer, 1))
                for j in range(4):
                    t, c = j // 2, j % 2
                    m = nc.tensor.transpose(b[:, j * P:(j + 1) * P], pj[:, 18 + c, t * HALF:(t + 1) * HALF], ident[:, :])
                m.then_inc(*pe_four.tick("xtok", layer))
                for g in range(2):
                    b = psum.claim(pe, "bcast", layer, g)
                    for j in range(2):
                        m = nc.tensor.matmul(b[:, j * T:(j + 1) * T], ident[0:4, 2 * g + j:2 * g + j + 1].to_broadcast([4, P]), rows[0:4, 0, :],
                                             start=True, stop=True)
                    m.then_inc(*pe_four.tick("bcast", layer, g))
                    b = psum.claim(pe, "bc", layer, g)
                    r = slice(64 * g, 64 * g + 64)
                    causal(b, pj[r, 20, :], pj[r, 21, :]).then_inc(*pe_four.tick("bc", layer, g))
                def rotated(r):
                    b = psum.claim(pe, "rot", layer, r)
                    pe.wait_ge(*dve_four.at("roped in", layer, r))
                    if r < 2:
                        nc.tensor.matmul(b[:, :], rot64[:, :], two(sq, r), start=True, stop=True)\
                            .then_inc(*pe_four.tick("rot", layer, r))
                    else:
                        nc.tensor.matmul(b[0:96, :], rot96[0:96, 0:96], two(xn, r - 2)[0:96, :], start=True, stop=True)\
                            .then_inc(*pe_four.tick("rot", layer, r))

                rotated(0)
                rotated(1)
                for h in range(4):
                    b = psum.claim(pe, "z", layer, h)
                    r = slice(64 * (h % 2), 64 * (h % 2) + 64)
                    causal(b, pj[r, 12 + h // 2, :], pj[r, 10 + h // 2, :]).then_inc(*pe_four.tick("z", layer, h))
                for n in range(8 + 3):
                    if n == 3:
                        stay_awake(FILL["softmax"])
                    if n < 8:
                        b = psum.claim(pe, "score", layer, n)
                        pe.wait_ge(*dve_four.at("roped", layer, 1 if n < 4 else 5))
                        if n < 4:
                            r = slice(64 * (n % 2), 64 * (n % 2) + 64)
                            q, k = pj[r, n // 2, :], pj[r, 2 + n // 2, :]
                        else:
                            q, k = yb_t[0:96, n - 4, :], yb_t[0:96, n, :]
                        nc.tensor.matmul(b[:, 0:HALF], q[:, 0:HALF], k[:, 0:HALF], start=True, stop=True)
                        nc.tensor.matmul(b[:, HALF:TRI], q[:, HALF:T], k[:, :], start=True, stop=True)\
                            .then_inc(*pe_four.tick("score", layer, n))
                    if n < 4:
                        rotated(2 + n)
                    if n >= 3:
                        n -= 3
                        b = psum.claim(pe, "probs", layer, n)
                        pe.wait_ge(*act_four.at("probs", layer, n))
                        p = prob(n)
                        nc.tensor.transpose(b[:, 0:HALF], p[:, 0:HALF], ident[:, :])
                        nc.tensor.transpose(b[:, HALF:T], p[:, HALF:T], ident[:, :])
                        nc.tensor.transpose(b[:, T:TRI], p[:, T:TRI], ident[:, :])\
                            .then_inc(*pe_four.tick("probs", layer, n))
                for h in range(4):
                    b = psum.claim(pe, "tail", layer, h)
                    pe.wait_ge(*pool_four.at("log1mb", layer, h))
                    l1 = sb_l1[:, h, :]
                    nc.tensor.matmul(b[:, 0:T], later[:, :], l1[:, 0:T], start=True, stop=False, skip_group_check=True)
                    nc.tensor.matmul(b[:, HALF:T], ones[:, :], l1[:, T:TRI], start=False, stop=True, skip_group_check=True)
                    nc.tensor.matmul(b[:, T:TRI], later[:, :], l1[:, T:TRI], start=True, stop=True)\
                        .then_inc(*pe_four.tick("tail", layer, h))
                for m in (0, 1, 3, 2):
                    b = psum.claim(pe, "o", layer, m)
                    pe.wait_ge(*(act_four if m < 2 else pool_four if m == 2 else dve_four).at("causal", layer, m))
                    mats = at if m < 2 else at2
                    for h in range(4):
                        c = m * T + h * 64
                        last = values(b[64 * (h % 2):64 * (h % 2) + 64, (h // 2) * T:(h // 2 + 1) * T],
                                      vb[:, 0, c:c + 64], vb[:, 1, c:c + 64], mats[:, 4 * (m % 2) + h, :])
                    last.then_inc(*pe_four.tick("o", layer, m))
                for m in (0, 1, 3, 2):
                    b = psum.claim(pe, "o2", layer, m)
                    pe.wait_ge(*act_four.at("o2", layer, m))
                    if m < 3:
                        nc.tensor.matmul(b[:, :], blk64[:, :], two(sq, m), start=True, stop=True)\
                            .then_inc(*pe_four.tick("o2", layer, m))
                    else:
                        nc.tensor.matmul(b[:, 0:T], ones[:, :], sq[:, 6, :], start=True, stop=False)
                        nc.tensor.matmul(b[:, 0:T], ones[:, :], sq[:, 7, :], start=False, stop=True)\
                            .then_inc(*pe_four.tick("o2", layer, m))

            def norm_sums(layer, r):
                b = psum.claim(pe, "n2", layer, r)
                pe.wait_ge(*act_four.at("n2", layer, r))
                if r < 2:
                    m = nc.tensor.matmul(b[:, :], blk64[:, :], nsq(r), start=True, stop=True)
                else:
                    m = nc.tensor.matmul(b[0:96, :], ones[0:96, 0:96], nsq(r)[0:96, :], start=True, stop=True)
                m.then_inc(*pe_four.tick("n2", layer, r))
            def parts(n):
                return {"high_ready": lambda k: act_norm.at("x hi", n, k),
                        "low_ready": lambda k: dve_norm.at("x lo", n, k // 2)}

            x_to_channels()
            norm = 0
            for layer, (kind, _) in enumerate(CHAIN[:layers]):
                if kind == "four":
                    rms_sum(norm)
                    norm += 1
                    stay_awake(FILL["normed"])
                    project(layer, kind, parts(norm - 1))
                    stay_awake(FILL["c2"])
                    four(layer)
                    stay_awake(FILL["mixed"])
                    out_project(layer)
                    rms_sum(norm)
                    norm += 1
                    stay_awake(FILL["normed"])
                    ffn(layer, parts(norm - 1))
                    stay_awake(FILL["residual"], bank=7)
                else:
                    if layer:
                        stay_awake(FILL["normed"])
                    project(layer, kind, parts(norm - 1))
                    if kind == "gdn":
                        stay_awake(FILL[kind])
                    gdn(layer) if kind == "gdn" else gla(layer, kind)
                    stay_awake(FILL["mixed"])
                    out_project(layer)
                    layer_norm(norm)
                    norm += 1
                    stay_awake(FILL["normed"])
                    ffn(layer, parts(norm - 1))
                    stay_awake(FILL["residual"], bank=7)
                    layer_norm(norm)
                    norm += 1
            if CHAIN[layers - 1][0] == "four":
                for n in range(4):
                    pe.wait_ge(*dve_norm.at("residual", norm, n))
            else:
                pe.wait_ge(*dve_norm.at("normed", norm - 1, KT - 1))
            for g in range(4):
                b = psum.claim(pe, "final", g)
                for j in range(4):
                    k, t = 2 * g + j // 2, j % 2
                    m = nc.tensor.transpose(b[:, j * P:(j + 1) * P], x[:, k, t * HALF:(t + 1) * HALF], ident[:, :])
                m.then_inc(*pe_out.tick("final", g))
        @block.sync
        def _(sp):
            unit = 0

            def load(dst, src, i=None):
                nonlocal unit
                if unit >= RING:
                    sp.wait_ge(*of_unit(pe_unit, unit - RING, i))
                sp.dma_start(dst, src).then_inc(w_loaded[unit % RING], 16)
                unit += 1

            def columns(w, l, c0, width):
                src = w[l, :, c0:c0 + width].rearrange("(k p) n -> p k n", p=P)
                return ring[:, unit % RING, 0:KT * width].rearrange("p (k n) -> p k n", k=KT), src

            def small_loads():
                for dst, src in IN_LOADS:
                    sp.dma_start(dst, src, allow_slow_non_contiguous=True).then_inc(in_loaded, 16)
                sp.wait_ge(*pool_setup.at("stage"))
                for dst, src in PARAM_LOADS:
                    sp.dma_start(dst, src, allow_slow_non_contiguous=True).then_inc(param_loaded, 16)

            sp.dma_start(yt, A["x"][0].rearrange("(t p) n -> p t n", p=P)).then_inc(x_loaded, 16)
            for layer, (kind, l) in enumerate(CHAIN[:layers]):
                w_in, w_out = {"gdn": ("gdn_w_in", "gdn_w_out"), "hgrn": ("hgrn_w_in", "hgrn_w_out"),
                               "gla": ("gla_w_in", "gla_w_out"), "four": ("w_in_2", "w_out_2")}[kind]
                if kind == "gla":
                    sp.wait_ge(*pe_gdn.at("o", 0, 3))
                    sp.dma_start(wgk2, A["gla_w_gk2"][l, :, :]).then_inc(gk_loaded, 16)
                for n, (c0, width, *_) in enumerate(units_in(kind)):
                    load(*columns(A[w_in], l, c0, width))
                    if layer == 0 and n == 2:
                        small_loads()
                if kind == "four":
                    sp.wait_ge(*(pe_gdn.at("o", layer - 1, 3) if layer == DEPTH else pe_four.at("o", layer - 1, 2)))
                    for dst, src in ((mlaw[:, 0:384], A["mla_w_uq_2"][l, 0:P, :]), (mlaw[0:64, 384:768], A["mla_w_uq_2"][l, P:P + 64, :]),
                                     (mlaw[:, 768:1280], A["mla_w_ukv_2"][l, :, :])):
                        sp.dma_start(dst, src).then_inc(mla_loaded, 16)
                for n in range(4):
                    load(*columns(A[w_out], l, 256 * n, 256))
                f_in, f_out, fl = (A["ffn_w_in"], A["ffn_w_down"], layer) if layer < DEPTH else \
                    (A["ffn_w_in_2"], A["ffn_w_out_2"], l)
                F = F_TILES * P
                w_up = f_in[fl, :, :].rearrange("(k p) n -> p k n", p=P)
                w_down = f_out[fl, :, :].rearrange("(k p) n -> p k n", p=P)

                def ffn_load(what, s, i=None):
                    slot = ring[:, unit % RING, :]
                    step = s if i is None else i * 2 + s
                    if what == "down":
                        load(slot.rearrange("p (k n) -> p k n", k=2), w_down[:, bass.ds(step * 2, 2), :], i)
                    else:
                        src = w_up[:, :, bass.ds(step * 256 + (F if what == "up" else 0), 256)]
                        load(slot.rearrange("p (k n) -> p k n", k=KT), src, i)

                def pair(s, i=None):
                    for what, step in (("gate", s), ("up", s), ("down", s - 1), ("gate", s + 1), ("up", s + 1), ("down", s)):
                        ffn_load(what, step, i)

                ffn_load("gate", 0)
                ffn_load("up", 0)
                pair(1)
                u0 = unit
                with Loop(book, sp, f"ffn{layer}", F_PAIRS) as i:
                    pair(3, i)
                unit = u0 + RING * F_PAIRS
                pair(F_STEPS - 2)
                ffn_load("down", F_STEPS - 1)
            for g in range(4):
                sp.wait_ge(*act_out.at("final", g))
                k = 2 * g
                for t in range(2):
                    sp.dma_start(out[0, t * HALF:(t + 1) * HALF, k * P:(k + 2) * P], yt[:, t, k * P:(k + 2) * P]).then_inc(out_stored, 16)
            sp.wait_ge(out_stored, 16 * 8)
        @block.gpsimd
        def _(pool):
            g = nc.gpsimd

            def settled():
                pool.wait_ge(*pool_setup.now())

            def fill(ap, value):
                g.memset(ap, value).then_inc(*pool_setup.tick())

            def keep(ap, pattern, base, row, op=ALU.is_ge, fill_=0.0):
                settled()
                g.affine_select(out=ap, in_=ap, compare_op=op, fill=fill_, base=base, pattern=pattern,
                                channel_multiplier=row).then_inc(*pool_setup.tick())

            fill(ident[:, :], 0.0)
            settled()
            g.affine_select(out=ident[:, :], in_=ident[:, :], compare_op=ALU.not_equal, fill=1.0, base=0,
                            pattern=[[-1, P]], channel_multiplier=1).then_inc(*pool_setup.tick("identity"))
            g.memset(stage[:, 0:PT_TILES * P], 0.0).then_inc(*pool_setup.tick("stage"))
            fill(ones[:, :], 1.0)
            fill(ones_d[:, :], 1.0 / D)
            for c, v in ((C_LN_EPS, 1e-5), (C_RMS_EPS, 1e-6), (C_QSCALE, -0.5 * float(np.log(128.0))),
                         (C_HALFPI, float(np.pi / 2)), (C_ONE, 1.0)):
                fill(const[:, c:c + 1], v)
            for ap in (blk64, incl, strict, later):
                fill(ap[:, :], 1.0)
            for ap in (rot64, rot96, amask):
                fill(ap[:, :], 0.0)
            b = blk64[:, :].rearrange("p (n c) -> p n c", n=2)
            keep(b, [[-64, 2], [0, 64]], 0, 1)
            keep(b, [[64, 2], [0, 64]], 63, -1)
            for c in (0, T):
                keep(incl[:, c:c + HALF], [[1, HALF]], 0, -1)
                keep(strict[:, c:c + HALF], [[1, HALF]], -1, -1)
                keep(amask[:, c:c + HALF], [[-1, HALF]], 0, 1, fill_=-1e30)
            keep(later[:, :], [[-1, P]], -1, 1)
            r = rot64[:, :].rearrange("p (n a c) -> p n a c", n=2, a=2)
            keep(r[:, :, 0, :], [[-64, 2], [-1, 32]], -32, 1, op=ALU.not_equal, fill_=-1.0)
            keep(r[:, :, 1, :], [[-64, 2], [-1, 32]], 0, 1, op=ALU.not_equal, fill_=1.0)
            keep(rot96[:, 64:80], [[-1, 16]], -80, 1, op=ALU.not_equal, fill_=-1.0)
            keep(rot96[:, 80:96], [[-1, 16]], -64, 1, op=ALU.not_equal, fill_=1.0)
            for lv in range(7):
                h = 1 << lv
                m = level[:, lv, :].rearrange("p (n a c) -> p n a c", a=2, c=h)
                fill(m[:, :, 0, :], 0.0)
                fill(m[:, :, 1, :], 1.0)
                keep(m[:, :, 1, :], [[-2 * h, P // (2 * h)], [0, h]], 0, 1)
                keep(m[:, :, 1, :], [[2 * h, P // (2 * h)], [0, h]], h - 1, -1)
            settled()
            g.memset(const[:, 7:8], 0.0).then_inc(*pool_setup.tick("constants"))

            unit = 0

            def split(count, i=None):
                nonlocal unit
                for _ in range(min(count, len(sizes) - unit)):
                    part = slice(sizes[unit] * DVE_SHARE // 8, sizes[unit])
                    pool.wait_ge(*of_unit(dve_hi, unit, i))
                    g.tensor_tensor(w_lo[:, unit % RING, part], ring[:, unit % RING, part], w_hi[:, unit % HI, part], ALU.subtract).then_inc(*pool_lo.tick())
                    unit += 1

            def rest(layer, count):
                nonlocal unit
                split(4 + 2 + RING)
                u0 = unit
                with Loop(book, pool, f"ffn{layer}", F_PAIRS) as i:
                    split(RING, i)
                unit = u0 + RING * F_PAIRS
                split(RING + 1 + count)

            def differences(layer, heads):
                pool.wait_ge(*dve_gla.at("cumulated", layer))
                pool.wait_ge(*act_gla.at("k", layer))
                for lv in range(8):
                    if lv >= 2:
                        pool.wait_ge(*dve_gla.at("decayed", layer, lv - 2))
                    g3 = flat(pj[:, 8:8 + heads, :]).rearrange("p (n c) -> p n c", c=2 << lv)
                    g.tensor_tensor(level_diff(lv, heads), g3,
                                    g3[:, :, (1 << lv) - 1:1 << lv].to_broadcast([P, heads * T // (2 << lv), 2 << lv]),
                                    ALU.subtract).then_inc(*pool_gla.tick("difference", layer, lv))

            def stick_breaking(layer):
                for r in range(6):
                    pool.wait_ge(*pe_four.at("rot", layer, r))
                    n = P if r < 2 else 96
                    cos = trig[0:n, (0 if r < 2 else 2):(1 if r < 2 else 3), :].to_broadcast([n, 2, T])
                    q2 = (two(sq, r) if r < 2 else two(xn, r - 2)[0:96, :]).rearrange("p (a n) -> p a n", a=2)
                    g.tensor_tensor(q2, q2, cos, ALU.mult).then_inc(*pool_four.tick("cos", layer, r))
                for h in range(4):
                    pool.wait_ge(*dve_four.at("log beta", layer, h))
                    l1 = sb_l1[:, h, :]
                    g.tensor_tensor(l1, sb_t[:, h, :], at2[:, h, :], ALU.subtract).then_inc(*pool_four.tick())
                    pool.wait_ge(*pool_four.now())
                    g.tensor_tensor(l1, l1, strict[:, :], ALU.mult).then_inc(*pool_four.tick("log1mb", layer, h))
                for h in range(4):
                    pool.wait_ge(*act_four.at("a", layer, h))
                    g.tensor_tensor(at2[:, h, :], sb_t[:, h, :], strict[:, :], ALU.mult).then_inc(*pool_four.tick("causal", layer, 2))

            split(HI)
            for layer, (kind, _) in enumerate(CHAIN[:layers]):
                split(len(units_in(kind)) - HI)
                if kind in ("hgrn", "gla"):
                    differences(layer, 8 if kind == "hgrn" else 4)
                if kind == "four":
                    stick_breaking(layer)
                if kind != "gdn":
                    rest(layer, HI)
                    continue
                for h in range(8):
                    pool.wait_ge(*act_gdn.at("decay", layer, h))
                    d = dec[:, h % 2, :]
                    g.tensor_tensor(d, d, incl[:, :], ALU.mult).then_inc(*pool_gdn.tick("decay", layer, h))
                for lv in range(7):
                    for q in range(4):
                        t, h0 = q // 2, 4 * (q % 2)
                        pool.wait_ge(*(dve_gdn.at("lt", layer, h0 + 3) if lv == 0 else
                                       dve_gdn.at("XT", layer, 0, q) if lv == 1 else pe_gdn.at("cx", layer, lv - 1, q)))
                        g.tensor_tensor(ct[:, 4 * q:4 * q + 4, :], lt[:, h0:h0 + 4, t * T:t * T + HALF],
                                        level[:, lv:lv + 1, :].to_broadcast([P, 4, HALF]), ALU.mult)\
                            .then_inc(*pool_gdn.tick("masked", layer, lv, q))
                rest(layer, HI)
        @block.scalar
        def _(act):
            def run(sig, out_, in_, func, *key, **kw):
                nc.scalar.activation(out_, in_, func, **kw).then_inc(*sig.tick(*key))

            def log_exp_tables():
                nc.scalar.preload_act_table_set("natural_log_exp_and_others")

            def rstd(sig, dst, bank_ap, bank_key, scale, eps, *key, bias=None):
                run(sig, dst, bank_ap, ACT.Ln, scale=scale, bias=const[0:dst.shape[0], eps:eps + 1])
                if bank_key:
                    psum.release(sig, *bank_key)
                act.wait_ge(*sig.now())
                kw = {} if bias is None else {"bias": bias}
                run(sig, dst, dst, ACT.Exp, *key, scale=-0.5, **kw)

            def log1p_exp(sig, ap, in_, *key):
                run(sig, ap, in_, ACT.Abs)
                act.wait_ge(*sig.now())
                run(sig, ap, ap, ACT.Exp, scale=-1.0)
                act.wait_ge(*sig.now())
                run(sig, ap, ap, ACT.Ln, *key, bias=1.0)

            def params_to_columns():
                for g in range(3):
                    act.wait_ge(*pe_setup.at("params", g))
                    w = min(512, PT_TILES * P - 512 * g)
                    run(act_setup, params[:, 512 * g:512 * g + w], psum.bank("params", g)[:, 0:w], ACT.Copy, "params", g)
                    psum.release(act_setup, "params", g)

            def x_to_channels():
                for g in range(4):
                    act.wait_ge(*pe_setup.at("x", g))
                    run(act_norm, two(xh, g), psum.bank("x", g)[:, :], ACT.Copy, "x hi", -1, 2 * g)
                    act_norm.name_also("x hi", -1, 2 * g + 1)
                    run(act_setup, two(x, g), psum.bank("x", g)[:, :], ACT.Copy, "x", g)
                    psum.release(act_setup, "x", g)

            def project(layer, kind, l):
                for n, (c0, w, how, name, idx) in enumerate(units_in(kind)):
                    key = ("proj", layer, n)
                    b = psum.bank(*key)
                    s = act_proj
                    if name in ("conv", "xbc"):
                        act.wait_ge(*dve_conv.at("conv", layer, idx // 2))
                        if name == "conv":
                            run(s, pj2(idx), pj2(idx), ACT.Silu, "conv", layer, idx // 2)
                            if n == N_QK:
                                act.wait_ge(*s.now())
                                qk_squares(layer)
                        else:
                            for c in (idx, idx + 1):
                                run(s, pj[:, 18 + c, :], pj[:, 18 + c, :], ACT.Silu, "xbc", layer, idx // 2,
                                    bias=par(PT_MISC * P + R_CONVB + l * 4 + c))
                        continue
                    if kind == "gdn" and n == N_CONV + 3:
                        act.wait_ge(*s.now())
                        log_exp_tables()
                        qk_rstds(layer, range(8))
                    act.wait_ge(*pe_unit.at("unit", layer, n))
                    if name == "ba":
                        run(s, rows[0:8, 2:4, :].rearrange("p a n -> p (a n)"), b[0:8, :], ACT.Copy, "ba", layer)
                    elif name == "gate":
                        run(s, pj2(24 + idx), b[:, :], ACT.Silu, "gate", layer, idx)
                    elif name == "f":
                        run(s, pj2(8 + idx), b[:, :], ACT.Copy, "f", layer, idx)
                    elif name == "qsilu":
                        run(s, pj2(idx), b[:, :], ACT.Silu, "q", layer, idx)
                    elif name in ("v", "vmoba", "vsb"):
                        c = {"v": T * idx, "vmoba": 0, "vsb": 2 * T}[name]
                        run(s, vb[:, :, c:c + T], b[:, :].rearrange("p (t n) -> p t n", t=2), ACT.Copy, name, layer, idx)
                    elif name == "gk":
                        run(s, rows[0:16, 4, :], b[0:16, 0:T], ACT.Copy, "gk", layer)
                    elif name == "qscaled":
                        run(s, pj2(idx), b[:, :], ACT.Copy, "q", layer, idx, scale=128.0 ** -0.5)
                    elif name == "k":
                        run(s, pj2(4 + idx), b[:, :], ACT.Copy, "k", layer, idx)
                    elif name == "dt":
                        run(s, rows[0:4, 2, :], b[0:4, 0:T], ACT.Copy, "dt", layer)
                    elif name == "plain":
                        run(s, pj2(idx), b[:, :], ACT.Copy, "plain", layer, idx)
                    elif name == "cq":
                        run(s, pj[:, 6, :], b[:, 0:T], ACT.Copy)
                        run(s, pj[0:64, 7, :], b[0:64, T:2 * T], ACT.Copy, "cq", layer)
                    elif name == "ckv":
                        run(s, pj[:, 8, :], b[:, 0:T], ACT.Copy)
                        run(s, yb_t[64:96, 4:8, :], b[64:96, T:2 * T].rearrange("p (a n) -> p a n", a=1).to_broadcast([32, 4, T]),
                            ACT.Copy, "ckv", layer)
                    elif name == "z":
                        run(s, pj2(16), b[:, :], ACT.Silu, "z", layer)
                    psum.release(s, *key)
                    if layer == 0 and n == 0:
                        params_to_columns()
                        act.wait_ge(*dve_setup.at("angles"))
                        run(act_setup, flat(trig), flat(trig), ACT.Sin, "trig")
                    if kind == "gdn" and n == 0:
                        act.wait_ge(*s.now())
                        decay_rows(layer, l)
                    if kind in ("hgrn", "gla") and (name, idx) in (("f", 6), ("k", 2)):
                        gla_decays(layer, kind)
                act.wait_ge(*act_proj.now())
                log_exp_tables()

            def norm_rstd(n, eps):
                act.wait_ge(*pe_norm.at("square", n))
                rstd(act_norm, stat[:, 0, 0:T], psum.bank("square", n)[:, 0:T], ("square", n), 1.0, eps, "rstd", n)

            def high_parts(n, biases=None):
                for k in range(KT):
                    act.wait_ge(*dve_norm.at("scaled", n, k))
                    if biases is None:
                        run(act_norm, xh[:, k, :], xn[:, k, :], ACT.Copy, "x hi", n, k)
                    else:
                        run(act_norm, xh[:, k, :], xn[:, k, :], ACT.Identity, "x hi", n, k, bias=par(biases + k))

            def layer_norm(n, b_col, is_input=True):
                for m in range(4):
                    act.wait_ge(*dve_norm.at("centred", n, m))
                    run(act_norm, two(sq, m), two(xn, m), ACT.Square, "square", n, m)
                norm_rstd(n, C_LN_EPS)
                if is_input:
                    high_parts(n, b_col)

            def rms_norm(n, ready):
                for m in range(4):
                    act.wait_ge(*ready(m))
                    run(act_norm, two(sq, m), two(x, m), ACT.Square, "square", n, m)
                norm_rstd(n, C_RMS_EPS)
                high_parts(n)

            def ffn(layer):
                conv = layer >= DEPTH

                def gated(par_, key, before):
                    src = fconv[:, par_, 0:2, :].rearrange("p a n -> p (a n)") if conv else banks[4 + 2 * par_][:, :]
                    act.wait_ge(*(dve_ffn.at("conv gate", layer, key) if conv else pe_unit.at("gate", layer, key)))
                    if before is not None:
                        act.wait_ge(*before)
                    run(act_ffn, flat(gact[:, par_]), src, ACT.Silu, "gated", layer, key)

                gated(0, 0, None)
                gated(1, 1, None)
                gated(0, 2, dve_ffn.at("hidden", layer, 0))
                with Loop(book, act, f"ffn{layer}", F_PAIRS):
                    gated(1, "a", dve_ffn.at("hidden", layer, "a", ago=1))
                    gated(0, "b", dve_ffn.at("hidden", layer, "b", ago=1))
                gated(1, 9, dve_ffn.at("hidden", layer, "a"))
                gated(0, 10, dve_ffn.at("hidden", layer, "b"))

            def head_norms(layer, sig, pe_sig, dve_sig, both, inv_dv):
                w = T if both else 2 * T

                def squares(g):
                    act.wait_ge(*pe_sig.at("o", layer, g))
                    run(sig, two(sq, g), psum.bank("o", layer, g)[:, :], ACT.Square, "o2", layer, g)

                def high(g):
                    act.wait_ge(*dve_sig.at("mixed", layer, g))
                    run(sig, two(xh, g), two(y, g), ACT.Copy, "mixed hi", layer, g)

                squares(0)
                for g in range(4):
                    if g < 3:
                        squares(g + 1)
                    act.wait_ge(*pe_sig.at("o2", layer, g))
                    rstd(sig, stat[:, g, 0:w], psum.bank("o2", layer, g)[:, 0:w], ("o2", layer, g), inv_dv, C_RMS_EPS,
                         "rstd", layer, g)
                    if g:
                        high(g - 1)
                high(3)

            def qk_squares(layer):
                for g in range(8):
                    run(act_gdn, gsq(g), pj2(2 * g), ACT.Square, "square", layer, g)

            def decay_rows(layer, l):
                s = act_gdn
                log_exp_tables()
                act.wait_ge(*dve_gdn.at("a + bias", layer))
                log1p_exp(s, rows[0:8, 4:6, :].rearrange("p a n -> p (a n)"), rows[0:8, 2:4, :].rearrange("p a n -> p (a n)"),
                          "log1p", layer)
                run(s, head[0:8, 6:7], head[0:8, l:l + 1], ACT.Exp, "a", layer)
                act.wait_ge(*dve_gdn.at("log beta", layer))
                run(s, rows[0:8, 1, :], rows[0:8, 1, :], ACT.Exp, "beta", layer)

            def qk_rstds(layer, gs):
                s = act_gdn
                for g in gs:
                    act.wait_ge(*pe_gdn.at("qk2", layer, g))
                    if g >= 4:
                        act.wait_ge(*dve_gdn.at("unit", layer, g - 4))
                    rstd(s, stat[:, g % 4, :], psum.bank("qk2", layer, g)[:, :], ("qk2", layer, g), 1.0, C_RMS_EPS,
                         "rstd", layer, "qk", g, bias=const[:, C_QSCALE:C_QSCALE + 1] if g < 4 else None)

            def gdn(layer, l):
                s = act_gdn
                for h in range(8):
                    act.wait_ge(*dve_gdn.at("difference", layer, h))
                    d = dec[:, h % 2, :]
                    run(s, d, d, ACT.Exp, "decay", layer, h)

                def transposed(lv, g):
                    act.wait_ge(*pe_gdn.at("transposed", layer, lv, g))
                    dst, key = (four_tiles(inv, g), ("X",)) if lv == 0 else (four_tiles(inv, 4 + g), ("XT",))
                    run(s, dst, psum.bank("transposed", layer, lv, g)[:, :], ACT.Copy, *key, layer, *([lv] if lv else []), g)
                    psum.release(s, "transposed", layer, lv, g)

                for g in range(4):
                    transposed(0, g)
                for lv in range(1, 7):
                    for g in range(4):
                        act.wait_ge(*pe_gdn.at("cx", layer, lv, g))
                        run(s, flat(cx[:, 4 * g:4 * g + 4, :]), psum.bank("cx", layer, lv, g)[:, 0:4 * HALF2], ACT.Copy,
                            "cx", layer, lv, g)
                        psum.release(s, "cx", layer, lv, g)
                        if g >= 2 and lv < 6:
                            transposed(lv, g - 2)
                    if lv < 6:
                        transposed(lv, 2)
                        transposed(lv, 3)
                for what, t in (("u0", 0), ("u1", 1)):
                    for g in range(2):
                        act.wait_ge(*pe_gdn.at(what, layer, g))
                        run(s, four_tiles(ct, 2 * t + g), psum.bank(what, layer, g)[:, :], ACT.Copy, what, layer, g)
                        psum.release(s, what, layer, g)
                head_norms(layer, s, pe_gdn, dve_gdn, False, 1.0 / 128)

            def gla_decays(layer, kind):
                s = act_gla
                heads = 8 if kind == "hgrn" else 4
                n = heads * T
                if kind == "hgrn":
                    act.wait_ge(*dve_gla.at("logits", layer))
                    run(s, flat(lbs[:, 0:4]), flat(lbs[:, 0:4]), ACT.Exp, "exp logits", layer)
                    act.wait_ge(*dve_gla.at("bounds", layer))
                    run(s, flat(lbs[:, 4:6]), flat(lbs[:, 4:6]), ACT.Ln, "log bounds", layer)
                else:
                    for g in range(2):
                        act.wait_ge(*pe_gla.at("gk", layer, g))
                        b = psum.bank("gk", layer, g)
                        for j in range(2):
                            c = 2 * g + j
                            run(s, pj[:, 8 + c, :], b[:, j * T:(j + 1) * T], ACT.Identity, "gk", layer, g,
                                bias=par(PT_MISC * P + R_BGK + c))
                        psum.release(s, "gk", layer, g)
                f = flat(pj[:, 8:8 + heads, :])
                act.wait_ge(*(act_proj.at("f", layer, 6) if kind == "hgrn" else s.now()))
                run(s, flat(ct)[:, 0:n], f, ACT.Abs)
                act.wait_ge(*s.now())
                run(s, flat(ct)[:, 0:n], flat(ct)[:, 0:n], ACT.Exp, scale=-1.0)
                act.wait_ge(*s.now())
                run(s, flat(sq)[:, 0:n], flat(ct)[:, 0:n], ACT.Ln, "log1p f", layer, bias=1.0)
                if kind == "hgrn":
                    act.wait_ge(*dve_gla.at("log k", layer))
                    for h in range(8):
                        run(s, yb_t[:, h, :], ct_t[:, h, :], ACT.Exp, "k", layer, bias=lbs[:, 5, h:h + 1])
                    act.wait_ge(*dve_gla.at("f against bound", layer))
                    run(s, flat(sq), flat(sq), ACT.Abs)
                    act.wait_ge(*s.now())
                    run(s, flat(sq), flat(sq), ACT.Exp, scale=-1.0)
                    act.wait_ge(*s.now())
                    run(s, flat(ct), flat(sq), ACT.Ln, "log1p f2", layer, bias=1.0)
                else:
                    run(s, const[:, 6:7], const[:, 0:1], ACT.Copy, "k", layer)

            def gla(layer, kind, l):
                s = act_gla
                heads = 8 if kind == "hgrn" else 4
                for lv in range(8):
                    act.wait_ge(*pool_gla.at("difference", layer, lv))
                    d = level_diff(lv, heads)
                    run(s, d[:, :, 0:1 << lv], d[:, :, 0:1 << lv], ACT.Exp, scale=-1.0)
                    run(s, d[:, :, 1 << lv:], d[:, :, 1 << lv:], ACT.Exp, "decay", layer, lv)
                head_norms(layer, s, pe_gla, dve_gla, kind == "gla", 1.0 / (128 if kind == "hgrn" else 256))

            def four(layer, l):
                s = act_four
                run(s, flat(sq[:, 0:3, :])[:, 0:T], pj[:, 6, :], ACT.Square)
                run(s, sq[0:64, 1, :], pj[0:64, 7, :], ACT.Square)
                run(s, sq[:, 2, :], pj[:, 8, :], ACT.Square, "csq", layer)
                for r in range(2):
                    run(s, nsq(r), pj2(2 * r), ACT.Square, "n2", layer, r)
                act.wait_ge(*dve_four.at("dt + bias", layer))
                log1p_exp(s, rows[0:4, 3, :], rows[0:4, 2, :], "log1p dt", layer)
                run(s, head[0:4, 6:7], hssm[0:4, l:l + 1], ACT.Exp, "a", layer)
                act.wait_ge(*pe_four.at("c2", layer))
                b = psum.bank("c2", layer)
                rstd(s, stat[:, 3, 0:T], b[:, 0:T], None, 1.0 / 192, C_RMS_EPS, "c rstd", layer, 0)
                rstd(s, stat[:, 3, T:2 * T], b[:, T:2 * T], ("c2", layer), 1.0 / 128, C_RMS_EPS, "c rstd", layer, 1)
                for r in range(2):
                    act.wait_ge(*pe_four.at("n2", layer, r))
                    rstd(s, stat[:, r, :], psum.bank("n2", layer, r)[:, :], ("n2", layer, r), 1.0 / 64, C_RMS_EPS,
                         "rstd", layer, "n", r)
                for g in range(2):
                    act.wait_ge(*pe_four.at("mlaq", layer, g))
                    run(s, yb_t[0:96, 2 * g:2 * g + 2, :].rearrange("p a n -> p (a n)"),
                        psum.bank("mlaq", layer, g)[0:96, :], ACT.Copy, "mlaq", layer, g)
                    psum.release(s, "mlaq", layer, g)
                for g in range(2):
                    act.wait_ge(*pe_four.at("mlak", layer, g))
                    run(s, yb_t[0:64, 4 + 2 * g:6 + 2 * g, :].rearrange("p a n -> p (a n)"),
                        psum.bank("mlak", layer, g)[0:64, :], ACT.Copy, "mlak", layer, g)
                    psum.release(s, "mlak", layer, g)
                act.wait_ge(*pe_four.at("mlav", layer))
                run(s, vb[:, :, T:2 * T], psum.bank("mlav", layer)[:, :].rearrange("p (t n) -> p t n", t=2), ACT.Copy,
                    "mlav", layer)
                psum.release(s, "mlav", layer)
                for r in range(2, 6):
                    act.wait_ge(*s.at("mlaq" if r < 4 else "mlak", layer, r % 2))
                    run(s, nsq(r)[0:96, :], flat(yb_t[:, 2 * (r - 2):2 * (r - 2) + 2, :])[0:96, :], ACT.Square, "n2", layer, r)
                for r in range(2, 6):
                    act.wait_ge(*pe_four.at("n2", layer, r))
                    act.wait_ge(*(dve_four.at("cn", layer) if r < 4 else dve_four.at("roped in", layer, r - 4)))
                    rstd(s, stat[0:96, r % 4, :], psum.bank("n2", layer, r)[0:96, :], ("n2", layer, r), 1.0 / 96, C_RMS_EPS,
                         "rstd", layer, "n", r)
                for h in range(4):
                    act.wait_ge(*dve_four.at("difference", layer, h))
                    run(s, at[:, h, :], at[:, h, :], ACT.Exp, "decay", layer, h)
                act.wait_ge(*dve_four.at("causal", layer, 3))
                for n in range(8 + 4):
                    if n < 8:
                        act.wait_ge(*dve_four.at("max", layer, n))
                        p = prob(n)
                        run(s, p[:, 0:HALF], p[:, 0:HALF], ACT.Exp, bias=small[:, n, 0:1], accum_out=small[:, n, 2:3])
                        run(s, p[:, HALF:TRI], p[:, HALF:TRI], ACT.Exp, "exp", layer, n, bias=small[:, n, 1:2],
                            accum_out=small[:, n, 3:4])
                        if n % 2 == 0:
                            h = n // 2
                            act.wait_ge(*dve_four.at("z", layer, h))
                            log1p_exp(s, sb_t[:, h, :], at2[:, h, :], "log1p z", layer, h)
                    if 2 <= n < 8 + 2:
                        p = prob(n - 2)
                        act.wait_ge(*dve_four.at("inverse sum", layer, n - 2))
                        run(s, p[:, 0:HALF], p[:, 0:HALF], ACT.Copy, scale=small[:, n - 2, 2:3])
                        run(s, p[:, HALF:TRI], p[:, HALF:TRI], ACT.Copy, "probs", layer, n - 2, scale=small[:, n - 2, 3:4])
                    if n >= 4:
                        n -= 4
                        act.wait_ge(*pe_four.at("probs", layer, n))
                        b = psum.bank("probs", layer, n)
                        run(s, at[:, n, :], b[:, 0:TRI], ACT.Copy, "causal", layer, n // 4)
                        psum.release(s, "probs", layer, n)
                for h in range(4):
                    act.wait_ge(*dve_four.at("log a", layer, h))
                    run(s, sb_t[:, h, :], sb_t[:, h, :], ACT.Exp, "a", layer, h)
                act.wait_ge(*pool_four.at("causal", layer, 2))
                for m in (0, 1, 3, 2):
                    if m < 3:
                        act.wait_ge(*pe_four.at("o", layer, m))
                        b = psum.bank("o", layer, m)
                        run(s, oc4[:, m, :], b[:, :], ACT.Copy, "o", layer, m)
                        run(s, two(sq, m), b[:, :], ACT.Square, "o2", layer, m)
                        psum.release(s, "o", layer, m)
                    else:
                        act.wait_ge(*dve_four.at("gated", layer))
                        run(s, two(sq, 3), oc4[:, 3, :], ACT.Square, "o2", layer, 3)
                for m in (0, 1, 3, 2):
                    act.wait_ge(*pe_four.at("o2", layer, m))
                    w, sc = (2 * T, 1.0 / 64) if m < 3 else (T, 1.0 / 256)
                    rstd(s, stat[:, m, 0:w], psum.bank("o2", layer, m)[:, 0:w], ("o2", layer, m), sc, C_RMS_EPS,
                         "rstd", layer, m)
                for m in (0, 1, 3, 2):
                    act.wait_ge(*dve_four.at("mixed", layer, m))
                    run(s, two(xh, m), two(y, m), ACT.Copy, "mixed hi", layer, m)

            x_to_channels()
            act.wait_ge(*pool_setup.at("constants"))
            norm = 0
            for layer, (kind, l) in enumerate(CHAIN[:layers]):
                if kind == "four":
                    rms_norm(norm, (lambda m: dve_norm.at("normed", norm - 1, 2 * m + 1)) if layer == DEPTH else
                             (lambda m: dve_norm.at("residual", norm - 0, m)))
                    norm += 1
                    project(layer, kind, l)
                    four(layer, l)
                    rms_norm(norm, lambda m: dve_norm.at("residual", norm, m))
                    norm += 1
                    ffn(layer)
                else:
                    project(layer, kind, l)
                    gdn(layer, l) if kind == "gdn" else gla(layer, kind, l)
                    layer_norm(norm, PT_LN * P + R_MIXB + 8 * layer)
                    norm += 1
                    ffn(layer)
                    log_exp_tables()
                    layer_norm(norm, PT_LN * P + R_FFNB + 8 * layer, layer < min(layers, DEPTH) - 1)
                    norm += 1
            for g in range(4):
                act.wait_ge(*pe_out.at("final", g))
                run(act_out, yt[:, :, 2 * g * P:(2 * g + 2) * P].rearrange("p t (k n) -> p k t n", k=2),
                    psum.bank("final", g)[:, :].rearrange("p (k t n) -> p k t n", k=2, t=2), ACT.Copy, "final", g)
        @block.vector
        def _(dve):
            v = nc.vector

            def tt(sig, out_, a, b, op, *key):
                v.tensor_tensor(out_, a, b, op).then_inc(*sig.tick(*key))

            def ts(sig, out_, a, s1, op0, s2=None, op1=None, *key):
                if op1 is None:
                    v.tensor_scalar(out_, a, s1, None, op0).then_inc(*sig.tick(*key))
                else:
                    v.tensor_scalar(out_, a, s1, s2, op0, op1).then_inc(*sig.tick(*key))

            def stt(sig, out_, a, s1, b, op0, op1, *key):
                v.scalar_tensor_tensor(out=out_, in0=a, scalar=s1, in1=b, op0=op0, op1=op1).then_inc(*sig.tick(*key))

            def scan(sig, out_, in_, *key):
                n = in_.shape[0]
                v.tensor_tensor_scan(out_, const[0:n, C_ONE:C_ONE + 1].to_broadcast([n, T]), in_, 0.0, ALU.mult, ALU.add)\
                    .then_inc(*sig.tick(*key))

            def conv(sig, dsts, srcs, weights, taps, key, biases=None, interleaved=None):
                for n, (d, s) in enumerate(zip(dsts, srcs)):
                    if biases is None:
                        ts(sig, d, s, weights(n, taps - 1), ALU.mult)
                    else:
                        ts(sig, d, s, weights(n, taps - 1), ALU.mult, biases(n), ALU.add)
                for back in range(1, taps):
                    dve.wait_ge(*sig.now())
                    for n, (d, s) in enumerate(zip(dsts, srcs)):
                        k = key if back == taps - 1 else ()
                        stt(sig, d[:, back:T], s[:, 0:T - back], weights(n, taps - 1 - back), d[:, back:T],
                            ALU.mult, ALU.add, *k)

            unit = 0

            def split(count=1, i=None):
                nonlocal unit
                for _ in range(min(count, len(sizes) - unit)):
                    n, share = sizes[unit], sizes[unit] * DVE_SHARE // 8
                    w, high = ring[:, unit % RING, :], w_hi[:, unit % HI, :]
                    dve.wait_ge(*loaded(unit, i))
                    if unit >= HI:
                        dve.wait_ge(*of_unit(pe_unit, unit - HI, i))
                    v.tensor_copy(high[:, 0:n], w[:, 0:n]).then_inc(*dve_hi.tick())
                    dve.wait_ge(*of_unit(dve_hi, unit, i))
                    v.tensor_tensor(w_lo[:, unit % RING, 0:share], w[:, 0:share], high[:, 0:share], ALU.subtract).then_inc(*dve_lo.tick())
                    unit += 1

            def hidden_parts(par_, *key):
                high, low, src = flat(hid_hi[:, par_]), flat(hid_lo[:, par_]), flat(hid[:, par_])
                dve.wait_ge(*dve_ffn.now())
                v.tensor_copy(high, src).then_inc(*dve_ffn.tick())
                dve.wait_ge(*dve_ffn.now())
                tt(dve_ffn, low, src, high, ALU.subtract, "hidden lo", *key)

            def setup():
                s = dve_setup
                dve.wait_ge(*pool_setup.at("constants"))
                dve.wait_ge(in_loaded, 16 * N_IN)
                v.tensor_copy(trig[:, 0, :], pos_i).then_inc(*s.tick())
                dve.wait_ge(*s.now())
                ts(s, trig[:, 3, :], trig[:, 0, :], freqs[:, 1:2], ALU.mult)
                ts(s, trig[:, 1, :], trig[:, 0, :], freqs[:, 0:1], ALU.mult)
                turn = sq[:, 0:4, :]
                for j in (1, 3):
                    dve.wait_ge(*s.now())
                    ts(s, turn[:, j, :], trig[:, j, :], float(1 / (2 * np.pi)), ALU.mult)
                    dve.wait_ge(*s.now())
                    ts(s, turn[:, j, :], turn[:, j, :], 12582912.0, ALU.add)
                    dve.wait_ge(*s.now())
                    ts(s, turn[:, j, :], turn[:, j, :], 12582912.0, ALU.subtract)
                    for part in TWO_PI:
                        dve.wait_ge(*s.now())
                        stt(s, trig[:, j, :], turn[:, j, :], -part, trig[:, j, :], ALU.mult, ALU.add)
                    dve.wait_ge(*s.now())
                    ts(s, trig[:, j - 1, :], trig[:, j, :], float(np.pi / 2), ALU.add)
                    dve.wait_ge(*s.now())
                    ts(s, turn[:, j, :], trig[:, j - 1, :], float(np.pi), ALU.is_gt, float(-2 * np.pi), ALU.mult)
                    dve.wait_ge(*s.now())
                    tt(s, trig[:, j - 1, :], trig[:, j - 1, :], turn[:, j, :], ALU.add)
                dve.wait_ge(*s.now())
                ts(s, flat(trig), flat(trig), 3.1415925, ALU.min, -3.1415925, ALU.max, "angles")

            def project(layer, kind, l):
                for n, (c0, w, how, name, idx) in enumerate(units_in(kind)):
                    if kind in ("hgrn", "gla"):
                        continue
                    if n + HI < len(units_in(kind)):
                        split()
                    if kind == "gdn" and n > N_CONV:
                        unit_qk(layer, ((), (0, 1, 2, 3), (4, 5), (6, 7))[n - N_CONV - 1])
                    if kind == "gdn" and n == 0:
                        decay_rows(layer, l)
                    if name not in ("conv", "xbc"):
                        continue
                    base, tiles, n_tiles = (0, (PT_CONV + l) * P, 24) if name == "conv" else \
                        (18, PT_SSM * P + l * 16, 4)
                    if layer == 0:
                        dve.wait_ge(*act_setup.at("params", 2))
                    dve.wait_ge(*pe_unit.at("unit", layer, n))
                    b = psum.bank("proj", layer, n)
                    conv(dve_conv, [pj[:, base + idx + j, :] for j in range(2)], [b[:, j * T:(j + 1) * T] for j in range(2)],
                         lambda j, tap: par(tiles + tap * n_tiles + idx + j), 4, ("conv", layer, idx // 2))
                    psum.release(dve_conv, "proj", layer, n)

            def residual(n, key, scale):
                for m in range(4):
                    if key[0] == "out":
                        split()
                    dve.wait_ge(*(pe_unit.at("out", key[1], m) if key[0] == "out" else 
                                  pe_unit.at("down", key[1], "last") if m == 3 else pe_norm.at("down", key[1], m)))
                    b = psum.bank(*key, m)[:, :]
                    xm = two(x, m)
                    if scale is None:
                        tt(dve_norm, xm, xm, b, ALU.add, "residual", n, m)
                    else:
                        stt(dve_norm, xm, xm, scale, b, ALU.mult, ALU.add, "residual", n, m)
                    psum.release(dve_norm, *key, m)

            def layer_norm(n, g_col, b_col, is_input=True):
                s = dve_norm
                dve.wait_ge(*pe_norm.at("mean", n))
                mean = psum.bank("mean", n)[:, 0:T].rearrange("p (a n) -> p a n", a=1).to_broadcast([P, 2, T])
                for m in range(4):
                    tt(s, xn[:, 2 * m:2 * m + 2, :], x[:, 2 * m:2 * m + 2, :], mean, ALU.subtract, "centred", n, m)
                psum.release(s, "mean", n)
                dve.wait_ge(*act_norm.at("rstd", n))
                for k in range(KT):
                    stt(s, xn[:, k, :], xn[:, k, :], par(g_col + k), stat[:, 0, 0:T], ALU.mult, ALU.mult, "scaled", n, k)
                for k in range(KT):
                    dve.wait_ge(*s.at("scaled", n, k))
                    ts(s, x[:, k, :], xn[:, k, :], par(b_col + k), ALU.add, None, None, "normed", n, k)
                if is_input:
                    low_parts(s, x, n)

            def low_parts(s, src, n):
                for m in range(4):
                    dve.wait_ge(*s.at("normed", n, 2 * m + 1))
                    dve.wait_ge(*act_norm.at("x hi", n, 2 * m + 1))
                    tt(s, two(xl, m), two(src, m), two(xh, m), ALU.subtract, "x lo", n, m)

            def rms_norm(n, g_col):
                dve.wait_ge(*act_norm.at("rstd", n))
                for k in range(KT):
                    stt(dve_norm, xn[:, k, :], x[:, k, :], par(g_col + k), stat[:, 0, 0:T], ALU.mult, ALU.mult,
                        "scaled", n, k)
                    dve_norm.name_also("normed", n, k)
                low_parts(dve_norm, xn, n)

            def ffn(layer, l):
                nonlocal unit
                s = dve_ffn
                conv_ffn = layer >= DEPTH

                def step(par_, key, i, f0):
                    if not conv_ffn:
                        split(2, i)
                        dve.wait_ge(*pe_unit.at("up", layer, key))
                        dve.wait_ge(*act_ffn.at("gated", layer, key))
                        tt(s, flat(hid[:, par_]), flat(gact[:, par_]), banks[5 + 2 * par_][:, :], ALU.mult, "hidden", layer, key)
                        hidden_parts(par_, layer, key)
                        return
                    for part, what in enumerate(("gate", "up")):
                        split(1, i)
                        b = banks[4 + 2 * par_ + part]
                        dve.wait_ge(*pe_unit.at(what, layer, key))

                        def at_tile(col, j):
                            c = col + part * F_TILES + f0 + j
                            return params[:, c:c + 1] if i is None else params[:, bass.ds(i * 4 + c, 1)]

                        conv(s, [fconv[:, par_, 2 * part + j, :] for j in range(2)], [b[:, j * T:(j + 1) * T] for j in range(2)],
                             lambda j, tap: at_tile(PT_FFN * P + (l * 3 + tap) * 2 * F_TILES, j), 3,
                             ("conv " + what, layer, key), biases=lambda j: at_tile(FFN_BIAS + l * 2 * F_TILES, j))
                    dve.wait_ge(*act_ffn.at("gated", layer, key))
                    dve.wait_ge(*s.now())
                    tt(s, flat(hid[:, par_]), flat(gact[:, par_]), flat(fconv[:, par_, 2:4, :]), ALU.mult, "hidden", layer, key)
                    hidden_parts(par_, layer, key)

                step(0, 0, None, 0)
                for k in (1, 2):
                    step(k % 2, k, None, 2 * k)
                    split()
                u0 = unit
                with Loop(book, dve, f"ffn{layer}", F_PAIRS) as i:
                    step(1, "a", i, 6)
                    split(1, i)
                    step(0, "b", i, 8)
                    split(1, i)
                unit = u0 + RING * F_PAIRS
                for k in (9, 10):
                    step(k % 2, k, None, 2 * k)
                    split()
                dve.wait_ge(*s.now())
                for b in range(4, 8):
                    psum.release(s, "ffn", layer, b)

            def head_norms(layer, sig, act_sig, pe_sig, both, w_col, w_step):
                dve.wait_ge(*act_proj.at("gate", layer, 6))
                for g in range(4):
                    if g == 3:
                        dve.wait_ge(*pe_sig.at("o", layer, 3))
                        split()
                    dve.wait_ge(*act_sig.at("rstd", layer, g))
                    for j in range(2):
                        stt(sig, oc[:, g, j * T:(j + 1) * T], psum.bank("o", layer, g)[:, j * T:(j + 1) * T],
                            par(w_col + w_step * j), stat[:, g, 0:T] if both else stat[:, g, j * T:(j + 1) * T],
                            ALU.mult, ALU.mult)
                    psum.release(sig, "o", layer, g)
                    dve.wait_ge(*sig.now())
                    tt(sig, two(y, g), oc[:, g, :], pj2(24 + 2 * g), ALU.mult, "mixed", layer, g)
                mixed_low(layer, sig, act_sig, range(4))
                split(HI - 1)

            def mixed_low(layer, sig, act_sig, order):
                for g in order:
                    dve.wait_ge(*act_sig.at("mixed hi", layer, g))
                    tt(sig, two(xl, g), two(y, g), two(xh, g), ALU.subtract, "mixed lo", layer, g)

            def decay_rows(layer, l):
                s = dve_gdn
                dve.wait_ge(*act_proj.at("ba", layer))
                ts(s, rows[0:8, 3, :], rows[0:8, 3, :], head[0:8, 2 + l:3 + l], ALU.add, None, None, "a + bias", layer)
                dve.wait_ge(*act_gdn.at("log1p", layer))
                stt(s, rows[0:8, 1, :], rows[0:8, 2, :], 0.0, rows[0:8, 4, :], ALU.min, ALU.subtract, "log beta", layer)
                stt(s, rows[0:8, 3, :], rows[0:8, 3, :], 0.0, rows[0:8, 5, :], ALU.max, ALU.add)
                dve.wait_ge(*act_gdn.at("a", layer))
                dve.wait_ge(*s.now())
                ts(s, rows[0:8, 3, :], rows[0:8, 3, :], head[0:8, 6:7], ALU.mult, -1.0, ALU.mult)
                dve.wait_ge(*s.now())
                scan(s, rows[0:8, 0, :], rows[0:8, 3, :])
                dve.wait_ge(*s.now())
                dve.wait_ge(*act_gdn.at("beta", layer))
                v.tensor_copy(rows[0:8, 5, :], rows[0:8, 1, :]).then_inc(*s.tick("rows", layer))

            def unit_qk(layer, gs):
                s = dve_gdn
                for g in gs:
                    dve.wait_ge(*act_gdn.at("rstd", layer, "qk", g))
                    tt(s, pj2(2 * g), pj2(2 * g), stat[:, g % 4, :], ALU.mult, "unit", layer, g)

            def gdn(layer, l):
                s = dve_gdn
                dve.wait_ge(*pe_gdn.at("tok", layer))
                v.tensor_copy(cols[:, 0:4, 0:8], psum.bank("tok", layer)[:, 0:32].rearrange("p (a h) -> p a h", a=4))\
                    .then_inc(*s.tick("tok", layer))
                psum.release(s, "tok", layer)
                dve.wait_ge(*s.now())
                for g in range(4):
                    t, h0 = g // 2, 4 * (g % 2)
                    dve.wait_ge(*pe_gdn.at("v", layer, g))
                    tt(s, vb[:, t, h0 * P:(h0 + 4) * P].rearrange("p (h n) -> p h n", h=4),
                       psum.bank("v", layer, g)[:, :].rearrange("p (h n) -> p h n", h=4),
                       cols[:, 2 * t + 1, h0:h0 + 4].rearrange("p (h n) -> p h n", n=1).to_broadcast([P, 4, P]), ALU.mult,
                       "vb", layer)
                    psum.release(s, "v", layer, g)

                def scores(h):
                    dve.wait_ge(*pool_gdn.at("decay", layer, h))
                    dve.wait_ge(*pe_gdn.at("kk", layer, h))
                    tt(s, lt[:, h, :], psum.bank("kk", layer, h)[:, 0:TRI], dec[:, h % 2, :], ALU.mult, "lt", layer, h)
                    psum.release(s, "kk", layer, h)
                    dve.wait_ge(*pe_gdn.at("qk", layer, h))
                    tt(s, at[:, h, :], psum.bank("qk", layer, h)[:, 0:TRI], dec[:, h % 2, :], ALU.mult)
                    psum.release(s, "qk", layer, h)

                for h in range(8):
                    dve.wait_ge(*pe_gdn.at("bcast", layer, h))
                    dve.wait_ge(*s.now())
                    b = psum.bank("bcast", layer, h)
                    ts(s, dec[:, h % 2, 0:T], b[:, 0:T], cols[:, 0, h:h + 1], ALU.subtract, 0.0, ALU.min)
                    ts(s, dec[:, h % 2, T:TRI], b[:, HALF:T], cols[:, 2, h:h + 1], ALU.subtract, 0.0, ALU.min,
                       "difference", layer, h)
                    tt(s, sq[:, h, :], pj[:, 8 + h, :], b[:, T:2 * T], ALU.mult, "kbeta", layer, h)
                    psum.release(s, "bcast", layer, h)
                    if h:
                        scores(h - 1)
                scores(7)
                for g in range(4):
                    dve.wait_ge(*pool_gdn.at("masked", layer, 0, g))
                    tt(s, inv[:, 16 + 4 * g:16 + 4 * g + 4, :], ident[:, :].rearrange("p (a n) -> p a n", a=1).to_broadcast([P, 4, P]),
                       ct[:, 4 * g:4 * g + 4, :], ALU.subtract, "XT", layer, 0, g)
                for lv in range(1, 7):
                    for g in range(4):
                        dve.wait_ge(*pe_gdn.at("z", layer, lv, g))
                        b = psum.bank("z", layer, lv, g)[:, 0:4 * HALF2].rearrange("p (h n) -> p h n", h=4)
                        if lv < 6:
                            X = first_halves(inv[:, 4 * g:4 * g + 4, :], lv)
                            tt(s, X, X, b.rearrange("p h (n c) -> p h n c", c=1 << lv), ALU.subtract, "X", layer, lv, g)
                        else:
                            XT = inv[0:HALF2, 16 + 4 * g:16 + 4 * g + 4, HALF2:HALF]
                            tt(s, XT, XT, b[0:HALF2], ALU.subtract, "XT", layer, lv, g)
                        psum.release(s, "z", layer, lv, g)
                for g in range(2):
                    dve.wait_ge(*pe_gdn.at("lu", layer, g))
                    r = vb[:, 1, 512 * g:512 * (g + 1)]
                    tt(s, r, r, psum.bank("lu", layer, g)[:, :], ALU.subtract, "rhs", layer, g)
                    psum.release(s, "lu", layer, g)
                head_norms(layer, s, act_gdn, pe_gdn, False, PT_MISC * P + R_GDN + l, 0)

            def gla(layer, kind, l):
                s = dve_gla
                heads = 8 if kind == "hgrn" else 4
                n = heads * T
                f = flat(pj[:, 8:8 + heads, :])
                q = pj[:, 0:heads, :]
                kk = yb_t if kind == "hgrn" else pj[:, 4:8, :]
                end = unit + len(units_in(kind)) - HI

                def due(count=1):
                    split(min(count, end - unit))

                due(3 if kind == "hgrn" else 4)
                if kind == "hgrn":
                    lg = params[:, PT_MISC * P + R_LB:PT_MISC * P + R_LB + 32].rearrange("p (d k) -> p d k", d=4)
                    m = lbs[:, 6, :]
                    tt(s, m, lg[:, 0, :], lg[:, 1, :], ALU.max)
                    for d in (2, 3):
                        dve.wait_ge(*s.now())
                        tt(s, m, m, lg[:, d, :], ALU.max)
                    dve.wait_ge(*s.now())
                    tt(s, lbs[:, 0:4, :], lg, lbs[:, 6:7, :].to_broadcast([P, 4, KT]), ALU.subtract, "logits", layer)
                    dve.wait_ge(*act_gla.at("exp logits", layer))
                    tt(s, lbs[:, 6, :], lbs[:, 0, :], lbs[:, 1, :], ALU.add)
                    tt(s, lbs[:, 7, :], lbs[:, 2, :], lbs[:, 3, :], ALU.add)
                    dve.wait_ge(*s.now())
                    tt(s, lbs[:, 6, :], lbs[:, 6, :], lbs[:, 7, :], ALU.add)
                    dve.wait_ge(*s.now())
                    v.reciprocal(lbs[:, 6, :], lbs[:, 6, :]).then_inc(*s.tick())
                    dve.wait_ge(*s.now())
                    tt(s, lbs[:, 0:2, :], lbs[:, 0:2, :], lbs[:, 6:7, :].to_broadcast([P, 2, KT]), ALU.mult)
                    dve.wait_ge(*s.now())
                    tt(s, lbs[:, 4, :], lbs[:, 0, :], lbs[:, 1, :], ALU.add)
                    dve.wait_ge(*s.now())
                    tt(s, lbs[:, 4, :], lbs[:, 4, :], lbs[:, 0, :], ALU.subtract)
                    dve.wait_ge(*s.now())
                    ts(s, lbs[:, 5, :], lbs[:, 4, :], -1.0, ALU.mult, 1.0, ALU.add)
                    dve.wait_ge(*s.now())
                    ts(s, flat(lbs[:, 4:6]), flat(lbs[:, 4:6]), 1e-19, ALU.max, None, None, "bounds", layer)
                    due()
                    dve.wait_ge(*act_proj.at("f", layer, 6))
                else:
                    dve.wait_ge(*act_gla.at("gk", layer, 1))
                due()
                dve.wait_ge(*act_gla.at("log1p f", layer))
                stt(s, decayed_sum[:, 0:n], f, 0.0, flat(sq)[:, 0:n], ALU.min, ALU.subtract)
                dve.wait_ge(*s.now())
                if kind == "hgrn":
                    tt(s, flat(ct), decayed_sum, f, ALU.subtract, "log k", layer)
                    due()
                    dve.wait_ge(*act_gla.at("log bounds", layer))
                    for h in range(8):
                        ts(s, sq[:, h, :], decayed_sum[:, h * T:(h + 1) * T], lbs[:, 5, h:h + 1], ALU.add, lbs[:, 4, h:h + 1], ALU.subtract,
                           "f against bound", layer)
                    due()
                    dve.wait_ge(*s.now())
                    for h in range(8):
                        ts(s, decayed_sum[:, h * T:(h + 1) * T], decayed_sum[:, h * T:(h + 1) * T], lbs[:, 5, h:h + 1], ALU.add, lbs[:, 4, h:h + 1], ALU.max)
                    due(2)
                    dve.wait_ge(*act_gla.at("log1p f2", layer))
                    dve.wait_ge(*s.now())
                    tt(s, decayed_sum, decayed_sum, flat(ct), ALU.add)
                else:
                    ts(s, decayed_sum[:, 0:n], decayed_sum[:, 0:n], 1.0 / 16, ALU.mult)
                dve.wait_ge(*s.now())
                for h in range(heads):
                    scan(s, pj[:, 8 + h, :], decayed_sum[:, h * T:(h + 1) * T], "cumulated", layer)
                    if h == 3:
                        due()
                due(2)
                dve.wait_ge(*act_proj.at("q", layer, 6 if kind == "hgrn" else 2))
                if kind == "hgrn":
                    ts(s, flat(q), flat(q), 128.0 ** -0.5, ALU.mult)
                s.name_also("qk", layer)
                due(len(units_in(kind)))
                dve.wait_ge(*s.now())
                dve.wait_ge(*act_gla.at("k", layer))

                def decayed(lv):
                    h, c = 1 << lv, 2 << lv
                    if lv >= 2:
                        dve.wait_ge(*(pe_gla.at("level", layer, lv - 2, heads // 2 - 1)))
                    dve.wait_ge(*act_gla.at("decay", layer, lv))
                    d = level_diff(lv, heads)
                    o = flat(at_level(lv)[:, 0:heads, :]).rearrange("p (n c) -> p n c", c=c)
                    k3 = flat(kk[:, 0:heads, :]).rearrange("p (n c) -> p n c", c=c)
                    q3 = flat(q).rearrange("p (n c) -> p n c", c=c)
                    tt(s, o[:, :, 0:h], k3[:, :, 0:h], d[:, :, 0:h], ALU.mult)
                    tt(s, o[:, :, h:c], q3[:, :, h:c], d[:, :, h:c], ALU.mult, "decayed", layer, lv)

                def masked(lv):
                    m = ident[:, :] if lv < 0 else level[:, lv, :]
                    m = m.bitcast(U32).rearrange("p (a b n) -> p a b n", a=1, b=1).to_broadcast([P, 2, 2, P])
                    a4 = at[:, :, :].rearrange("p h (a n) -> p h a n", a=3)
                    for g in range(heads // 2):
                        dve.wait_ge(*pe_gla.at("level", layer, lv, g))
                        v.copy_predicated(a4[:, 2 * g:2 * g + 2, 0:3:2, :], m,
                                          psum.bank("level", layer, lv, g)[:, :].rearrange("p (h a n) -> p h a n", h=2, a=2))\
                            .then_inc(*s.tick("masked", layer, lv))
                        psum.release(s, "level", layer, lv, g)

                for lv in range(8):
                    if lv == 0:
                        dve.wait_ge(*pe_unit.at("unit", layer, len(units_in(kind)) - 1))
                    decayed(lv)
                    if lv == 0:
                        v.memset(flat(at), 0.0).then_inc(*s.tick("zero", layer))
                    dve.wait_ge(*s.now())
                    masked(lv - 1)
                for g in range(heads // 4):
                    dve.wait_ge(*pe_gla.at("cross", layer, g))
                    v.tensor_copy(at[:, 4 * g:4 * g + 4, HALF:T],
                                  psum.bank("cross", layer, g)[:, :].rearrange("p (h n) -> p h n", h=4))\
                        .then_inc(*s.tick("causal", layer))
                    psum.release(s, "cross", layer, g)
                head_norms(layer, s, act_gla, pe_gla, kind == "gla", PT_MISC * P + (R_HGRN if kind == "hgrn" else R_GLA),
                           kind == "gla")

            def four(layer, l):
                s = dve_four
                dve.wait_ge(*act_proj.at("dt", layer))
                ts(s, rows[0:4, 2, :], rows[0:4, 2, :], hssm[0:4, 2 + l:3 + l], ALU.add, None, None, "dt + bias", layer)
                dve.wait_ge(*act_four.at("log1p dt", layer))
                stt(s, rows[0:4, 1, :], rows[0:4, 2, :], 0.0, rows[0:4, 3, :], ALU.max, ALU.add)
                dve.wait_ge(*act_four.at("a", layer))
                dve.wait_ge(*s.now())
                ts(s, rows[0:4, 2, :], rows[0:4, 1, :], head[0:4, 6:7], ALU.mult, -1.0, ALU.mult)
                dve.wait_ge(*s.now())
                scan(s, rows[0:4, 0, :], rows[0:4, 2, :], "rows", layer)
                dve.wait_ge(*act_four.at("c rstd", layer, 0))
                stt(s, pj[:, 6, :], pj[:, 6, :], par(PT_MISC * P + R_QG0 + l), stat[:, 3, 0:T], ALU.mult, ALU.mult)
                stt(s, pj[0:64, 7, :], pj[0:64, 7, :], params[0:64, PT_MISC * P + R_QG1 + l:PT_MISC * P + R_QG1 + l + 1],
                    stat[0:64, 3, 0:T], ALU.mult, ALU.mult)
                dve.wait_ge(*act_four.at("c rstd", layer, 1))
                stt(s, pj[:, 8, :], pj[:, 8, :], par(PT_MISC * P + R_KVG + l), stat[:, 3, T:2 * T], ALU.mult, ALU.mult,
                    "cn", layer)

                def pair(r):
                    if r < 2:
                        return P, pj2(2 * r), two(sq, r), pj2(2 * r)
                    q = flat(yb_t[:, 2 * (r - 2):2 * (r - 2) + 2, :])[0:96, :]
                    return 96, q, two(xn, r - 2)[0:96, :], q

                for r in range(6):
                    n, q, o, _ = pair(r)
                    dve.wait_ge(*act_four.at("rstd", layer, "n", r))
                    g = PT_MISC * P + (R_MOBAG + 2 * l + r if r < 2 else R_MLAG + 2 * l + (r - 2) // 2)
                    stt(s, o, q, params[0:n, g:g + 1], stat[0:n, r % 4, :], ALU.mult, ALU.mult, "roped in", layer, r)
                dve.wait_ge(*pe_four.at("tok", layer))
                v.tensor_copy(cols[:, 0:4, 0:4], psum.bank("tok", layer)[:, 0:32].rearrange("p (a h) -> p a h", a=4)[:, :, 0:4])\
                    .then_inc(*s.tick())
                psum.release(s, "tok", layer)
                dve.wait_ge(*s.now())
                dve.wait_ge(*pe_four.at("xtok", layer))
                for t in range(2):
                    tt(s, vb[:, t, 3 * T:4 * T].rearrange("p (h n) -> p h n", h=4),
                       psum.bank("xtok", layer)[:, t * T:(t + 1) * T].rearrange("p (h n) -> p h n", h=4),
                       cols[:, 2 * t + 1, 0:4].rearrange("p (h n) -> p h n", n=1).to_broadcast([P, 4, 64]), ALU.mult)
                psum.release(s, "xtok", layer)
                for g in range(2):
                    dve.wait_ge(*pe_four.at("bcast", layer, g))
                    b = psum.bank("bcast", layer, g)
                    for j in range(2):
                        h = 2 * g + j
                        ts(s, at[:, h, 0:T], b[:, j * T:(j + 1) * T], cols[:, 0, h:h + 1], ALU.subtract, 0.0, ALU.min)
                        ts(s, at[:, h, T:TRI], b[:, j * T + HALF:(j + 1) * T], cols[:, 2, h:h + 1], ALU.subtract, 0.0, ALU.min,
                           "difference", layer, h)
                    psum.release(s, "bcast", layer, g)
                for h in range(4):
                    dve.wait_ge(*act_four.at("decay", layer, h))
                    dve.wait_ge(*pe_four.at("bc", layer, h // 2))
                    tt(s, at[:, h, :], at[:, h, :], incl[:, :], ALU.mult)
                    dve.wait_ge(*s.now())
                    tt(s, at2[:, 4 + h, :], psum.bank("bc", layer, h // 2)[:, 0:TRI], at[:, h, :], ALU.mult, "causal", layer, 3)
                    if h % 2:
                        psum.release(s, "bc", layer, h // 2)

                def rope(r):
                    n, _, qn, o = pair(r)
                    c = 1 if r < 2 else 3
                    sin = trig[0:n, c:c + 1, :].to_broadcast([n, 2, T])
                    dve.wait_ge(*pe_four.at("rot", layer, r))
                    half = oc4[0:n, r % 4, :].rearrange("p (a n) -> p a n", a=2)
                    dve.wait_ge(*s.now())
                    tt(s, half, psum.bank("rot", layer, r)[0:n, :].rearrange("p (a n) -> p a n", a=2), sin, ALU.mult)
                    psum.release(s, "rot", layer, r)
                    dve.wait_ge(*s.now())
                    dve.wait_ge(*pool_four.at("cos", layer, r))
                    tt(s, o, qn, oc4[0:n, r % 4, :], ALU.add, "roped", layer, r)

                rope(0)
                rope(1)
                dve.wait_ge(*s.now())
                for h in range(4):
                    dve.wait_ge(*pe_four.at("z", layer, h))
                    b = psum.bank("z", layer, h)
                    ts(s, at2[:, h, :], b[:, 0:TRI], 0.125, ALU.mult, None, None, "z", layer, h)
                    psum.release(s, "z", layer, h)
                for n in range(8 + 2):
                    if n < 8:
                        p = prob(n)
                        dve.wait_ge(*pe_four.at("score", layer, n))
                        if n >= 4:
                            dve.wait_ge(*pe_four.at("probs", layer, n - 4))
                        dve.wait_ge(*s.now())
                        stt(s, p, psum.bank("score", layer, n)[:, 0:TRI], 0.125 if n < 4 else 96.0 ** -0.5, amask[:, :],
                            ALU.mult, ALU.add)
                        psum.release(s, "score", layer, n)
                        dve.wait_ge(*s.now())
                        v.tensor_reduce(small[:, n, 0:1], p[:, 0:HALF], AX.X, ALU.max, negate=True).then_inc(*s.tick())
                        v.tensor_reduce(small[:, n, 1:2], p[:, HALF:TRI], AX.X, ALU.max, negate=True)\
                            .then_inc(*s.tick("max", layer, n))
                    if n < 4:
                        rope(2 + n)
                    if n >= 2:
                        n -= 2
                        dve.wait_ge(*act_four.at("exp", layer, n))
                        v.reciprocal(small[:, n, 2:4], small[:, n, 2:4]).then_inc(*s.tick("inverse sum", layer, n))
                        if n % 2:
                            h = n // 2
                            dve.wait_ge(*act_four.at("log1p z", layer, h))
                            stt(s, sb_t[:, h, :], at2[:, h, :], 0.0, sb_t[:, h, :], ALU.min, ALU.subtract, "log beta", layer, h)
                for h in range(4):
                    dve.wait_ge(*pe_four.at("tail", layer, h))
                    tt(s, sb_t[:, h, :], sb_t[:, h, :], psum.bank("tail", layer, h)[:, 0:TRI], ALU.add, "log a", layer, h)
                    psum.release(s, "tail", layer, h)
                dve.wait_ge(*pe_four.at("o", layer, 1))
                split()
                dve.wait_ge(*pe_four.at("o", layer, 3))
                b = psum.bank("o", layer, 3)
                dve.wait_ge(*act_proj.at("z", layer))
                for j in range(2):
                    stt(s, oc4[:, 3, j * T:(j + 1) * T], pj[:, 18 + j, :], par(PT_MISC * P + R_SSMD + 2 * l + j),
                        b[:, j * T:(j + 1) * T], ALU.mult, ALU.add)
                psum.release(s, "o", layer, 3)
                dve.wait_ge(*s.now())
                tt(s, oc4[:, 3, :], oc4[:, 3, :], pj2(16), ALU.mult, "gated", layer)
                dve.wait_ge(*s.now())
                for m in (0, 1, 3, 2):
                    dve.wait_ge(*act_four.at("rstd", layer, m))
                    for j in range(2):
                        g = PT_MISC * P + (R_HEADG + 6 * l + 2 * m if m < 3 else R_SSMG + 2 * l) + j
                        r = stat[:, m, j * T:(j + 1) * T] if m < 3 else stat[:, 3, 0:T]
                        stt(s, y[:, 2 * m + j, :], oc4[:, m, j * T:(j + 1) * T], par(g), r, ALU.mult, ALU.mult, "mixed", layer, m)
                mixed_low(layer, s, act_four, (0, 1, 3, 2))
                split(HI - 1)

            split()
            dve.wait_ge(*act_setup.at("x", 3))
            for m in range(4):
                tt(dve_norm, two(xl, m), two(x, m), two(xh, m), ALU.subtract, "x lo", -1, m)
            split(HI - 1)
            setup()
            norm = 0
            for layer, (kind, l) in enumerate(CHAIN[:layers]):
                if kind == "four":
                    rms_norm(norm, PT_MISC * P + R_RMSMIX + 8 * l)
                    norm += 1
                    project(layer, kind, l)
                    four(layer, l)
                    residual(norm, ("out", layer), None)
                    rms_norm(norm, PT_MISC * P + R_RMSFFN + 8 * l)
                    norm += 1
                    ffn(layer, l)
                    split()
                    residual(norm, ("ffn", layer), None)
                else:
                    project(layer, kind, l)
                    gdn(layer, l) if kind == "gdn" else gla(layer, kind, l)
                    residual(norm, ("out", layer), DN_ALPHA)
                    layer_norm(norm, PT_LN * P + R_MIXG + 8 * layer, PT_LN * P + R_MIXB + 8 * layer)
                    norm += 1
                    ffn(layer, l)
                    split()
                    residual(norm, ("ffn", layer), DN_ALPHA)
                    layer_norm(norm, PT_LN * P + R_FFNG + 8 * layer, PT_LN * P + R_FFNB + 8 * layer,
                               is_input=layer < min(layers, DEPTH) - 1)
                    norm += 1


_INS = ["x", "gdn_w_in", "gdn_conv_w", "gdn_a_log", "gdn_dt_bias", "gdn_norm_w", "gdn_w_out", "hgrn_w_in",
        "hgrn_lb_logits", "hgrn_norm_w", "hgrn_w_out", "gla_w_in", "gla_w_gk2", "gla_b_gk", "gla_norm_w", "gla_w_out",
        "mix_ln_g", "mix_ln_b", "ffn_w_in", "ffn_w_down", "ffn_ln_g", "ffn_ln_b", "positions_2", "mix_norm_g_2", "w_in_2",
        "moba_qk_g_2", "mla_q_norm_g_2", "mla_kv_norm_g_2", "mla_w_uq_2", "mla_w_ukv_2", "mla_qk_g_2", "ssm_conv_w_2",
        "ssm_conv_b_2", "ssm_dt_bias_2", "ssm_a_log_2", "ssm_d_2", "ssm_norm_g_2", "head_out_g_2", "w_out_2",
        "ffn_norm_g_2", "ffn_w_in_2", "ffn_conv_w_2", "ffn_conv_b_2", "ffn_w_out_2"]


def rope_freqs():
    def inverse(dim):
        e = np.arange(0, dim, 2, dtype=np.float32) / np.float32(dim)
        return (np.float32(1.0) / (np.float32(10000.0) ** e)).astype(np.float32)

    f = np.zeros((P, 2), np.float32)
    f[:, 0] = np.tile(inverse(64), 4)
    f[64:96, 1] = np.tile(inverse(32), 2)
    return f


def write(nc, arrays, book, layers=len(CHAIN)):
    A = {n: nc.dram_tensor(f"in_{n}_dram", a.shape, mybir.dt.from_np(a.dtype), kind="ExternalInput").ap()
         for n, a in arrays.items()}
    out = nc.dram_tensor("out_0_dram", (1, T, D), F32, kind="ExternalOutput").ap()
    build(nc, A, out, book, layers)


def kernel(**inputs):
    import concourse.bacc as bacc
    from concourse.bass_utils import run_bass_kernel_spmd

    arrays = {n: np.ascontiguousarray(inputs[n]) for n in _INS}
    arrays["rope_freqs"] = rope_freqs()
    book = Book()
    write(bacc.Bacc("TRN2", target_bir_lowering=False, num_devices=1), arrays, book)
    nc = bacc.Bacc("TRN2", target_bir_lowering=False, num_devices=1)
    write(nc, arrays, book)
    r = run_bass_kernel_spmd(nc, [{f"in_{n}_dram": a for n, a in arrays.items()}], core_ids=[0])
    return r.results[0]["out_0_dram"]
```
